# Optimizing a Trainium2 kernel written in Bass

```python
import jax, jax.numpy as jnp
from jax import lax
import numpy as np
import jax
import jax.numpy as jnp

D_MODEL = 1024
BATCH = 1
SEQ = 256
DEPTH = 2

HEAD_DIM = 64
A_HEADS = 8
B_HEADS = 8
M_HEADS = 4
M_HEAD_DIM = 128
BRANCH_WIDTH = 512
N_BRANCH = 3
MOBA_BLOCK = 256
MOBA_TOPK = 3
IDX_HEADS = 8
IDX_DIM = 64
IDX_TOPK_MAX = 256
N_MEM = 256
ROPE_THETA = 500000.0
ROT_FRACTION = 4
Q_BLOCK = 128
RMS_EPS = 1e-6
IN_WIDTHS = (
    BRANCH_WIDTH, BRANCH_WIDTH, BRANCH_WIDTH, BRANCH_WIDTH,
    BRANCH_WIDTH, BRANCH_WIDTH, BRANCH_WIDTH, BRANCH_WIDTH,
    IDX_HEADS * IDX_DIM, IDX_DIM, IDX_HEADS,
    BRANCH_WIDTH, BRANCH_WIDTH,
    N_BRANCH * D_MODEL,
)
IN_COLS = sum(IN_WIDTHS)


def rmsnorm(x, g):
    xf = x.astype(jnp.float32)
    y = xf * lax.rsqrt(jnp.mean(xf * xf, axis=-1, keepdims=True) + RMS_EPS)
    return (y * g.astype(jnp.float32)).astype(x.dtype)

def partial_rope(x, pos):
    d = x.shape[-1]
    rot = d // ROT_FRACTION
    half = rot // 2
    inv_freq = ROPE_THETA ** (-jnp.arange(half, dtype=jnp.float32) / half)
    ang = pos.astype(jnp.float32)[:, None] * inv_freq[None, :]
    cos = jnp.cos(ang)[:, None, :].astype(x.dtype)
    sin = jnp.sin(ang)[:, None, :].astype(x.dtype)
    x1 = x[..., :half]
    x2 = x[..., half:rot]
    return jnp.concatenate([x1 * cos - x2 * sin, x2 * cos + x1 * sin, x[..., rot:]], axis=-1)

def masked_softmax(s, mask):
    s = jnp.where(mask, s.astype(jnp.float32), -jnp.inf)
    return jax.nn.softmax(s, axis=-1)

def moba_attention(q, k, v):
    b, s, h, d = q.shape
    nb = -(-s // MOBA_BLOCK)
    pad = nb * MOBA_BLOCK - s
    padw = ((0, 0), (0, pad), (0, 0), (0, 0))
    kb = jnp.pad(k, padw).reshape(b, nb, MOBA_BLOCK, h, d).transpose(0, 3, 1, 2, 4)
    vb = jnp.pad(v, padw).reshape(b, nb, MOBA_BLOCK, h, d).transpose(0, 3, 1, 2, 4)
    kmean = jnp.mean(kb.astype(jnp.float32), axis=3).astype(q.dtype)
    kk = min(MOBA_TOPK, nb - 1)
    scale = d ** -0.5
    b_idx = jnp.arange(b)[:, None, None, None]
    h_idx = jnp.arange(h)[None, :, None, None]
    blk_ids = jnp.arange(nb)

    def one_block(qi):
        start = qi * Q_BLOCK
        own = start // MOBA_BLOCK
        qpos = start + jnp.arange(Q_BLOCK)
        qb = lax.dynamic_slice_in_dim(q, start, Q_BLOCK, axis=1).transpose(0, 2, 1, 3)
        k_own = lax.dynamic_index_in_dim(kb, own, axis=2, keepdims=False)
        v_own = lax.dynamic_index_in_dim(vb, own, axis=2, keepdims=False)
        kpos_own = own * MOBA_BLOCK + jnp.arange(MOBA_BLOCK)
        s_own = jnp.einsum('bhqd,bhkd->bhqk', qb, k_own) * scale
        m_own = jnp.broadcast_to(kpos_own[None, :] <= qpos[:, None], s_own.shape)
        if kk == 0:
            p = masked_softmax(s_own, m_own).astype(v.dtype)
            o = jnp.einsum('bhqk,bhkd->bhqd', p, v_own)
        else:
            gate = jnp.einsum('bhqd,bhnd->bhqn', qb, kmean).astype(jnp.float32)
            gate = jnp.where(blk_ids < own, gate, -jnp.inf)
            _, sel = lax.top_k(gate, kk)
            valid = sel < own
            kg = kb[b_idx, h_idx, sel]
            vg = vb[b_idx, h_idx, sel]
            s_past = jnp.einsum('bhqd,bhqjkd->bhqjk', qb, kg) * scale
            m_past = jnp.broadcast_to(valid[..., None], s_past.shape)
            n_past = kk * MOBA_BLOCK
            s_all = jnp.concatenate([s_past.reshape(b, h, Q_BLOCK, n_past), s_own], axis=-1)
            m_all = jnp.concatenate([m_past.reshape(b, h, Q_BLOCK, n_past), m_own], axis=-1)
            p = masked_softmax(s_all, m_all).astype(v.dtype)
            p_past = p[..., :n_past].reshape(b, h, Q_BLOCK, kk, MOBA_BLOCK)
            o = (jnp.einsum('bhqjk,bhqjkd->bhqd', p_past, vg)
                 + jnp.einsum('bhqk,bhkd->bhqd', p[..., n_past:], v_own))
        return o.transpose(0, 2, 1, 3)

    out = lax.map(one_block, jnp.arange(s // Q_BLOCK))
    return out.transpose(1, 0, 2, 3, 4).reshape(b, s, h, d)

def dsa_attention(q, k, v, qi, ki, wi):
    b, s, h, d = q.shape
    n_sel = min(IDX_TOPK_MAX, s // 4)
    scale = d ** -0.5
    kpos = jnp.arange(s)
    b_idx = jnp.arange(b)[:, None, None]

    def one_block(blk):
        start = blk * Q_BLOCK
        qpos = start + jnp.arange(Q_BLOCK)
        q_b = lax.dynamic_slice_in_dim(q, start, Q_BLOCK, axis=1)
        qi_b = lax.dynamic_slice_in_dim(qi, start, Q_BLOCK, axis=1)
        wi_b = lax.dynamic_slice_in_dim(wi, start, Q_BLOCK, axis=1)
        rel = jax.nn.relu(jnp.einsum('bqhd,bsd->bqhs', qi_b, ki))
        idx_score = jnp.einsum('bqhs,bqh->bqs', rel, wi_b).astype(jnp.float32)
        idx_score = jnp.where(kpos[None, :] <= qpos[:, None], idx_score, -jnp.inf)
        _, sel = lax.top_k(idx_score, n_sel)
        valid = sel <= qpos[None, :, None]
        kg = k[b_idx, sel]
        vg = v[b_idx, sel]
        sc = jnp.einsum('bqhd,bqnhd->bqhn', q_b, kg) * scale
        p = masked_softmax(sc, valid[:, :, None, :]).astype(v.dtype)
        return jnp.einsum('bqhn,bqnhd->bqhd', p, vg)

    out = lax.map(one_block, jnp.arange(s // Q_BLOCK))
    return out.transpose(1, 0, 2, 3, 4).reshape(b, s, h, d)

def memory_attention(qm, km, vm):
    sc = jnp.einsum('bshd,bmhd->bhsm', qm, km) * (qm.shape[-1] ** -0.5)
    p = jax.nn.softmax(sc.astype(jnp.float32), axis=-1).astype(vm.dtype)
    return jnp.einsum('bhsm,bmhd->bshd', p, vm)

def hybrid_layer(x, mem, pos, norm_g, w_in, mem_norm_g, w_mem_kv, w_branch, w_out):
    b, s, _ = x.shape
    h = rmsnorm(x, norm_g)
    proj = jnp.einsum('bsd,dc->bsc', h, w_in)
    offs = np.cumsum(IN_WIDTHS)[:-1].tolist()
    (a_q, a_k, a_v, a_g, b_q, b_k, b_v, b_g,
     i_q, i_k, i_w, m_q, m_g, mix) = jnp.split(proj, offs, axis=-1)

    qa = partial_rope(a_q.reshape(b, s, A_HEADS, HEAD_DIM), pos)
    ka = partial_rope(a_k.reshape(b, s, A_HEADS, HEAD_DIM), pos)
    va = a_v.reshape(b, s, A_HEADS, HEAD_DIM)
    ya = moba_attention(qa, ka, va).reshape(b, s, BRANCH_WIDTH) * jax.nn.silu(a_g)

    qb = partial_rope(b_q.reshape(b, s, B_HEADS, HEAD_DIM), pos)
    kb = partial_rope(b_k.reshape(b, s, B_HEADS, HEAD_DIM), pos)
    vb = b_v.reshape(b, s, B_HEADS, HEAD_DIM)
    qi = partial_rope(i_q.reshape(b, s, IDX_HEADS, IDX_DIM), pos) * (IDX_DIM ** -0.5)
    ki = partial_rope(i_k[:, :, None, :], pos)[:, :, 0, :]
    wi = i_w * (IDX_HEADS ** -0.5)
    yb = dsa_attention(qb, kb, vb, qi, ki, wi).reshape(b, s, BRANCH_WIDTH) * jax.nn.silu(b_g)

    mn = rmsnorm(mem, mem_norm_g)
    km, vm = jnp.split(jnp.einsum('bmd,dc->bmc', mn, w_mem_kv), 2, axis=-1)
    km = km.reshape(b, -1, M_HEADS, M_HEAD_DIM)
    vm = vm.reshape(b, -1, M_HEADS, M_HEAD_DIM)
    ym = memory_attention(m_q.reshape(b, s, M_HEADS, M_HEAD_DIM), km, vm)
    ym = ym.reshape(b, s, BRANCH_WIDTH) * jax.nn.silu(m_g)

    ys = jnp.stack([ya, yb, ym], axis=2)
    up = jnp.einsum('bsnw,nwd->bsnd', ys, w_branch)
    gates = jax.nn.sigmoid(mix.reshape(b, s, N_BRANCH, D_MODEL))
    merged = jnp.sum(gates * up, axis=2)
    return x + jnp.einsum('bsd,de->bse', merged, w_out)

def first_inputs(seed: int = 0) -> dict:
    key = jax.random.key(seed)
    ks = jax.random.split(key, 9)
    f32 = jnp.float32
    x = jax.random.normal(ks[0], (BATCH, SEQ, D_MODEL), f32)
    mem = jax.random.normal(ks[1], (BATCH, N_MEM, D_MODEL), f32)
    norm_g = 1.0 + 0.02 * jax.random.normal(ks[2], (DEPTH, D_MODEL), f32)
    w_in = jax.random.normal(ks[3], (DEPTH, D_MODEL, IN_COLS), f32) * (D_MODEL ** -0.5)
    mem_norm_g = 1.0 + 0.02 * jax.random.normal(ks[4], (DEPTH, D_MODEL), f32)
    w_mem_kv = jax.random.normal(ks[5], (DEPTH, D_MODEL, 2 * BRANCH_WIDTH), f32) * (D_MODEL ** -0.5)
    w_branch = jax.random.normal(ks[6], (DEPTH, N_BRANCH, BRANCH_WIDTH, D_MODEL), f32) * (BRANCH_WIDTH ** -0.5)
    w_out = jax.random.normal(ks[7], (DEPTH, D_MODEL, D_MODEL), f32) * (D_MODEL ** -0.5)
    final_g = 1.0 + 0.02 * jax.random.normal(ks[8], (D_MODEL,), f32)
    return {'x': x, 'mem': mem, 'norm_g': norm_g, 'w_in': w_in, 'mem_norm_g': mem_norm_g,
            'w_mem_kv': w_mem_kv, 'w_branch': w_branch, 'w_out': w_out, 'final_g': final_g}

def first_block(x, mem, norm_g, w_in, mem_norm_g, w_mem_kv, w_branch, w_out, final_g):
    pos = jnp.arange(x.shape[1], dtype=jnp.int32)
    for l in range(DEPTH):
        x = hybrid_layer(x, mem, pos, norm_g[l], w_in[l], mem_norm_g[l], w_mem_kv[l],
                         w_branch[l], w_out[l])
    return rmsnorm(x, final_g)


GLA_HEADS = 4
GLA_WIDTH = GLA_HEADS * HEAD_DIM
GLA_GATE_RANK = 16
GLA_TAU = 16.0
GLA_CHUNK = 64
RWKV_HEADS = 4
RWKV_WIDTH = RWKV_HEADS * HEAD_DIM
RWKV_DECAY_RANK = 64
RWKV_ICLR_RANK = 64
RWKV_VRES_RANK = 32
RWKV_GATE_RANK = 160
RWKV_GN_EPS = 64e-5
NSA_HEADS = 8
NSA_KV_HEADS = 2
NSA_WIDTH = NSA_HEADS * HEAD_DIM
NSA_KV_WIDTH = NSA_KV_HEADS * HEAD_DIM
NSA_CMP_BLOCK = 32
NSA_CMP_STRIDE = 16
NSA_CMP_HIDDEN = 256
NSA_SEL_BLOCK = 64
NSA_N_SELECT = 16
NSA_WINDOW = 512
NSA_SEL_QCHUNK = 32
NSA_WIN_QBLOCK = 128
ROPE_THETA_2 = 10000.0
FFN_HIDDEN = ((8 * D_MODEL + 3 * 256 - 1) // (3 * 256)) * 256
DEEPNORM_ALPHA = (2 * DEPTH) ** 0.25
DEEPNORM_BETA = (8 * DEPTH) ** -0.25
LN_EPS = 1e-5
MASK_NEG = -1e30

GLA_COLS = (GLA_WIDTH, GLA_WIDTH, GLA_WIDTH, GLA_WIDTH, GLA_GATE_RANK)
RWKV_COLS = (RWKV_WIDTH, RWKV_WIDTH, RWKV_WIDTH,
             RWKV_DECAY_RANK, RWKV_ICLR_RANK, RWKV_GATE_RANK)
NSA_COLS = (NSA_WIDTH,) + (NSA_KV_WIDTH,) * 6 + (3 * NSA_HEADS,)
IN_COLS_2 = sum(GLA_COLS) + sum(RWKV_COLS) + sum(NSA_COLS)


def _split(h, widths):
    idx = np.cumsum(np.asarray(widths))[:-1].tolist()
    return jnp.split(h, idx, axis=-1)

def _layer_norm(x, w, b):
    xf = x.astype(jnp.float32)
    mu = xf.mean(-1, keepdims=True)
    var = jnp.square(xf - mu).mean(-1, keepdims=True)
    return ((xf - mu) * lax.rsqrt(var + LN_EPS) * w + b).astype(x.dtype)

def _head_norm(x, w, b, n_heads, eps):
    shp = x.shape
    xh = x.astype(jnp.float32).reshape(shp[:-1] + (n_heads, shp[-1] // n_heads))
    mu = xh.mean(-1, keepdims=True)
    var = jnp.square(xh - mu).mean(-1, keepdims=True)
    xh = (xh - mu) * lax.rsqrt(var + eps)
    return xh.reshape(shp) * w + b

def _rope(x, pos):
    half = x.shape[-1] // 2
    inv = ROPE_THETA_2 ** (-jnp.arange(half, dtype=jnp.float32) / half)
    ang = pos.astype(jnp.float32)[:, None] * inv
    shape = (ang.shape[0],) + (1,) * (x.ndim - 3) + (half,)
    cos = jnp.cos(ang).reshape(shape).astype(x.dtype)
    sin = jnp.sin(ang).reshape(shape).astype(x.dtype)
    x1, x2 = x[..., :half], x[..., half:]
    return jnp.concatenate([x1 * cos - x2 * sin, x1 * sin + x2 * cos], axis=-1)

def _token_shift_mix(p, mu):
    prev = jnp.pad(p, ((0, 0), (1, 0), (0, 0)))[:, :-1]
    return p + (prev - p) * mu

def _gla_mixer(q, k, v, g, a_lr, w_a2, b_a, ln_w, ln_b):
    dt = q.dtype
    B, S, _ = q.shape
    H, dk, C = GLA_HEADS, HEAD_DIM, GLA_CHUNK
    n = S // C
    f32 = jnp.float32
    log_a = jax.nn.log_sigmoid((a_lr @ w_a2 + b_a).astype(f32)) / GLA_TAU

    def chunks(t):
        return t.astype(f32).reshape(B, n, C, H, dk).transpose(1, 0, 3, 2, 4)

    qc, kc, vc, ac = chunks(q * dk ** -0.5), chunks(k), chunks(v), chunks(log_a)
    causal = jnp.tril(jnp.ones((C, C), bool))[:, :, None]

    def step(state, inp):
        qi, ki, vi, ai = inp
        b = jnp.cumsum(ai, axis=2)
        inter = jnp.einsum('bhtk,bhkv->bhtv', qi * jnp.exp(b), state)
        diff = b[:, :, :, None, :] - b[:, :, None, :, :]
        decay = jnp.exp(jnp.where(causal, diff, -jnp.inf))
        scores = jnp.einsum('bhtk,bhsk,bhtsk->bhts', qi, ki, decay)
        intra = jnp.einsum('bhts,bhsv->bhtv', scores, vi)
        b_end = b[:, :, -1:, :]
        state = (jnp.exp(b_end[:, :, 0, :, None]) * state
                 + jnp.einsum('bhsk,bhsv->bhkv', ki * jnp.exp(b_end - b), vi))
        return state, inter + intra

    s0 = jnp.zeros((B, H, dk, dk), f32)
    _, o = lax.scan(step, s0, (qc, kc, vc, ac))
    o = o.transpose(1, 0, 3, 2, 4).reshape(B, S, H * dk)
    o = _head_norm(o, ln_w, ln_b, H, LN_EPS)
    return (o * jax.nn.silu(g.astype(f32))).astype(dt)

def _rwkv7_mixer(r, k, v, w_lr, a_lr, g_lr, w0, w2, a0, a2, g2, k_k, k_a, r_k, ln_w, ln_b):
    dt = r.dtype
    B, S, _ = r.shape
    H, N = RWKV_HEADS, HEAD_DIM
    f32 = jnp.float32
    r, k, v = r.astype(f32), k.astype(f32), v.astype(f32)
    w_log = -jax.nn.softplus(-(w0 + jnp.tanh(w_lr) @ w2).astype(f32)) - 0.5
    decay = jnp.exp(-jnp.exp(w_log))
    a = jax.nn.sigmoid((a0 + a_lr @ a2).astype(f32))
    g = (jax.nn.sigmoid(g_lr) @ g2).astype(f32)
    kk = (k * k_k).reshape(B, S, H, N)
    kk = kk / jnp.maximum(jnp.sqrt(jnp.sum(kk * kk, axis=-1, keepdims=True)), 1e-12)
    k = k * (1.0 + (a - 1.0) * k_a)

    def heads(t):
        return t.reshape(B, S, H, N).transpose(1, 0, 2, 3)

    a_h = a.reshape(B, S, H, N)
    xs = (heads(r), heads(decay), heads(k), heads(v),
          (-kk).transpose(1, 0, 2, 3), (kk * a_h).transpose(1, 0, 2, 3))

    def step(state, inp):
        r_t, w_t, k_t, v_t, a_t, b_t = inp
        sa = jnp.einsum('bhvk,bhk->bhv', state, a_t)
        state = (state * w_t[:, :, None, :] + sa[..., None] * b_t[:, :, None, :]
                 + v_t[..., None] * k_t[:, :, None, :])
        return state, jnp.einsum('bhvk,bhk->bhv', state, r_t)

    s0 = jnp.zeros((B, H, N, N), f32)
    _, y = lax.scan(step, s0, xs)
    y = y.transpose(1, 0, 2, 3).reshape(B, S, H * N)
    y = _head_norm(y, ln_w, ln_b, H, RWKV_GN_EPS)
    bonus = (jnp.sum((r * k).reshape(B, S, H, N) * r_k, axis=-1, keepdims=True)
             * v.reshape(B, S, H, N)).reshape(B, S, H * N)
    return ((y + bonus) * g).astype(dt)

def _compress(t, pos_emb, w1, w2):
    B, S, G, hd = t.shape
    n_sub = NSA_CMP_BLOCK // NSA_CMP_STRIDE
    ncb = S // NSA_CMP_STRIDE
    nc = ncb - n_sub + 1
    t_s = t.reshape(B, ncb, NSA_CMP_STRIDE, G, hd)
    blocks = jnp.concatenate([t_s[:, j:j + nc] for j in range(n_sub)], axis=2)
    blocks = blocks + pos_emb[None, None, :, None, :]
    flat = blocks.transpose(0, 1, 3, 2, 4).reshape(B, nc, G, NSA_CMP_BLOCK * hd)
    return jax.nn.gelu(flat @ w1) @ w2

def _overlap_matrix(seq):
    nc = seq // NSA_CMP_STRIDE - NSA_CMP_BLOCK // NSA_CMP_STRIDE + 1
    ns = seq // NSA_SEL_BLOCK
    c0 = np.arange(nc) * NSA_CMP_STRIDE
    s0 = np.arange(ns) * NSA_SEL_BLOCK
    lo = np.maximum(c0[:, None], s0[None, :])
    hi = np.minimum(c0[:, None] + NSA_CMP_BLOCK, s0[None, :] + NSA_SEL_BLOCK)
    return (np.maximum(hi - lo, 0) / NSA_CMP_STRIDE).astype(np.float32)

def _selected_attention(q, k, v, idx, pos):
    B, S, G, HPG, hd = q.shape
    n = idx.shape[-1]
    ns = S // NSA_SEL_BLOCK
    kb = k.reshape(B, ns, NSA_SEL_BLOCK, G, hd).transpose(0, 3, 1, 2, 4)
    vb = v.reshape(B, ns, NSA_SEL_BLOCK, G, hd).transpose(0, 3, 1, 2, 4)
    qcs = NSA_SEL_QCHUNK
    nq = S // qcs
    q_ch = q.reshape(B, nq, qcs, G, HPG, hd).transpose(1, 0, 2, 3, 4, 5)
    idx_ch = idx.reshape(B, G, nq, qcs, n).transpose(2, 0, 1, 3, 4)
    pos_ch = pos.reshape(nq, qcs)
    bi = jnp.arange(B)[:, None, None, None]
    gi = jnp.arange(G)[None, :, None, None]
    offs = jnp.arange(NSA_SEL_BLOCK)

    def one(args):
        qc, ic, tc = args
        kg = kb[bi, gi, ic]
        vg = vb[bi, gi, ic]
        s = jnp.einsum('bqghd,bgqnkd->bghqnk', qc, kg).astype(jnp.float32)
        kpos = ic[..., None] * NSA_SEL_BLOCK + offs
        valid = kpos <= tc[None, None, :, None, None]
        s = jnp.where(valid[:, :, None], s, MASK_NEG).reshape(B, G, HPG, qcs, n * NSA_SEL_BLOCK)
        pr = jax.nn.softmax(s, axis=-1).reshape(B, G, HPG, qcs, n, NSA_SEL_BLOCK)
        return jnp.einsum('bghqnk,bgqnkd->bqghd', pr.astype(vg.dtype), vg)

    o = lax.map(one, (q_ch, idx_ch, pos_ch))
    return o.transpose(1, 0, 2, 3, 4, 5).reshape(B, S, G, HPG, hd)

def _window_attention(q, k, v):
    B, S, G, HPG, hd = q.shape
    qb_sz, win = NSA_WIN_QBLOCK, NSA_WINDOW
    nb = S // qb_sz
    kp = jnp.pad(k, ((0, 0), (win, 0), (0, 0), (0, 0)))
    vp = jnp.pad(v, ((0, 0), (win, 0), (0, 0), (0, 0)))
    q_bl = q.reshape(B, nb, qb_sz, G, HPG, hd).transpose(1, 0, 2, 3, 4, 5)
    rel = jnp.arange(qb_sz)[:, None] + win - jnp.arange(qb_sz + win)[None, :]

    def one(args):
        qb, i = args
        start = i * qb_sz
        kb = lax.dynamic_slice_in_dim(kp, start, qb_sz + win, axis=1)
        vb = lax.dynamic_slice_in_dim(vp, start, qb_sz + win, axis=1)
        s = jnp.einsum('bqghd,bkgd->bghqk', qb, kb).astype(jnp.float32)
        kpos = start - win + jnp.arange(qb_sz + win)
        valid = (rel >= 0) & (rel < win) & (kpos[None, :] >= 0)
        pr = jax.nn.softmax(jnp.where(valid, s, MASK_NEG), axis=-1)
        return jnp.einsum('bghqk,bkgd->bqghd', pr.astype(vb.dtype), vb)

    o = lax.map(one, (q_bl, jnp.arange(nb)))
    return o.transpose(1, 0, 2, 3, 4, 5).reshape(B, S, G, HPG, hd)

def _nsa_mixer(h, pos, pos_k, pos_v, wk1, wk2, wv1, wv2):
    dt = h.dtype
    B, S, _ = h.shape
    G, HPG, hd = NSA_KV_HEADS, NSA_HEADS // NSA_KV_HEADS, HEAD_DIM
    q, kc, vc, ks, vs, kw, vw, gate = _split(h, NSA_COLS)
    q = _rope(q.reshape(B, S, G, HPG, hd), pos) * hd ** -0.5
    kc, ks, kw = (_rope(t.reshape(B, S, G, hd), pos) for t in (kc, ks, kw))
    vc, vs, vw = (t.reshape(B, S, G, hd) for t in (vc, vs, vw))

    k_cmp = _compress(kc, pos_k, wk1, wk2)
    v_cmp = _compress(vc, pos_v, wv1, wv2)
    nc = k_cmp.shape[1]
    s_cmp = jnp.einsum('bsghd,bcgd->bghsc', q, k_cmp).astype(jnp.float32)
    block_end = jnp.arange(nc) * NSA_CMP_STRIDE + NSA_CMP_BLOCK - 1
    valid_c = block_end[None, :] <= pos[:, None]
    p_cmp = jax.nn.softmax(jnp.where(valid_c, s_cmp, MASK_NEG), axis=-1) * valid_c
    o_cmp = jnp.einsum('bghsc,bcgd->bsghd', p_cmp.astype(v_cmp.dtype), v_cmp)

    ns = S // NSA_SEL_BLOCK
    overlap = jnp.asarray(_overlap_matrix(S))
    imp = jnp.einsum('bghsc,cj->bgsj', p_cmp, overlap)
    cur = pos // NSA_SEL_BLOCK
    j = jnp.arange(ns)[None, :]
    forced = (j == 0) | (j == cur[:, None]) | (j == cur[:, None] - 1)
    sel_score = jnp.where(forced, 1e9, jnp.where(j > cur[:, None], -1e9, imp))
    _, idx = lax.top_k(sel_score, min(NSA_N_SELECT, ns))
    o_slc = _selected_attention(q, ks, vs, idx, pos)

    o_win = _window_attention(q, kw, vw)

    gt = jax.nn.sigmoid(gate.astype(jnp.float32)).reshape(B, S, G, HPG, 3)
    o = gt[..., 0:1] * o_cmp + gt[..., 1:2] * o_slc + gt[..., 2:3] * o_win
    return o.reshape(B, S, NSA_WIDTH).astype(dt)

def second_inputs(seed: int = 0) -> dict:
    key = jax.random.key(seed)
    ks = jax.random.split(key, 40)
    D, L = D_MODEL, DEPTH

    def nrm(k, shape, scale):
        return jax.random.normal(k, shape, jnp.float32) * scale

    def gain(k, shape):
        return 1.0 + 0.05 * jax.random.normal(k, shape, jnp.float32)

    rw_in = sum(RWKV_COLS)
    return {
        'x': nrm(ks[0], (BATCH, SEQ, D), 1.0),
        'w_in': nrm(ks[1], (L, D, IN_COLS_2), D ** -0.5),
        'w_in_vres': nrm(ks[2], (L - 1, D, RWKV_VRES_RANK), D ** -0.5),
        'gla_w_a2': nrm(ks[3], (L, GLA_GATE_RANK, GLA_WIDTH), GLA_GATE_RANK ** -0.5),
        'gla_b_a': nrm(ks[4], (L, GLA_WIDTH), 0.1),
        'gla_ln_w': gain(ks[5], (L, GLA_WIDTH)),
        'gla_ln_b': nrm(ks[6], (L, GLA_WIDTH), 0.02),
        'rwkv_mu': jax.random.uniform(ks[7], (L, rw_in), jnp.float32),
        'rwkv_mu_vres': jax.random.uniform(ks[8], (L - 1, RWKV_VRES_RANK), jnp.float32),
        'rwkv_w0': jax.random.uniform(ks[9], (L, RWKV_WIDTH), jnp.float32, -5.0, 1.0),
        'rwkv_w2': nrm(ks[10], (L, RWKV_DECAY_RANK, RWKV_WIDTH), 0.5 * RWKV_DECAY_RANK ** -0.5),
        'rwkv_a0': nrm(ks[11], (L, RWKV_WIDTH), 0.1),
        'rwkv_a2': nrm(ks[12], (L, RWKV_ICLR_RANK, RWKV_WIDTH), RWKV_ICLR_RANK ** -0.5),
        'rwkv_v0': nrm(ks[13], (L - 1, RWKV_WIDTH), 0.1),
        'rwkv_v2': nrm(ks[14], (L - 1, RWKV_VRES_RANK, RWKV_WIDTH), RWKV_VRES_RANK ** -0.5),
        'rwkv_g2': nrm(ks[15], (L, RWKV_GATE_RANK, RWKV_WIDTH), RWKV_GATE_RANK ** -0.5),
        'rwkv_k_k': 0.85 + 0.05 * jax.random.normal(ks[16], (L, RWKV_WIDTH), jnp.float32),
        'rwkv_k_a': gain(ks[17], (L, RWKV_WIDTH)),
        'rwkv_r_k': nrm(ks[18], (L, RWKV_HEADS, HEAD_DIM), 0.1),
        'rwkv_ln_w': gain(ks[19], (L, RWKV_WIDTH)),
        'rwkv_ln_b': nrm(ks[20], (L, RWKV_WIDTH), 0.02),
        'nsa_pos_k': nrm(ks[21], (L, NSA_CMP_BLOCK, HEAD_DIM), 0.02),
        'nsa_pos_v': nrm(ks[22], (L, NSA_CMP_BLOCK, HEAD_DIM), 0.02),
        'nsa_wk1': nrm(ks[23], (L, NSA_CMP_BLOCK * HEAD_DIM, NSA_CMP_HIDDEN), (NSA_CMP_BLOCK * HEAD_DIM) ** -0.5),
        'nsa_wk2': nrm(ks[24], (L, NSA_CMP_HIDDEN, HEAD_DIM), NSA_CMP_HIDDEN ** -0.5),
        'nsa_wv1': nrm(ks[25], (L, NSA_CMP_BLOCK * HEAD_DIM, NSA_CMP_HIDDEN), (NSA_CMP_BLOCK * HEAD_DIM) ** -0.5),
        'nsa_wv2': nrm(ks[26], (L, NSA_CMP_HIDDEN, HEAD_DIM), NSA_CMP_HIDDEN ** -0.5),
        'w_out': nrm(ks[27], (L, D, D), DEEPNORM_BETA * D ** -0.5),
        'ln1_w': gain(ks[28], (L, D)),
        'ln1_b': nrm(ks[29], (L, D), 0.02),
        'ffn_w_gate': nrm(ks[30], (L, D, FFN_HIDDEN), D ** -0.5),
        'ffn_w_up': nrm(ks[31], (L, D, FFN_HIDDEN), D ** -0.5),
        'ffn_w_down': nrm(ks[32], (L, FFN_HIDDEN, D), DEEPNORM_BETA * FFN_HIDDEN ** -0.5),
        'ln2_w': gain(ks[33], (L, D)),
        'ln2_b': nrm(ks[34], (L, D), 0.02),
    }

def second_block(x, w_in, w_in_vres, gla_w_a2, gla_b_a, gla_ln_w, gla_ln_b,
              rwkv_mu, rwkv_mu_vres, rwkv_w0, rwkv_w2, rwkv_a0, rwkv_a2, rwkv_v0, rwkv_v2,
              rwkv_g2, rwkv_k_k, rwkv_k_a, rwkv_r_k, rwkv_ln_w, rwkv_ln_b,
              nsa_pos_k, nsa_pos_v, nsa_wk1, nsa_wk2, nsa_wv1, nsa_wv2,
              w_out, ln1_w, ln1_b, ffn_w_gate, ffn_w_up, ffn_w_down, ln2_w, ln2_b):
    pos = jnp.arange(x.shape[1], dtype=jnp.int32)
    v_first = None
    for l in range(DEPTH):
        w_cols = w_in[l] if l == 0 else jnp.concatenate([w_in[l], w_in_vres[l - 1]], axis=1)
        h = x @ w_cols
        h_gla, h_rwkv, h_nsa, h_vres = _split(
            h, (sum(GLA_COLS), sum(RWKV_COLS), sum(NSA_COLS), h.shape[-1] - IN_COLS_2))

        gq, gk, gv, gg, galr = _split(h_gla, GLA_COLS)
        o_gla = _gla_mixer(gq, gk, gv, gg, galr, gla_w_a2[l], gla_b_a[l], gla_ln_w[l], gla_ln_b[l])

        rr, rk, rv, rwlr, ralr, rglr = _split(_token_shift_mix(h_rwkv, rwkv_mu[l]), RWKV_COLS)
        if l == 0:
            v_first = rv
        else:
            vlr = _token_shift_mix(h_vres, rwkv_mu_vres[l - 1])
            rv = rv + (v_first - rv) * jax.nn.sigmoid(rwkv_v0[l - 1] + vlr @ rwkv_v2[l - 1])
        o_rwkv = _rwkv7_mixer(rr, rk, rv, rwlr, ralr, rglr, rwkv_w0[l], rwkv_w2[l], rwkv_a0[l],
                              rwkv_a2[l], rwkv_g2[l], rwkv_k_k[l], rwkv_k_a[l], rwkv_r_k[l],
                              rwkv_ln_w[l], rwkv_ln_b[l])

        o_nsa = _nsa_mixer(h_nsa, pos, nsa_pos_k[l], nsa_pos_v[l], nsa_wk1[l], nsa_wk2[l],
                           nsa_wv1[l], nsa_wv2[l])

        mix = jnp.concatenate([o_gla, o_rwkv, o_nsa], axis=-1) @ w_out[l]
        x = _layer_norm(DEEPNORM_ALPHA * x + mix, ln1_w[l], ln1_b[l])

        ffn = (jax.nn.silu(x @ ffn_w_gate[l]) * (x @ ffn_w_up[l])) @ ffn_w_down[l]
        x = _layer_norm(DEEPNORM_ALPHA * x + ffn, ln2_w[l], ln2_b[l])
    return x


def setup_inputs(seed=0):
    out = dict(first_inputs(seed))
    for name, value in second_inputs(seed + 1).items():
        if name != "x":
            out[name + "_2"] = value
    return out


def reference(
    x, mem, norm_g, w_in, mem_norm_g, w_mem_kv, w_branch, w_out, final_g, w_in_2, w_in_vres_2,
    gla_w_a2_2, gla_b_a_2, gla_ln_w_2, gla_ln_b_2, rwkv_mu_2, rwkv_mu_vres_2, rwkv_w0_2,
    rwkv_w2_2, rwkv_a0_2, rwkv_a2_2, rwkv_v0_2, rwkv_v2_2, rwkv_g2_2, rwkv_k_k_2, rwkv_k_a_2,
    rwkv_r_k_2, rwkv_ln_w_2, rwkv_ln_b_2, nsa_pos_k_2, nsa_pos_v_2, nsa_wk1_2, nsa_wk2_2,
    nsa_wv1_2, nsa_wv2_2, w_out_2, ln1_w_2, ln1_b_2, ffn_w_gate_2, ffn_w_up_2, ffn_w_down_2,
    ln2_w_2, ln2_b_2,
):
    x = first_block(
        x, mem, norm_g, w_in, mem_norm_g, w_mem_kv, w_branch, w_out, final_g,
    )
    return second_block(
        x, w_in_2, w_in_vres_2, gla_w_a2_2, gla_b_a_2, gla_ln_w_2, gla_ln_b_2, rwkv_mu_2,
        rwkv_mu_vres_2, rwkv_w0_2, rwkv_w2_2, rwkv_a0_2, rwkv_a2_2, rwkv_v0_2, rwkv_v2_2,
        rwkv_g2_2, rwkv_k_k_2, rwkv_k_a_2, rwkv_r_k_2, rwkv_ln_w_2, rwkv_ln_b_2, nsa_pos_k_2,
        nsa_pos_v_2, nsa_wk1_2, nsa_wk2_2, nsa_wv1_2, nsa_wv2_2, w_out_2, ln1_w_2, ln1_b_2,
        ffn_w_gate_2, ffn_w_up_2, ffn_w_down_2, ln2_w_2, ln2_b_2,
    )


_drawn_inputs = setup_inputs


def setup_inputs(seed=0):
    import zlib

    import numpy as np

    out = dict(_drawn_inputs(seed))
    spreads = {}
    factors = {'norm_g': 3.803,
     'mem_norm_g': 8.0,
     'final_g': 2.699,
     'gla_w_a2_2': 3.524,
     'gla_b_a_2': 8.0,
     'gla_ln_w_2': 7.358,
     'gla_ln_b_2': 8.0,
     'rwkv_mu_vres_2': 3.957,
     'rwkv_w2_2': 8.0,
     'rwkv_a0_2': 8.0,
     'rwkv_v0_2': 8.0,
     'rwkv_k_k_2': 40.163,
     'rwkv_k_a_2': 6.683,
     'rwkv_ln_w_2': 8.0,
     'rwkv_ln_b_2': 33.752,
     'nsa_pos_k_2': 64.0,
     'nsa_pos_v_2': 47.053}
    for name, (base, spread) in spreads.items():
        noise = np.random.default_rng([zlib.crc32(name.encode()), seed]).standard_normal(out[name].shape)
        drawn = base * np.exp(spread * noise) if base else spread * noise
        out[name] = jnp.asarray(drawn.astype(out[name].dtype))
    for name, factor in factors.items():
        out[name] = (out[name] * factor).astype(out[name].dtype)
    return out
```

```python
from contextlib import ExitStack

import numpy as np
import concourse.bass as bass
from concourse import mybir

P = 128
F32 = mybir.dt.float32
ALU = mybir.AluOpType
ACT = mybir.ActivationFunctionType
AX_X = mybir.AxisListType.X

D = 1024
S = 256
NT = S // P
KC = D // P
DEPTH = 2
HALF = 512
BR = 512
HD = 64
NEG = -1.0e30
TAKEN = -3.0e38
RMS_EPS = 1e-6
LN_EPS = 1e-5

AQ, AK, AV, AG, BQ, BK, BV, BG, IQ = [BR * i for i in range(9)]
IK = IQ + 512
IW = IK + 64
MQ = IW + 8
MG = MQ + BR
MIX = MG + BR
IN1 = MIX + 3 * D
TOPK = 64
RING = 5


class Count:

    def __init__(self, ctx, nc, name):
        self.sem = ctx.enter_context(nc.semaphore(name))
        ctx.sems.append(self.sem)
        self.n = 0


class Scope(ExitStack):

    def __init__(self):
        super().__init__()
        self.sems = []


class Lane:

    def __init__(self, ctx, nc, eng, name):
        self.eng = eng
        self.chain = Count(ctx, nc, name)
        self.open = {}

    def done(self, ins, signal=None):
        c = signal or self.chain
        ins.then_inc(c.sem, 1)
        c.n += 1
        self.open[c] = c.n

    def settle(self):
        for c, n in self.open.items():
            self.eng.wait_ge(c.sem, n)
        self.open = {}


class Banks:

    def __init__(self, ctx, nc, name, aps, uses):
        self.aps = aps
        self.at = {u: i for i, u in enumerate(uses)}
        assert len(self.at) == len(uses)
        self.filled = Count(ctx, nc, name + "_filled")
        self.emptied = [Count(ctx, nc, f"{name}_emptied{i}") for i in range(len(aps))]

    def fill(self, pe, use):
        i, n = self.at[use], len(self.aps)
        assert self.filled.n == i, (use, i, self.filled.n)
        if i >= n:
            pe.wait_ge(self.emptied[i % n].sem, i // n)
        return self.aps[i % n]

    def fill_ahead(self, pe, use, ahead):
        i, n = self.at[use], len(self.aps)
        assert self.filled.n + ahead == i and ahead < n
        if i >= n:
            pe.wait_ge(self.emptied[i % n].sem, i // n)
        return self.aps[i % n]

    def full(self, ins):
        ins.then_inc(self.filled.sem, 1)
        self.filled.n += 1

    def read(self, eng, use):
        i = self.at[use]
        eng.wait_ge(self.filled.sem, i + 1)
        return self.aps[i % len(self.aps)]

    def drained(self, eng, use):
        i, n = self.at[use], len(self.aps)
        for k in range(max(0, i - n + 1), i + 1):
            eng.wait_ge(self.emptied[k % n].sem, k // n + 1)

    def empty(self, lane, ins, use):
        i, n = self.at[use], len(self.aps)
        c = self.emptied[i % n]
        c.n = i // n
        lane.done(ins, c)


def close_layer(nc, sems):
    nc.all_engine_barrier()
    for s in sems:
        nc.gpsimd.sem_clear(s)
    nc.all_engine_barrier()


class Chip:

    def __init__(self, ctx, nc):
        def sb(name, shape):
            return ctx.enter_context(nc.sbuf_tensor(name, shape, F32))

        self.x = sb("x", [P, NT, D])
        self.xT = sb("xT", [P, KC, S])
        self.ring = sb("ring", [P, RING, 4, HALF])
        self.ident = sb("ident", [P, P])
        self.cbias = sb("cbias", [P, NT, S])
        self.ps = ctx.enter_context(nc.psum_tensor("ps", [P, 8, HALF], F32))

    def bank(self, i):
        return self.ps[:, i, :]


def first_prologue(nc, chip, A):
    with Scope() as ctx:
        c_in = Count(ctx, nc, "consts_in")
        raw = ctx.enter_context(nc.sbuf_tensor("mem_raw", [P, NT, D], F32))
        junk = ctx.enter_context(nc.sbuf_tensor("mem_junk", [P, D], F32))
        ss = ctx.enter_context(nc.sbuf_tensor("mem_ss", [P, 3, NT], F32))
        tp = Banks(ctx, nc, "ptp", [chip.bank(2), chip.bank(3)], [("mem", i) for i in range(KC // 2)])
        sq, rt, sc = (Count(ctx, nc, n) for n in ("mem_squares", "mem_root", "mem_scaled"))
        block = ctx.enter_context(nc.Block())

        @block.sync
        def _(sp):
            for dst, src in ((chip.ident, A["ident"]), (chip.cbias, A["cbias"]), (chip.rope1, A["rope1"]),
                             (chip.x, A["x"].rearrange("b (t p) d -> p (b t) d", p=P)),
                             (raw, A["mem"].rearrange("b (t p) d -> p (b t) d", p=P))):
                sp.dma_start(dst[:], src).then_inc(c_in.sem, 16)

        @block.scalar
        def _(act):
            lane = Lane(ctx, nc, act, "act0")
            act.wait_ge(c_in.sem, 80)
            for t in range(NT):
                lane.done(nc.scalar.activation(junk[:], raw[:, t, :], ACT.Square, accum_out=ss[:, 0, t:t + 1]), sq)
                lane.settle()
            act.wait_ge(sc.sem, 1)
            lane.done(nc.scalar.activation(ss[:, 2, :], ss[:, 1, :], ACT.Sqrt), rt)

        @block.vector
        def _(dve):
            lane = Lane(ctx, nc, dve, "dve0")
            dve.wait_ge(sq.sem, 2)
            lane.done(nc.vector.tensor_scalar(ss[:, 1, :], ss[:, 0, :], 1.0 / D, RMS_EPS, ALU.mult, ALU.add), sc)
            dve.wait_ge(rt.sem, 1)
            lane.done(nc.vector.reciprocal(ss[:, 0, :], ss[:, 2, :]))
            lane.settle()
            for t in range(NT):
                lane.done(nc.vector.tensor_scalar(raw[:, t, :], raw[:, t, :], ss[:, 0, t:t + 1], None, ALU.mult), sc)
            for i in range(KC // 2):
                b = tp.read(dve, ("mem", i))
                tp.empty(lane, nc.vector.tensor_copy(chip.memT[:, 2 * i:2 * i + 2, :],
                                                     b[:, :].rearrange("p (c t) -> p c t", c=2)), ("mem", i))
            lane.settle()

        @block.tensor
        def _(pe):
            pe.wait_ge(sc.sem, 3)
            for i in range(KC // 2):
                b = tp.fill(pe, ("mem", i))
                for c in range(2):
                    for t in range(NT):
                        ins = pe.transpose(b[:, c * S + t * P:c * S + t * P + P],
                                           raw[:, t, (2 * i + c) * P:(2 * i + c + 1) * P], chip.ident[:])
                tp.full(ins)


IDX = [("i", t, g) for t in range(NT) for g in range(2)]
ATT = ([("a", t, g) for t in range(NT) for g in range(2)] + [("m", t, 0) for t in range(NT)]
       + [("b", t, g) for t in range(NT) for g in range(2)])
GROUPS1 = IDX + ATT


HEAD = [0, 2, 1, 3]


def nkeys(kind, t):
    return S if kind == "m" else P * (t + 1)


def first_layers(nc, chip, A, layers=DEPTH):
    ctx = Scope()
    with ctx:
        def sb(name, shape):
            return ctx.enter_context(nc.sbuf_tensor(name, shape, F32))

        H = sb("H", [P, NT, IN1])
        mnT = sb("mnT", [P, KC, S])
        M = mnT[:, :, :].rearrange("p c s -> p (c s)").rearrange("p (t d) -> p t d", t=NT)
        QKT = sb("QKT", [P, 5, 4, S])
        ysT = QKT[:, 0:3, :, :].rearrange("p a c s -> p (a c) s")
        ikT = sb("ikT", [P, S])
        mqT = sb("mqT", [P, 4, S])
        kmT = sb("kmT", [P, 4, S])
        KV = sb("KV", [P, NT, D])
        gv = sb("gv", [P, 2 * KC])
        sm = sb("sm", [P, 2, 4, S])
        PT = sb("PT", [P, 2, NT, 4, P])
        ra, rb = PT[:, 0, :, :, :].rearrange("p a b c -> p (a b c)"), PT[:, 1, :, :, :].rearrange("p a b c -> p (a b c)")
        acc = sb("acc", [P, NT, S])
        bbias = sb("bbias", [P, NT, S])
        ikd = sb("ikd", [P, NT, P])
        wi = sb("wi", [P, NT, 8])
        m8 = sb("m8", [P, 8])
        st = sb("st", [P, 3, NT])
        nmx = sb("nmx", [P, len(ATT), 4])
        den = sb("den", [P, len(ATT), 4])
        rden = sb("rden", [P, len(ATT), 4])
        up = sm[:, 0, 0:2, :].rearrange("p a s -> p (a s)")
        hT = chip.xT
        x = chip.x

        w_in = A["w_in"]
        early = [8, 9, 10, 11, 4, 5, 6, 0, 1, 2]
        late = [3, 7] + list(range(12, 18))
        cols = [(j * HALF, HALF) for j in range(11)] + [(11 * HALF, MIX - 11 * HALF)] \
            + [(MIX + j * HALF, HALF) for j in range(6)]
        steps = ([("in", j) for j in early] + [("mem", 0), ("mem", 1)] + [("in", j) for j in late]
                 + [("up", h, n) for h in range(2) for n in range(3)] + [("out", 0), ("out", 1)])
        pj_uses = [(s, t) for s in steps for t in range(NT)]
        PJ = Banks(ctx, nc, "pj", [chip.bank(0), chip.bank(1)], pj_uses)
        tp_uses = [("h", i) for i in range(4)] + [("q", w, i) for w in (4, 0, 1, 2, 3) for i in range(2)] \
            + [("ik",), ("mq", 0), ("mq", 1), ("km", 0), ("km", 1)]
        tp_uses += [("o", i) for i in range(len(ATT))]
        tp_uses += [("y", i) for i in range(6)] + [("m", i) for i in range(4)]
        TP = Banks(ctx, nc, "tp", [chip.bank(2), chip.bank(3)], tp_uses)

        def chunks(ap, k0, nk, c0, w):
            return ap[k0 * P:(k0 + nk) * P, c0:c0 + w].rearrange("(c p) n -> p c n", p=P)

        g_in = Count(ctx, nc, "gains_in")
        h_sq, h_rt, h_sc, h_nm = (Count(ctx, nc, n) for n in ("h_squares", "h_root", "h_scaled", "h_normed"))
        mn_ok = Count(ctx, nc, "mn_ready")
        roped = Count(ctx, nc, "roped")
        sc_full, sc_read = Count(ctx, nc, "scores_full"), Count(ctx, nc, "scores_read")
        relu_ok, relu_used = Count(ctx, nc, "relu_ready"), Count(ctx, nc, "relu_used")
        mx_ok, p_ok = Count(ctx, nc, "max_ready"), Count(ctx, nc, "p_ready")
        pt_full, pt_ok = Count(ctx, nc, "pT_full"), Count(ctx, nc, "pT_ready")
        y_ok, g_free, g_sig, y_gated = (Count(ctx, nc, n) for n in ("y_ready", "g_free", "g_sigmoid", "y_gated"))
        m_ok = Count(ctx, nc, "m_ready")
        act_lane = Lane(ctx, nc, nc.scalar, "act1")
        dve_lane = Lane(ctx, nc, nc.vector, "dve1")
        landed = [Count(ctx, nc, f"w_landed{i}") for i in range(RING)]

        scb = chip.ps[:, 4:6, :].rearrange("p a (b n) -> p (a b) n", b=2)
        ptb = chip.ps[:, 6:8, :]

        def smv(a, j):
            kind, t, g = ATT[a]
            return sm[:, a % 2, j, 0:nkeys(kind, t)]

        def turned(b, n=2):
            return b[:, 0:n * S].rearrange("p (c t) -> p c t", c=n)

        with nc.Fori(0, layers) as l:
            items = []
            first_item = {}
            for s in steps:
                first_item[s] = len(items)
                last = (s, NT - 1)
                if s[0] == "in":
                    c0, w = cols[s[1]]
                    for kh in range(2):
                        items.append((lambda l, kh=kh, c0=c0, w=w: chunks(w_in[l], 4 * kh, 4, c0, w), w, last))
                elif s[0] == "mem":
                    for kh in range(2):
                        items.append((lambda l, kh=kh, j=s[1]: chunks(A["w_mem_kv"][l], 4 * kh, 4, j * HALF, HALF), HALF, last))
                elif s[0] == "up":
                    items.append((lambda l, h=s[1], n=s[2]: chunks(A["w_branch"][l, n], 0, 4, h * HALF, HALF), HALF, last))
                else:
                    for kh in range(2):
                        items.append((lambda l, kh=kh, j=s[1]: chunks(A["w_out"][l], 4 * kh, 4, j * HALF, HALF), HALF, last))

            with nc.Block() as block:

                @block.sync
                def _(sp):
                    sp.dma_start(gv[:], A["vec1"][l]).then_inc(g_in.sem, 16)
                    for i, (src, w, _) in enumerate(items):
                        if i >= RING:
                            sp.wait_ge(PJ.filled.sem, PJ.at[items[i - RING][2]] + 1)
                        sp.dma_start(chip.ring[:, i % RING, :, 0:w], src(l)).then_inc(landed[i % RING].sem, 16)

                @block.tensor
                def _(pe):
                    def turn(use, srcs):
                        b = TP.fill(pe, use)
                        for k, src in enumerate(srcs):
                            ins = pe.transpose(b[:, k * P:(k + 1) * P], src, chip.ident[:])
                        TP.full(ins)

                    def product(s, t, lhsT, nk, w, items_from):
                        b = PJ.fill(pe, (s, t))
                        for k in range(nk):
                            i = items_from + k // 4
                            if t == 0 and k % 4 == 0:
                                pe.wait_ge(landed[i % RING].sem, 16 * (i // RING + 1))
                            ins = pe.matmul(b[:, 0:w], lhsT[:, k, t * P:(t + 1) * P],
                                            chip.ring[:, i % RING, k % 4, 0:w], start=(k == 0), stop=(k == nk - 1))
                        PJ.full(ins)

                    def step(s, t):
                        if s[0] == "in":
                            product(s, t, hT, KC, cols[s[1]][1], first_item[s])
                        elif s[0] == "mem":
                            if s[1] == 0 and t == 0:
                                pe.wait_ge(mn_ok.sem, 1)
                            product(s, t, mnT, KC, HALF, first_item[s])
                        elif s[0] == "up":
                            product(s, t, ysT[:, 4 * s[2]:4 * s[2] + 4, :], 4, HALF, first_item[s])
                        else:
                            product(s, t, hT, KC, HALF, first_item[s])

                    def scores(n):
                        kind, t, g = GROUPS1[n]
                        if n >= 1:
                            pe.wait_ge(sc_read.sem, n)
                        for s in (0, 2, 1, 3):
                            j = HEAD[s]
                            h = 4 * g + j
                            nk = S if kind == "i" else nkeys(kind, t)
                            r = slice(64 * (h % 2), 64 * (h % 2) + 64)
                            q, k = {"i": (QKT[r, 4, h // 2], ikT[r]), "a": (QKT[r, 0, h // 2], QKT[r, 1, h // 2]),
                                    "b": (QKT[r, 2, h // 2], QKT[r, 3, h // 2]), "m": (mqT[:, j % 4], kmT[:, j % 4])}[kind]
                            ins = pe.matmul(scb[:, s, 0:nk], q[:, t * P:(t + 1) * P], k[:, 0:nk],
                                            start=True, stop=True)
                        ins.then_inc(sc_full.sem, 1)

                    def turn_p(a):
                        kind, t, g = ATT[a]
                        pe.wait_ge(p_ok.sem, a + 1)
                        if a >= 1:
                            pe.wait_ge(pt_ok.sem, a)
                        for kt in range(nkeys(kind, t) // P):
                            for j in range(4):
                                ins = pe.transpose(ptb[:, kt, j * P:(j + 1) * P], smv(a, j)[:, kt * P:(kt + 1) * P],
                                                   chip.ident[:])
                        ins.then_inc(pt_full.sem, 1)

                    def values(a):
                        kind, t, g = ATT[a]
                        b = TP.fill(pe, ("o", a))
                        pe.wait_ge(pt_ok.sem, a + 1)
                        dv = P if kind == "m" else HD
                        for s in range(4):
                            n = nkeys(kind, t) // P
                            for kt in range(n):
                                j = HEAD[s]
                                h = 4 * g + j
                                v = {"a": H[:, kt, AV + h * HD:AV + (h + 1) * HD], "b": H[:, kt, BV + h * HD:BV + (h + 1) * HD],
                                     "m": KV[:, kt, BR + (j * P) % BR:BR + (j * P) % BR + P]}[kind]
                                ins = pe.matmul(b[:, s * dv:(s + 1) * dv], PT[:, a % 2, kt, s, :], v,
                                                start=(kt == 0), stop=(kt == n - 1))
                        TP.full(ins)

                    pe.wait_ge(h_nm.sem, NT)
                    for i in range(4):
                        turn(("h", i), [H[:, t, (2 * i + c) * P:(2 * i + c + 1) * P] for c in range(2) for t in range(NT)])
                    TP.drained(pe, ("h", 3))
                    for j in early:
                        for t in range(NT):
                            step(("in", j), t)
                    for j in range(2):
                        for t in range(NT):
                            step(("mem", j), t)
                    for w, c0 in ((4, IQ), (0, AQ), (1, AK), (2, BQ), (3, BK)):
                        pe.wait_ge(roped.sem, {4: 1, 0: 2, 1: 2, 2: 3, 3: 3}[w])
                        for i in range(2):
                            turn(("q", w, i), [H[:, t, c0 + (2 * i + c) * P:c0 + (2 * i + c + 1) * P]
                                               for c in range(2) for t in range(NT)])
                    pe.wait_ge(roped.sem, 4)
                    turn(("ik",), [ikd[:, t, :] for t in range(NT)])
                    for i in range(2):
                        turn(("mq", i), [H[:, t, MQ + (2 * i + c) * P:MQ + (2 * i + c + 1) * P] for c in range(2) for t in range(NT)])
                    PJ.drained(pe, (("mem", 1), 1))
                    for i in range(2):
                        turn(("km", i), [KV[:, t, (2 * i + c) * P:(2 * i + c + 1) * P] for c in range(2) for t in range(NT)])
                    halves = [(("in", j), t) for j in late for t in range(NT)]
                    for k in range(max(len(halves), len(GROUPS1) + 2)):
                        if k < len(halves):
                            step(*halves[k])
                        if k == 0:
                            TP.drained(pe, ("km", 1))
                        if k < len(GROUPS1):
                            scores(k)
                        a = k - len(IDX)
                        if 0 <= a - 1 < len(ATT):
                            turn_p(a - 1)
                        if 0 <= a - 2 < len(ATT):
                            values(a - 2)
                    pe.wait_ge(y_gated.sem, 6)
                    for i in range(6):
                        c0 = [AQ, BQ, MQ][i // 2] + (i % 2) * 256
                        turn(("y", i), [H[:, t, c0 + c * P:c0 + (c + 1) * P] for c in range(2) for t in range(NT)])
                    TP.drained(pe, ("y", 5))
                    for s in steps:
                        if s[0] == "up":
                            for t in range(NT):
                                step(s, t)
                    pe.wait_ge(m_ok.sem, 4)
                    for i in range(4):
                        turn(("m", i), [M[:, t, (2 * i + c) * P:(2 * i + c + 1) * P] for c in range(2) for t in range(NT)])
                    TP.drained(pe, ("m", 3))
                    for h in range(2):
                        for t in range(NT):
                            step(("out", h), t)

                @block.scalar
                def _(act):
                    lane = act_lane
                    for t in range(NT):
                        lane.done(nc.scalar.activation(H[:, 0, t * D:(t + 1) * D], x[:, t, :], ACT.Square,
                                                       accum_out=st[:, 0, t:t + 1]), h_sq)
                    act.wait_ge(h_sc.sem, 1)
                    lane.done(nc.scalar.activation(st[:, 2, :], st[:, 1, :], ACT.Sqrt), h_rt)
                    lane.settle()

                    def take(s, t):
                        b = PJ.read(act, (s, t))
                        if s[0] == "in":
                            c0, w = cols[s[1]]
                            PJ.empty(lane, nc.scalar.copy(H[:, t, c0:c0 + w], b[:, 0:w]), (s, t))
                        else:
                            PJ.empty(lane, nc.scalar.copy(KV[:, t, s[1] * HALF:(s[1] + 1) * HALF], b[:, 0:HALF]), (s, t))
                    for n, j in enumerate(early):
                        for t in range(NT):
                            if n == 0 and t == 0:
                                TP.drained(act, ("h", 3))
                            take(("in", j), t)
                    for j in range(2):
                        for t in range(NT):
                            take(("mem", j), t)
                    halves = [(("in", j), t) for j in late for t in range(NT)]
                    for k in range(max(len(halves), len(GROUPS1) + 2)):
                        if k < len(halves):
                            take(*halves[k])
                        a = k - len(IDX)
                        if 0 <= a - 1 < len(ATT):
                            kind, t, g = ATT[a - 1]
                            nk = nkeys(kind, t) // P
                            act.wait_ge(pt_full.sem, a)
                            if a - 1 >= 2:
                                act.wait_ge(TP.filled.sem, TP.at[("o", a - 3)] + 1)
                            if a - 1 == 0:
                                act.wait_ge(roped.sem, 4)
                            lane.done(nc.scalar.copy(PT[:, (a - 1) % 2, 0:nk].rearrange("p k j s -> p (k j s)"),
                                                     ptb[:, 0:nk, :].rearrange("p k n -> p (k n)")), pt_ok)
                        if k < len(IDX):
                            act.wait_ge(sc_full.sem, k + 1)
                            if k >= 2:
                                act.wait_ge(relu_used.sem, k - 1)
                            lane.done(nc.scalar.activation(sm[:, k % 2], scb, ACT.Relu,
                                                           scale=float(HD) ** -0.5), sc_read)
                        elif a < len(ATT):
                            act.wait_ge(mx_ok.sem, a + 1)
                            for j in range(4):
                                lane.done(nc.scalar.activation(smv(a, j), smv(a, j), ACT.Exp, bias=nmx[:, a, j:j + 1],
                                                               accum_out=den[:, a, j:j + 1]),
                                          p_ok if j == 3 else None)
                    lane.settle()
                    act.wait_ge(g_free.sem, 3)
                    for t in range(NT):
                        lane.done(nc.scalar.activation(H[:, t, MIX:IN1], H[:, t, MIX:IN1], ACT.Sigmoid), g_sig)
                    for c0 in (AG, BG, MG):
                        lane.done(nc.scalar.activation(H[:, :, c0:c0 + BR], H[:, :, c0:c0 + BR], ACT.Sigmoid), g_sig)
                    lane.settle()
                    for i in range(4):
                        b = TP.read(act, ("m", i))
                        TP.empty(lane, nc.scalar.copy(hT[:, 2 * i:2 * i + 2, :], turned(b)), ("m", i))

                @block.vector
                def _(dve):
                    lane = dve_lane
                    v = nc.vector
                    dve.wait_ge(h_sq.sem, NT)
                    lane.done(v.tensor_scalar(st[:, 1, :], st[:, 0, :], 1.0 / D, RMS_EPS, ALU.mult, ALU.add), h_sc)
                    dve.wait_ge(h_rt.sem, 1)
                    lane.done(v.reciprocal(st[:, 0, :], st[:, 2, :]))
                    lane.settle()
                    for t in range(NT):
                        lane.done(v.tensor_scalar(H[:, t, 0:D], x[:, t, :], st[:, 0, t:t + 1], None, ALU.mult), h_nm)
                    dve.wait_ge(g_in.sem, 16)
                    for i in range(4):
                        b = TP.read(dve, ("h", i))
                        TP.empty(lane, v.tensor_tensor(hT[:, 2 * i:2 * i + 2, :], turned(b),
                                                       gv[:, 2 * i:2 * i + 2].unsqueeze(2).to_broadcast([P, 2, S]), ALU.mult),
                                 ("h", i))
                    lane.done(v.tensor_tensor(mnT[:, :, :], chip.memT[:, :, :],
                                              gv[:, KC:2 * KC].unsqueeze(2).to_broadcast([P, KC, S]), ALU.mult), mn_ok)

                    def rope(c0, nh):
                        X = H[:, :, c0:c0 + nh * HD].rearrange("p t (h d) -> p t h d", d=HD)
                        n = NT * nh * 16
                        a_ = ra[:, 0:n].rearrange("p (t h d) -> p t h d", t=NT, d=16)
                        b_ = rb[:, 0:n].rearrange("p (t h d) -> p t h d", t=NT, d=16)
                        C = chip.rope1[:, :, 0, :]
                        Sn = chip.rope1[:, :, 1, :]
                        lane.done(v.tensor_tensor(a_, X[:, :, :, 0:16], C.unsqueeze(2).to_broadcast([P, NT, nh, 16]), ALU.mult))
                        lane.done(v.tensor_tensor(b_[:, :, :, 0:8], X[:, :, :, 8:16],
                                                  Sn[:, :, 0:8].unsqueeze(2).to_broadcast([P, NT, nh, 8]), ALU.mult))
                        lane.done(v.tensor_tensor(b_[:, :, :, 8:16], X[:, :, :, 0:8],
                                                  Sn[:, :, 8:16].unsqueeze(2).to_broadcast([P, NT, nh, 8]), ALU.mult))
                        lane.settle()
                        lane.done(v.tensor_tensor(X[:, :, :, 0:16], a_, b_, ALU.add), roped)
                        lane.settle()

                    PJ.drained(dve, (("in", 9), 1))
                    rope(IQ, 9)
                    lane.done(v.tensor_scalar(wi[:, :, :], H[:, :, IW:IW + 8], 8.0 ** -0.5, None, ALU.mult))
                    PJ.drained(dve, (("in", 1), 1))
                    rope(AQ, 16)
                    rope(BQ, 16)
                    lane.done(v.tensor_copy(ikd[:, :, 0:HD], H[:, :, IK:IK + HD]))
                    lane.settle()
                    lane.done(v.tensor_copy(ikd[:, :, HD:P], H[:, :, IK:IK + HD]), roped)
                    for w in (4, 0, 1, 2, 3):
                        for i in range(2):
                            b = TP.read(dve, ("q", w, i))
                            TP.empty(lane, v.tensor_copy(QKT[:, w, 2 * i:2 * i + 2, :], turned(b)), ("q", w, i))
                    b = TP.read(dve, ("ik",))
                    TP.empty(lane, v.tensor_copy(ikT[:, :], b[:, 0:S]), ("ik",))
                    for nm, dst in (("mq", mqT), ("km", kmT)):
                        for i in range(2):
                            b = TP.read(dve, (nm, i))
                            TP.empty(lane, v.tensor_copy(dst[:, 2 * i:2 * i + 2, :], turned(b)), (nm, i))

                    def top(t):
                        nk = P * (t + 1)
                        a_ = acc[:, t, 0:nk]
                        for _ in range(TOPK // 8):
                            lane.done(v.max(m8[:, :], a_))
                            lane.settle()
                            lane.done(v.match_replace(a_, m8[:, :], a_, TAKEN))
                            lane.settle()
                        lane.done(v.tensor_scalar(bbias[:, t, 0:nk], a_, TAKEN / 2, NEG, ALU.is_gt, ALU.mult))
                        lane.settle()
                        lane.done(v.tensor_tensor(bbias[:, t, 0:nk], bbias[:, t, 0:nk], chip.cbias[:, t, 0:nk], ALU.add))
                        lane.settle()

                    def output(a):
                        kind, t, g = ATT[a]
                        dv = P if kind == "m" else HD
                        b = TP.read(dve, ("o", a))
                        dve.wait_ge(p_ok.sem, a + 1)
                        lane.done(v.reciprocal(rden[:, a, :], den[:, a, :]))
                        lane.settle()
                        c0 = {"a": AQ, "b": BQ, "m": MQ}[kind] + g * 4 * dv
                        TP.empty(lane, v.tensor_tensor(H[:, t, c0:c0 + 4 * dv].rearrange("p (a b d) -> p b a d", a=2, b=2),
                                                       b[:, 0:4 * dv].rearrange("p (b a d) -> p b a d", a=2, b=2),
                                                       rden[:, a, :].rearrange("p (b a) -> p b a", a=2).unsqueeze(3)
                                                       .to_broadcast([P, 2, 2, dv]), ALU.mult), ("o", a))

                    for k in range(len(GROUPS1) + 2):
                        a = k - len(IDX)
                        if k < len(IDX):
                            _, t, g = IDX[k]
                            dve.wait_ge(sc_read.sem, k + 1)
                            for j in range(4):
                                prev = chip.cbias[:, t, :] if g == 0 and j == 0 else acc[:, t, :]
                                lane.settle()
                                lane.done(v.scalar_tensor_tensor(out=acc[:, t, :], in0=sm[:, k % 2, HEAD.index(j), :],
                                                                 scalar=wi[:, t, 4 * g + j:4 * g + j + 1], in1=prev,
                                                                 op0=ALU.mult, op1=ALU.add), relu_used if j == 3 else None)
                            lane.settle()
                        elif a < len(ATT):
                            kind, t, g = ATT[a]
                            nk = nkeys(kind, t)
                            dve.wait_ge(sc_full.sem, k + 1)
                            if a >= 2:
                                dve.wait_ge(pt_full.sem, a - 1)
                            s_ = sm[:, a % 2, :, 0:nk]
                            if kind == "m":
                                lane.done(v.tensor_scalar(s_, scb[:, :, 0:nk], float(P) ** -0.5, None, ALU.mult), sc_read)
                            else:
                                bias = (chip.cbias if kind == "a" else bbias)[:, t, 0:nk].unsqueeze(1).to_broadcast([P, 4, nk])
                                lane.done(v.scalar_tensor_tensor(out=s_, in0=scb[:, :, 0:nk],
                                                                 scalar=float(HD) ** -0.5, in1=bias,
                                                                 op0=ALU.mult, op1=ALU.add), sc_read)
                            lane.settle()
                            lane.done(v.tensor_reduce(nmx[:, a, :], s_, AX_X, ALU.max,
                                                      negate=True), mx_ok)
                            if a in (1, 3):
                                top(a // 2)
                        if 0 <= a - 2 < len(ATT):
                            output(a - 2)
                    lane.settle()
                    PJ.drained(dve, (("in", late[-1]), 1))
                    pairs = ((AQ, AG), (BQ, BG), (MQ, MG))
                    for c0, g0 in pairs:
                        lane.done(v.tensor_tensor(H[:, :, c0:c0 + BR], H[:, :, c0:c0 + BR], H[:, :, g0:g0 + BR], ALU.mult), g_free)
                    for n, (c0, g0) in enumerate(pairs):
                        dve.wait_ge(g_sig.sem, 3 + n)
                        for t in range(NT):
                            lane.done(v.tensor_tensor(H[:, t, c0:c0 + BR], H[:, t, c0:c0 + BR], H[:, t, g0:g0 + BR], ALU.mult),
                                      y_gated)
                    for i in range(6):
                        b = TP.read(dve, ("y", i))
                        TP.empty(lane, v.tensor_copy(ysT[:, 2 * i:2 * i + 2, :], turned(b)), ("y", i))
                    for s in steps:
                        if s[0] != "up":
                            continue
                        _, h, n = s
                        for t in range(NT):
                            b = PJ.read(dve, (s, t))
                            gate = H[:, t, MIX + n * D + h * HALF:MIX + n * D + (h + 1) * HALF]
                            dst = M[:, t, h * HALF:(h + 1) * HALF]
                            if n == 0:
                                PJ.empty(lane, v.tensor_tensor(dst, b[:, :], gate, ALU.mult), (s, t))
                            else:
                                lane.settle()
                                PJ.empty(lane, v.tensor_tensor(up, b[:, :], gate, ALU.mult), (s, t))
                                lane.settle()
                                lane.done(v.tensor_tensor(dst, dst, up, ALU.add), m_ok if n == 2 else None)
                    for h in range(2):
                        for t in range(NT):
                            b = PJ.read(dve, (("out", h), t))
                            xs = x[:, t, h * HALF:(h + 1) * HALF]
                            PJ.empty(lane, v.tensor_tensor(xs, b[:, :], xs, ALU.add), (("out", h), t))
                    lane.settle()
            close_layer(nc, ctx.sems)
GQ, GK, GV, GG, GLR = 0, 256, 512, 768, 1024
RR, RK_, RV, RWA, RG = 1040, 1296, 1552, 1808, 1936
NQ = 2096
NKC, NVC, NKS, NVS, NKW, NVW, NGT = [2608 + 128 * i for i in range(7)]
VRES = NGT + 24
IN2 = VRES + 32
FFN = 2816
FC = FFN // P
ALPHA = (2 * DEPTH) ** 0.25
WIN = [0, 128, 256, 384, 768, 896, 1024, 1040, 1168, 1296, 1424, 1552, 1680, 1808, 1936, NQ - P, IN2 - P]
F_GQ, F_GK, F_GG, F_LR, F_R, F_K, F_V, F_WA, F_G0, F_G1, F_VR = 0, 2, 4, 6, 7, 9, 11, 13, 14, 15, 16
V_MU, V_W0, V_A0, V_V0, V_KK, V_KA, V_RK, V_BA, V_LNW, V_LNB, V_FLAG = 0, 10, 12, 14, 16, 18, 20, 22, 24, 28, 32
NV2 = 33
CH = 64
LEVELS = 6
M_STRICT, M_INCL, M_EYE = 6, 7, 8
E_HALF = float(np.exp(-0.5))
RWKV_GN_EPS = 64e-5
NC = 15
GROUPS2 = [(k, t, g) for k in "swc" for t in range(NT) for g in range(2)]


def second_prologue(nc, chip, A):
    with Scope() as ctx:
        c_in = Count(ctx, nc, "consts2_in")
        s_sq, s_ms, s_rt, s_rs = (Count(ctx, nc, n) for n in ("fin_squares", "fin_mean", "fin_root", "fin_scaled"))
        fg = ctx.enter_context(nc.sbuf_tensor("final_gain", [P, D], F32))
        junk = ctx.enter_context(nc.sbuf_tensor("fin_junk", [P, D], F32))
        ss = ctx.enter_context(nc.sbuf_tensor("fin_ss", [P, 3, NT], F32))
        block = ctx.enter_context(nc.Block())

        @block.sync
        def _(sp):
            for dst, src in ((fg, A["final_g"].partition_broadcast(P)), (chip.rope2, A["rope2"]), (chip.cmpb, A["cmpb"]),
                             (chip.rowv, A["rowv"]), (chip.ones, A["ones"]), (chip.masks, A["masks"]), (chip.reset, A["reset"])):
                sp.dma_start(dst[:], src).then_inc(c_in.sem, 16)

        @block.gpsimd
        def _(pool):
            pool.wait_ge(c_in.sem, 112)

        @block.scalar
        def _(act):
            lane = Lane(ctx, nc, act, "act_f")
            for t in range(NT):
                lane.done(nc.scalar.activation(junk[:], chip.x[:, t, :], ACT.Square, accum_out=ss[:, 0, t:t + 1]), s_sq)
                lane.settle()
            act.wait_ge(s_ms.sem, 1)
            lane.done(nc.scalar.activation(ss[:, 2, :], ss[:, 1, :], ACT.Sqrt), s_rt)

        @block.vector
        def _(dve):
            lane = Lane(ctx, nc, dve, "dve_f")
            lane.done(nc.vector.memset(chip.vfirst[:, :, :], 0.0))
            dve.wait_ge(s_sq.sem, NT)
            lane.done(nc.vector.tensor_scalar(ss[:, 1, :], ss[:, 0, :], 1.0 / D, RMS_EPS, ALU.mult, ALU.add), s_ms)
            dve.wait_ge(s_rt.sem, 1)
            lane.done(nc.vector.reciprocal(ss[:, 0, :], ss[:, 2, :]))
            dve.wait_ge(c_in.sem, 112)
            lane.settle()
            for t in range(NT):
                lane.done(nc.vector.scalar_tensor_tensor(out=chip.x[:, t, :], in0=chip.x[:, t, :], scalar=ss[:, 0, t:t + 1],
                                                         in1=fg[:, :], op0=ALU.mult, op1=ALU.mult), s_rs)
            lane.settle()


def second_layers(nc, chip, A, layers=DEPTH):
    ctx = Scope()
    with ctx:
        def sb(name, shape):
            return ctx.enter_context(nc.sbuf_tensor(name, shape, F32))

        x, xT, masks = chip.x, chip.xT, chip.masks
        H = sb("H2", [P, NT, IN2])
        acts = H[:, :, 0:FFN]
        OT = xT
        FT = sb("FT", [P, len(WIN), S])
        LD = sb("LD", [P, 4, S])
        CUM = sb("CUM", [P, 4, S])
        EP = sb("EP", [P, 4, S])
        EE = sb("EE", [P, 4, S])
        EN = sb("EN", [P, 2, S])
        EM = LD[:, 2:4, :]
        IC = sb("IC", [P, 2, S])
        GT = sb("GT", [P, 2, S])
        BON = sb("BON", [P, 2, S])
        KK = sb("KK", [P, 2, S])
        BB = sb("BB", [P, 2, S])
        BP = sb("BP", [P, 2, S])
        KP = sb("KP", [P, 4, S])
        GQt = sb("GQt", [P, 2, S])
        TM = sb("TM", [P, 2, S])
        TM2 = sb("TM2", [P, 2, S])
        BAt = H[:, :, 0:HALF]
        KPt = H[:, :, NQ:NQ + HALF]
        VT = H[:, :, NKC:NKC + S]
        Us = H[:, :, GG:GG + S]
        PTf = LD[:, 0:2, :]
        Wb = H[:, 0, NKS:NKS + 8 * CH].rearrange("p (u d) -> p u d", u=8)
        Qb = H[:, 1, NKS:NKS + 8 * CH].rearrange("p (u d) -> p u d", u=8)
        SP = sb("SP", [P, 4, P])
        NS = H[:, :, RR:RR + HALF]
        Y = H[:, :, RV:RV + HALF]

        gate = sb("gate", [P, NT, 24])
        st = sb("st2", [P, 4, 16])
        vec = sb("vec2s", [P, NV2])
        posT = sb("posT", [P, 2, 16])
        sw = sb("smallw", [P, 6, S])
        w2k = sb("w2k", [P, 2, P])
        w2v = sb("w2v", [P, 2, HD])
        nmx = sb("nmx2", [P, len(GROUPS2), 4])
        den = sb("den2", [P, len(GROUPS2), 4])
        fac = sb("fac2", [P, len(GROUPS2), 4])
        bn = sb("bn", [P, NT, 2, 6])
        mv = sb("mv", [P, NT, 2])
        arena = sb("arena", [P, 11264])
        top_of = {}

        def carve(part, shape):
            n = int(np.prod(shape))
            o = top_of.get(part, 0)
            top_of[part] = o + n
            assert o + n <= 11264, part
            names = "abcd"[:len(shape)]
            return arena[:, o:o + n].rearrange(f"p ({' '.join(names)}) -> p {' '.join(names)}", **dict(zip(names, shape)))

        qT = carve("nsa", [4, S])
        DD = carve("nsa", [NT, 8, 2, HD])
        KT = carve("nsa", [8, S])
        sm = carve("nsa", [2, 4, S])
        PT = carve("nsa", [2, NT, 4 * P])
        BLK = carve("nsa", [2, 16, 2 * NC])
        HID = carve("nsa", [2, 2, 2 * P])
        kcT = EP[:, 0, :].rearrange("p (g n) -> p g n", g=2)
        vcp = EP[:, 1, 0:P].rearrange("p (g n) -> p g n", g=2)
        ge = EP[:, 2:4, :].rearrange("p a s -> p (a s)")[:, 0:24 * NC].rearrange("p (i k n) -> p i k n", i=3, k=2)
        AB, AK, RB, RK, SC = (carve("rec", [8, P]) for _ in range(5))
        T_, TT, BT, UU = (carve("rec", [8, P]) for _ in range(4))
        PN = carve("rec", [2, 2, S])
        DL = arena[:, 0:10 * S].rearrange("p (c s) -> p c s", c=10)
        aT = carve("ffn", [FC, S])
        ln = carve("ffn", [4, D])
        sg = carve("ffn", [2, HALF])

        cols = [(j * HALF, min(HALF, IN2 - j * HALF)) for j in range(7)]
        fcols = [(j * HALF, min(HALF, FFN - j * HALF)) for j in range(6)]
        dk = [(4 * i, min(4, FC - 4 * i)) for i in range(6)]
        steps = ([("in", j) for j in range(7)] + [("cmp", kv) for kv in range(2)] + [("out", 0), ("out", 1)]
                 + [(k, j) for j in range(6) for k in ("gt", "up")] + [("dn", 0), ("dn", 1)])
        uses = []
        for s in steps:
            uses += [(s, 0)] if s[0] == "cmp" else [(s, t) for t in range(NT)]
        PJ = Banks(ctx, nc, "pj2", [chip.bank(0), chip.bank(1)], uses)
        items, first_item = [], {}

        def chunks(ap, k0, nk, c0, w):
            return ap[k0 * P:(k0 + nk) * P, c0:c0 + w].rearrange("(c p) n -> p c n", p=P)

        for s in steps:
            first_item[s] = len(items)
            if s[0] == "cmp":
                src = ("nsa_wk1_2", "nsa_wv1_2")[s[1]]
                items += [(lambda l, n=src, i=i: A[n][l, :, 8 * i:8 * i + 8, :].rearrange("p (c i) f -> p c (i f)", c=4), 4, HALF, (s, 0))
                          for i in range(2)]
            elif s[0] == "dn":
                items += [(lambda l, k0=k0, nk=nk, j=s[1]: chunks(A["ffn_w_down_2"][l], k0, nk, j * HALF, HALF), nk, HALF,
                           (s, 1) if k0 + nk == FC else 6 * s[1] + k0 // 4 + 1 - s[1]) for k0, nk in dk]
            else:
                name = {"in": "w_in_2", "out": "w_out_2", "gt": "ffn_w_gate_2", "up": "ffn_w_up_2"}[s[0]]
                c0, w = {"in": cols, "out": [(0, HALF), (HALF, HALF)], "gt": fcols, "up": fcols}[s[0]][s[1]]
                items += [(lambda l, n=name, kh=kh, c0=c0, w=w: chunks(A[n][l], 4 * kh, 4, c0, w), 4, w, (s, 1)) for kh in range(2)]
        landed = [Count(ctx, nc, f"w2_landed{i}") for i in range(RING)]

        tp = [("x", i) for i in range(4)] + [("f", i) for i in range(9)] + [("q", i) for i in range(2)] + [("d", i) for i in range(4)]
        tp += [("kc",), ("vc",)] + [("o", a) for a in range(len(GROUPS2))]
        tp += [("mv",), ("mw",), ("ma",), ("mg",), ("mz",), ("kn",), ("bn",), ("kp", 0), ("kp", 1), ("ba", 0), ("ba", 1), ("vt",)]
        tp += [("W",), ("Q",)]
        tp += [(k, i) for i in range(4) for k in ("U", "I", "D") if (k, i) != ("D", 3)] + [("Y", 0), ("Y", 1), ("y", 0), ("y", 1), ("n", 0), ("n", 1)]
        tp += [("x1", i) for i in range(4)] + [("a", i) for i in range(FC // 2)]
        TP = Banks(ctx, nc, "tp2", [chip.bank(2), chip.bank(3)], tp)
        pair0 = chip.ps[:, 4:6, :].rearrange("p a (b n) -> p (a b) n", b=4)
        pair1 = chip.ps[:, 6:8, :].rearrange("p a (b n) -> p (a b) n", b=4)
        ub = [("g", n) for n in range(LEVELS + 1)] + ["AB", "AK", "RB", "RK"]
        ub += [(k, n) for n in range(LEVELS) for k in ("U", "X", "XT")] + ["P"]
        UB = Banks(ctx, nc, "ub", [pair0, pair1], ub)
        scb = chip.ps[:, 4:6, :].rearrange("p a (b n) -> p (a b) n", b=2)
        ptb = chip.ps[:, 6:8, :]

        ev = {}

        def E(name):
            if name not in ev:
                ev[name] = Count(ctx, nc, "e_" + name)
            return ev[name]

        act_lane = Lane(ctx, nc, nc.scalar, "act2")
        dve_lane = Lane(ctx, nc, nc.vector, "dve2")
        HEADS = [(par, c, t) for par in range(2) for c in range(2) for t in range(NT)]

        def turned(b, n=2):
            return b[:, 0:n * S].rearrange("p (c t) -> p c t", c=n)

        def both(b):
            return b[:, :].rearrange("p (c t) -> p c t", c=2)

        def keys(g):
            return P * (GROUPS2[g][1] + 1) if GROUPS2[g][0] != "c" else P

        with nc.Fori(0, layers) as l:
          with nc.Block() as block:

            @block.sync
            def _(sp):
                for dst, src in ((vec[:], A["vec2"][l]), (sw[:], A["smallw"][l]), (posT[:], A["pos"][l]),
                                 (w2k[:, :, 0:HD], A["nsa_wk2_2"][l].rearrange("(c p) d -> p c d", p=P)),
                                 (w2k[:, :, HD:P], A["nsa_wk2_2"][l].rearrange("(c p) d -> p c d", p=P)),
                                 (w2v[:], A["nsa_wv2_2"][l].rearrange("(c p) d -> p c d", p=P))):
                    sp.dma_start(dst, src).then_inc(E("small_in").sem, 16)
                for i, (src, nk, w, _) in enumerate(items):
                    if i >= RING:
                        last = items[i - RING][3]
                        if isinstance(last, int):
                            sp.wait_ge(E("dn_used").sem, last)
                        else:
                            sp.wait_ge(PJ.filled.sem, PJ.at[last] + 1)
                    sp.dma_start(chip.ring[:, i % RING, 0:nk, 0:w], src(l)).then_inc(landed[i % RING].sem, 16)

            @block.tensor
            def _(pe):
                def turn(use, srcs):
                    b = TP.fill(pe, use)
                    for k, src in enumerate(srcs):
                        ins = pe.transpose(b[:, k * P:(k + 1) * P], src, chip.ident[:])
                    TP.full(ins)

                def landed_item(i):
                    pe.wait_ge(landed[i % RING].sem, 16 * (i // RING + 1))

                def product(s, t, lhsT, nk, w):
                    b = PJ.fill(pe, (s, t))
                    for k in range(nk):
                        i = first_item[s] + k // 4
                        if t == 0 and k % 4 == 0:
                            landed_item(i)
                        ins = pe.matmul(b[:, 0:w], lhsT[:, k, t * P:(t + 1) * P],
                                        chip.ring[:, i % RING, k % 4, 0:w], start=(k == 0), stop=(k == nk - 1))
                    PJ.full(ins)

                for i in range(4):
                    turn(("x", i), [x[:, t, (2 * i + c) * P:(2 * i + c + 1) * P] for c in range(2) for t in range(NT)])
                TP.drained(pe, ("x", 3))
                for j in range(7):
                    for t in range(NT):
                        product(("in", j), t, xT, KC, cols[j][1])
                PJ.drained(pe, (("in", 6), 1))
                for i in range(9):
                    w = WIN[2 * i:2 * i + 2]
                    turn(("f", i), [H[:, t, c0:c0 + P] for c0 in w for t in range(NT)])
                pe.wait_ge(E("roped").sem, 1)
                for i in range(2):
                    turn(("q", i), [H[:, t, NQ + (2 * i + c) * P:NQ + (2 * i + c + 1) * P] for c in range(2) for t in range(NT)])
                pe.wait_ge(E("dup").sem, 1)
                for i in range(4):
                    turn(("d", i), [DD[:, t, 2 * i + c, :, :].rearrange("p a b -> p (a b)") for c in range(2) for t in range(NT)])
                for kv in range(2):
                    s = ("cmp", kv)
                    b = PJ.fill(pe, (s, 0))
                    pe.wait_ge(E("blk").sem, kv + 1)
                    landed_item(first_item[s])
                    landed_item(first_item[s] + 1)
                    for f in range(2):
                        for i in range(16):
                            slot = chip.ring[:, (first_item[s] + i // 8) % RING].rearrange("p c (i f) -> p (c i) f", i=2)
                            ins = pe.matmul(b[:, f * 2 * NC:(f + 1) * 2 * NC], slot[:, i % 8, f * P:(f + 1) * P],
                                            BLK[:, kv, i, :], start=(i == 0), stop=(i == 15))
                    PJ.full(ins)
                pe.wait_ge(E("small_in").sem, 96)
                b = TP.fill(pe, ("kc",))
                pe.wait_ge(E("hid").sem, 1)
                for f in range(2):
                    ins = pe.matmul(b[:, 0:2 * P], w2k[:, f, :], HID[:, 0, f, :], start=(f == 0), stop=(f == 1))
                TP.full(ins)
                b = TP.fill(pe, ("vc",))
                for g in range(2):
                    for f in range(2):
                        ins = pe.matmul(b[:, g * HD:(g + 1) * HD], HID[:, 1, f, g * P:(g + 1) * P], w2v[:, f, :],
                                        start=(f == 0), stop=(f == 1))
                TP.full(ins)

                def scores(a):
                    kind, t, g = GROUPS2[a]
                    if a >= 1:
                        pe.wait_ge(E("sc_read").sem, a)
                    if kind == "c":
                        TP.drained(pe, ("vc",))
                    for s in (0, 2, 1, 3):
                        h = 4 * g + HEAD[s]
                        r = slice(64 * (h % 2), 64 * (h % 2) + 64)
                        k = {"s": KT[r, g], "w": KT[r, 2 + g], "c": kcT[r, g]}[kind]
                        ins = pe.matmul(scb[:, s, 0:keys(a)], qT[r, h // 2, t * P:(t + 1) * P], k[:, 0:keys(a)],
                                        start=True, stop=True)
                    ins.then_inc(E("sc_full").sem, 1)

                def turn_p(a):
                    pe.wait_ge(E("p").sem, a + 1)
                    if a >= 1:
                        pe.wait_ge(E("pt").sem, a)
                    for kt in range(keys(a) // P):
                        for s in range(4):
                            ins = pe.transpose(ptb[:, kt, s * P:(s + 1) * P], sm[:, a % 2, s, kt * P:(kt + 1) * P], chip.ident[:])
                    ins.then_inc(E("pt_full").sem, 1)

                def values(a):
                    kind, t, g = GROUPS2[a]
                    b = TP.fill(pe, ("o", a))
                    pe.wait_ge(E("pt").sem, a + 1)
                    n = keys(a) // P
                    for s in range(4):
                        for kt in range(n):
                            v = vcp[:, g, :] if kind == "c" else H[:, kt, {"s": NVS, "w": NVW}[kind] + g * HD:][:, 0:HD]
                            ins = pe.matmul(b[:, s * HD:(s + 1) * HD], PT[:, a % 2, kt, s * P:(s + 1) * P], v,
                                            start=(kt == 0), stop=(kt == n - 1))
                    TP.full(ins)

                TP.drained(pe, ("d", 3))
                G = len(GROUPS2)
                for k in range(G + 2):
                    if k < G:
                        scores(k)
                    if 0 <= k - 1 < G:
                        turn_p(k - 1)
                    if 0 <= k - 2 < G:
                        values(k - 2)

                def small(use, w, rhs, start=True, stop=True):
                    b = TP.aps[TP.at[use] % 2]
                    for c in range(2):
                        ins = pe.matmul(b[:, c * S:(c + 1) * S], sw[:, w, c * P:(c + 1) * P], rhs, start=start, stop=stop)
                    return ins

                TP.fill(pe, ("mv",))
                pe.wait_ge(E("shifted").sem, 1)
                TP.full(small(("mv",), 1, FT[:, F_VR, :]))
                TP.fill(pe, ("mw",))
                pe.wait_ge(E("ranks").sem, 1)
                TP.full(small(("mw",), 2, TM[:, 0, :]))
                TP.fill(pe, ("ma",))
                TP.full(small(("ma",), 3, FT[:, F_WA, :]))
                b = TP.fill(pe, ("mg",))
                pe.wait_ge(E("ranks").sem, 3)
                for c in range(2):
                    for k in range(2):
                        ins = pe.matmul(b[:, c * S:(c + 1) * S], sw[:, 4 + k, c * P:(c + 1) * P], FT[:, F_G0 + k, :],
                                        start=(k == 0), stop=(k == 1))
                TP.full(ins)
                TP.fill(pe, ("mz",))
                TP.full(small(("mz",), 0, FT[:, F_LR, :]))
                for use, e in ((("kn",), "ksq"), (("bn",), "rkr")):
                    b = TP.fill(pe, use)
                    pe.wait_ge(E(e).sem, 1)
                    TP.full(pe.matmul(b[:, :], chip.ones[:], TM2[:, :, :].rearrange("p c s -> p (c s)"), start=True, stop=True))

                def units(use, L, R, rows=True):
                    b = UB.fill(pe, use)
                    for n in range(4):
                        for par in range(2):
                            u = 4 * par + n
                            c, t = n // 2, n % 2
                            if rows:
                                r = slice(64 * par, 64 * par + 64)
                                ins = pe.matmul(b[:, u, :], L[r, c, t * P:(t + 1) * P], R[r, c, t * P:(t + 1) * P],
                                                start=True, stop=True)
                            else:
                                ins = pe.matmul(b[:, u, :], L[:, u, :], R[:, u, :], start=True, stop=True)
                    UB.full(ins)

                units(("g", 0), FT[:, F_GK:F_GK + 2, :], FT[:, F_GQ:F_GQ + 2, :])
                for n in range(LEVELS):
                    pe.wait_ge(E("pn").sem, n + 1)
                    units(("g", n + 1), PN[:, n % 2], PN[:, n % 2])
                pe.wait_ge(E("tilde").sem, 1)
                units("AB", BB, KK)
                units("AK", FT[:, F_K:F_K + 2, :], KK)
                units("RB", BB, FT[:, F_R:F_R + 2, :])
                units("RK", FT[:, F_K:F_K + 2, :], FT[:, F_R:F_R + 2, :])
                for t in range(NT):
                    turn(("kp", t), [KP[:, c, t * P:(t + 1) * P] for c in range(4)])
                for t in range(NT):
                    turn(("ba", t), [BP[:, 0, t * P:(t + 1) * P], BP[:, 1, t * P:(t + 1) * P],
                                     KK[:, 0, t * P:(t + 1) * P], KK[:, 1, t * P:(t + 1) * P]])
                turn(("vt",), [FT[:, F_V + c, t * P:(t + 1) * P] for t in range(NT) for c in range(2)])
                for n in range(LEVELS):
                    pe.wait_ge(E("bt").sem, n + 1)
                    units(("U", n), BT, T_, rows=False)
                    UB.drained(pe, ("U", n))
                    units(("X", n), TT, UU, rows=False)
                    units(("XT", n), UU, TT, rows=False)
                UB.drained(pe, ("XT", LEVELS - 1))
                TP.drained(pe, ("vt",))
                b = TP.fill(pe, ("W",))
                for u, (par, c, t) in enumerate(HEADS):
                    ins = pe.matmul(b[:, u * CH:(u + 1) * CH], AK[:, u, :], VT[:, t, (2 * c + par) * HD:(2 * c + par + 1) * HD],
                                    start=True, stop=True)
                TP.full(ins)
                b = TP.fill(pe, ("Q",))
                TP.drained(pe, ("W",))
                for u in range(8):
                    ins = pe.matmul(b[:, u * CH:(u + 1) * CH], TT[:, u, :], Wb[:, u, :], start=True, stop=True)
                TP.full(ins)
                b = UB.fill(pe, "P")
                for u, (par, c, t) in enumerate(HEADS):
                    ins = pe.matmul(b[:, u, :], BAt[:, t, 256 + c * P:256 + (c + 1) * P], TT[:, u, :], start=True, stop=True)
                UB.full(ins)
                UB.drained(pe, "P")
                for i in range(4):
                    t, r = i // 2, slice(64 * (i % 2), 64 * (i % 2) + 64)
                    pe.wait_ge(E("state").sem, 1)
                    if i:
                        TP.drained(pe, ("D", i - 1))
                    b = TP.fill(pe, ("U", i))
                    for c in range(2):
                        ins = pe.matmul(b[:, c * P:(c + 1) * P], PTf[:, c, t * P:(t + 1) * P], SP[:, 2 + c, :], start=True, stop=True)
                    TP.full(ins)
                    b = TP.fill(pe, ("I", i))
                    for c in range(4):
                        q = GQt[:, c] if c < 2 else FT[:, F_R + c - 2]
                        ins = pe.matmul(b[:, c * P:(c + 1) * P], q[:, t * P:(t + 1) * P], SP[:, c, :], start=True, stop=True)
                    TP.full(ins)
                    if i == 3:
                        continue
                    b = TP.fill(pe, ("D", i))
                    TP.drained(pe, ("U", i))
                    for c in range(4):
                        v = H[r, t, GV + c * P:GV + (c + 1) * P] if c < 2 else VT[r, t, (c - 2) * P:(c - 1) * P]
                        ins = pe.matmul(b[:, c * P:(c + 1) * P], KPt[r, t, c * P:(c + 1) * P], v, start=True, stop=(c < 2))
                        if c >= 2:
                            ins = pe.matmul(b[:, c * P:(c + 1) * P], BAt[r, t, (c - 2) * P:(c - 1) * P],
                                            Us[r, t, (c - 2) * P:(c - 1) * P], start=False, stop=True)
                    TP.full(ins)
                for t in range(NT):
                    b = TP.fill(pe, ("Y", t))
                    for c in range(2):
                        for par in range(2):
                            u, h = 4 * par + 2 * c + t, 2 * c + par
                            pe.matmul(b[:, h * HD:(h + 1) * HD], SC[:, u, :], H[:, t, GV + h * HD:GV + (h + 1) * HD],
                                      start=True, stop=True)
                            o = b[:, 256 + h * HD:256 + (h + 1) * HD]
                            pe.matmul(o, RK[:, u, :], VT[:, t, h * HD:(h + 1) * HD], start=True, stop=False)
                            ins = pe.matmul(o, RB[:, u, :], Us[:, t, h * HD:(h + 1) * HD], start=False, stop=True)
                    TP.full(ins)
                pe.wait_ge(E("normed").sem, 1)
                for i in range(2):
                    turn(("y", i), [Y[:, t, (2 * i + c) * P:(2 * i + c + 1) * P] for c in range(2) for t in range(NT)])
                for i in range(2):
                    turn(("n", i), [NS[:, t, (2 * i + c) * P:(2 * i + c + 1) * P] for c in range(2) for t in range(NT)])
                pe.wait_ge(E("mixed").sem, 2)
                TP.drained(pe, ("n", 1))
                for j in range(2):
                    for t in range(NT):
                        product(("out", j), t, OT, KC, HALF)
                pe.wait_ge(E("x1").sem, NT)
                for i in range(4):
                    turn(("x1", i), [x[:, t, (2 * i + c) * P:(2 * i + c + 1) * P] for c in range(2) for t in range(NT)])
                TP.drained(pe, ("x1", 3))

                def turn_acts(j):
                    c0, w = fcols[j]
                    PJ.drained(pe, (("up", j), 1))
                    for i in range(c0 // 256, (c0 + w) // 256):
                        turn(("a", i), [H[:, t, (2 * i + c) * P:(2 * i + c + 1) * P] for c in range(2) for t in range(NT)])

                for j in range(6):
                    for k in ("gt", "up"):
                        for t in range(NT):
                            product((k, j), t, xT, KC, fcols[j][1])
                            if j >= 1 and (k, t) == ("gt", 1):
                                turn_acts(j - 1)
                turn_acts(5)
                TP.drained(pe, ("a", FC // 2 - 1))
                for j in range(2):
                    b = [PJ.fill_ahead(pe, (("dn", j), t), t) for t in range(NT)]
                    for i, (k0, nk) in enumerate(dk):
                        landed_item(first_item[("dn", j)] + i)
                        for t in range(NT):
                            for k in range(k0, k0 + nk):
                                ins = pe.matmul(b[t][:, 0:HALF], aT[:, k, t * P:(t + 1) * P],
                                                chip.ring[:, (first_item[("dn", j)] + i) % RING, k - k0, :],
                                                start=(k == 0), stop=(k == FC - 1))
                            if i == len(dk) - 1:
                                PJ.full(ins)
                            elif t == NT - 1:
                                ins.then_inc(E("dn_used").sem, 1)

            @block.scalar
            def _(act):
                lane = act_lane
                sc = nc.scalar
                for i in range(4):
                    b = TP.read(act, ("x", i))
                    TP.empty(lane, sc.copy(xT[:, 2 * i:2 * i + 2, :], turned(b)), ("x", i))
                for j in range(7):
                    for t in range(NT):
                        b = PJ.read(act, (("in", j), t))
                        c0, w = cols[j]
                        PJ.empty(lane, sc.copy(H[:, t, c0:c0 + w], b[:, 0:w]), (("in", j), t))
                for i in range(9):
                    b = TP.read(act, ("f", i))
                    n = len(WIN[2 * i:2 * i + 2])
                    TP.empty(lane, sc.activation(FT[:, 2 * i:2 * i + n, :], turned(b, n), ACT.Copy,
                                                 scale=0.125 if i == 0 else 1.0), ("f", i))
                for i in range(2):
                    b = TP.read(act, ("q", i))
                    TP.empty(lane, sc.copy(qT[:, 2 * i:2 * i + 2, :], turned(b)), ("q", i))
                for i in range(4):
                    b = TP.read(act, ("d", i))
                    TP.empty(lane, sc.copy(KT[:, 2 * i:2 * i + 2, :], turned(b)), ("d", i))
                lane.settle()
                lane.done(sc.activation(gate[:, :, :], H[:, :, NGT:NGT + 24], ACT.Sigmoid), E("gate"))
                act.wait_ge(E("ge_in").sem, 1)
                lane.done(sc.activation(ge[:, 2], ge[:, 1], ACT.Sigmoid, scale=2.0 * 0.7978845608028654), E("ge_sig"))
                G = len(GROUPS2)
                for a in range(G + 1):
                    if a >= 1:
                        act.wait_ge(E("pt_full").sem, a)
                        if a - 1 >= 2:
                            act.wait_ge(TP.filled.sem, TP.at[("o", a - 3)] + 1)
                        n = keys(a - 1) // P
                        lane.done(sc.copy(PT[:, (a - 1) % 2, 0:n, :], ptb[:, 0:n, :]), E("pt"))
                    if a < G:
                        act.wait_ge(E("mx").sem, a + 1)
                        for s in range(4):
                            p = sm[:, a % 2, s, 0:keys(a)]
                            lane.done(sc.activation(p, p, ACT.Exp, bias=nmx[:, a, s:s + 1], accum_out=den[:, a, s:s + 1]),
                                      E("p") if s == 3 else None)
                act.wait_ge(E("shifted").sem, 1)
                lane.done(sc.activation(TM[:, 0, :], FT[:, F_WA, :], ACT.Tanh), E("ranks"))
                for k in range(2):
                    lane.done(sc.activation(FT[:, F_G0 + k, :], FT[:, F_G0 + k, :], ACT.Sigmoid), E("ranks"))
                b = TP.read(act, ("mv",))
                for c in range(2):
                    ins = sc.activation(BON[:, c, :], b[:, c * S:(c + 1) * S], ACT.Sigmoid, bias=vec[:, V_V0 + c:V_V0 + c + 1])
                    lane.done(ins) if c == 0 else TP.empty(lane, ins, ("mv",))
                b = TP.read(act, ("mw",))
                for c in range(2):
                    ins = sc.activation(LD[:, 2 + c, :], b[:, c * S:(c + 1) * S], ACT.Sigmoid, bias=vec[:, V_W0 + c:V_W0 + c + 1])
                    lane.done(ins) if c == 0 else TP.empty(lane, ins, ("mw",))
                b = TP.read(act, ("ma",))
                for c in range(2):
                    ins = sc.activation(IC[:, c, :], b[:, c * S:(c + 1) * S], ACT.Sigmoid, bias=vec[:, V_A0 + c:V_A0 + c + 1])
                    lane.done(ins) if c == 0 else TP.empty(lane, ins, ("ma",))
                b = TP.read(act, ("mg",))
                TP.empty(lane, sc.copy(GT[:, :, :], both(b)), ("mg",))
                lane.done(sc.activation(EN[:, :, :], FT[:, F_GG:F_GG + 2, :], ACT.Sigmoid), E("gg_sig"))
                b = TP.read(act, ("kn",))
                TP.empty(lane, sc.activation(TM[:, :, :], both(b), ACT.Sqrt), ("kn",))
                act.wait_ge(E("az").sem, 1)
                lane.done(sc.activation(GQt[:, :, :], GQt[:, :, :], ACT.Exp, scale=-1.0))
                lane.settle()
                lane.done(sc.activation(GQt[:, :, :], GQt[:, :, :], ACT.Ln, bias=1.0), E("lnz"))
                act.wait_ge(E("cum").sem, 1)
                lane.done(sc.activation(EP[:, :, :], CUM[:, :, :], ACT.Exp), E("exps"))
                lane.done(sc.activation(EE[:, :, :], EE[:, :, :], ACT.Exp), E("exps"))
                lane.done(sc.activation(EN[:, :, :], CUM[:, 2:4, :], ACT.Exp, scale=-1.0), E("exps"))
                lane.done(sc.activation(EM[:, :, :], EM[:, :, :], ACT.Exp), E("exps"))
                for n in range(LEVELS):
                    act.wait_ge(E("pd").sem, n + 1)
                    lane.done(sc.activation(PN[:, n % 2], PN[:, n % 2], ACT.Exp), E("pe"))
                for use, dst in ((("kp", 0), KPt[:, 0]), (("kp", 1), KPt[:, 1]), (("ba", 0), BAt[:, 0]), (("ba", 1), BAt[:, 1]),
                                 (("vt",), VT)):
                    b = TP.read(act, use)
                    TP.empty(lane, sc.copy(dst, both(b) if use == ("vt",) else b[:, :]), use)
                for n in range(LEVELS):
                    b = UB.read(act, ("U", n))
                    if n >= 1:
                        act.wait_ge(UB.filled.sem, UB.at[("XT", n - 1)] + 1)
                    UB.empty(lane, sc.copy(UU[:, :, :], b), ("U", n))
                b = TP.read(act, ("W",))
                TP.empty(lane, sc.copy(Wb[:, :, :].rearrange("p u d -> p (u d)"), b[:, :]), ("W",))
                b = TP.read(act, ("Q",))
                TP.empty(lane, sc.copy(Qb[:, :, :].rearrange("p u d -> p (u d)"), b[:, :]), ("Q",))
                b = UB.read(act, "P")
                lane.done(sc.copy(PTf[0:64, :, :].rearrange("p c s -> p (c s)"), b[0:64, 0:4, :].rearrange("p u n -> p (u n)")))
                UB.empty(lane, sc.copy(PTf[64:128, :, :].rearrange("p c s -> p (c s)"), b[64:128, 4:8, :].rearrange("p u n -> p (u n)")), "P")
                for i in range(4):
                    r = slice(64 * (i % 2), 64 * (i % 2) + 64)
                    b = TP.read(act, ("I", i))
                    TP.empty(lane, sc.copy(Y[r, i // 2, :], b[r, :]), ("I", i))
                act.wait_ge(E("var").sem, 1)
                lane.done(sc.activation(st[:, 2, :], st[:, 1, :], ACT.Sqrt), E("sd"))
                TP.drained(act, ("Y", 1))
                for k, n in enumerate(("ln1_w_2", "ln1_b_2", "ln2_w_2", "ln2_b_2")):
                    act.dma_start(ln[:, k, :], A[n][l].partition_broadcast(P)).then_inc(E("ln_in").sem, 16)
                for i in range(2):
                    b = TP.read(act, ("n", i))
                    TP.empty(lane, sc.copy(OT[:, 4 + 2 * i:6 + 2 * i, :], turned(b)), ("n", i))
                for k in range(2):
                    act.wait_ge(E("lnv").sem, k + 1)
                    lane.done(sc.activation(mv[:, :, 1], mv[:, :, 1], ACT.Sqrt), E("lns"))
                    if k == 0:
                        for i in range(4):
                            b = TP.read(act, ("x1", i))
                            TP.empty(lane, sc.copy(xT[:, 2 * i:2 * i + 2, :], turned(b)), ("x1", i))

                        def turned_acts(j):
                            c0, w = fcols[j]
                            for i in range(c0 // 256, (c0 + w) // 256):
                                b = TP.read(act, ("a", i))
                                TP.empty(lane, sc.copy(aT[:, 2 * i:2 * i + 2, :], turned(b)), ("a", i))

                        for j in range(6):
                            for t in range(NT):
                                b = PJ.read(act, (("gt", j), t))
                                if j >= 1:
                                    PJ.drained(act, (("up", j - 1), t))
                                w = fcols[j][1]
                                lane.done(sc.activation(sg[:, t, 0:w], b[:, 0:w], ACT.Sigmoid), E("sig"))
                            if j >= 1:
                                turned_acts(j - 1)
                        turned_acts(5)

            @block.vector
            def _(dve):
                lane = dve_lane
                v = nc.vector

                def tt(out, a, b, op, e=None, settle=True):
                    if settle:
                        lane.settle()
                    lane.done(v.tensor_tensor(out, a, b, op), e)

                def ts(out, a, s1, s2, o1, o2=None, e=None, settle=True):
                    if settle:
                        lane.settle()
                    ins = v.tensor_scalar(out, a, s1, s2, o1, o2) if o2 is not None else v.tensor_scalar(out, a, s1, None, o1)
                    lane.done(ins, e)

                def stt(out, a, s, b, o0, o1, e=None, settle=True):
                    if settle:
                        lane.settle()
                    lane.done(v.scalar_tensor_tensor(out=out, in0=a, scalar=s, in1=b, op0=o0, op1=o1), e)

                PJ.drained(dve, (("in", 6), 1))
                ra = sm.rearrange("p a b s -> p (a b s)")[:, 0:NT * 512].rearrange("p (t h d) -> p t h d", t=NT, d=HD)
                rb = PT.rearrange("p a b s -> p (a b s)")[:, 0:NT * 512].rearrange("p (t h d) -> p t h d", t=NT, d=HD)

                def rope(X, a_, b_, C, Sn, shape):
                    def bc(w):
                        for _ in shape[1:-1] if len(shape) == 4 else shape[1:-1]:
                            w = w.unsqueeze(len(w.shape) - 1)
                        return w
                    n = len(shape)
                    lo, hi = (slice(None),) * (n - 1) + (slice(0, 32),), (slice(None),) * (n - 1) + (slice(32, 64),)
                    c_, s_ = C, Sn
                    while len(c_.shape) < n:
                        c_, s_ = c_.unsqueeze(len(c_.shape) - 1), s_.unsqueeze(len(s_.shape) - 1)
                    half = shape[:-1] + [32]
                    tt(a_, X, c_.to_broadcast(shape), ALU.mult)
                    tt(b_[lo], X[hi], s_[(slice(None),) * (n - 1) + (slice(0, 32),)].to_broadcast(half), ALU.mult, settle=False)
                    tt(b_[hi], X[lo], s_[(slice(None),) * (n - 1) + (slice(32, 64),)].to_broadcast(half), ALU.mult, settle=False)
                    tt(X, a_, b_, ALU.add)

                rope(H[:, :, NQ:NQ + 512].rearrange("p t (h d) -> p t h d", d=HD), ra, rb,
                     chip.rope2[:, :, 0, :], chip.rope2[:, :, 1, :], [P, NT, 8, HD])
                lane.settle()
                lane.done(v.memset(HID[:, :, :, :], 0.0), E("roped"))
                for t in range(NT):
                    rope(H[:, t, NKC:NKC + 768].rearrange("p (k o d) -> p k o d", k=3, o=4)[:, :, 0:2, :],
                         ra[:, t, 0:6, :].rearrange("p (k g) d -> p k g d", k=3), rb[:, t, 0:6, :].rearrange("p (k g) d -> p k g d", k=3),
                         chip.rope2[:, t, 0, :], chip.rope2[:, t, 1, :], [P, 3, 2, HD])
                lane.settle()
                for n, c0 in enumerate((NKS, NKW, NKC, NVC)):
                    for t in range(NT):
                        src = H[:, t, c0:c0 + P].rearrange("p (g d) -> p g d", g=2).unsqueeze(2).to_broadcast([P, 2, 2, HD])
                        last = (n, t) == (3, 1)
                        if last:
                            lane.settle()
                        lane.done(v.tensor_copy(DD[:, t, 2 * n:2 * n + 2, :, :], src), E("dup") if last else None)
                TP.drained(dve, ("d", 3))
                dve.wait_ge(E("small_in").sem, 96)
                for kv in range(2):
                    for g in range(2):
                        for hf in range(2):
                            r = slice(64 * hf, 64 * hf + 64)
                            src = KT[r, 4 + 2 * kv + g, :]
                            src = src[:, 16 * hf:16 * hf + 16 * NC].rearrange("p (c i) -> p i c", i=16)
                            last = (g, hf) == (1, 1)
                            tt(BLK[r, kv, :, g * NC:(g + 1) * NC], src, posT[r, kv, :].unsqueeze(2).to_broadcast([64, 16, NC]),
                               ALU.add, E("blk") if last else None, settle=last)
                for kv in range(2):
                    b = PJ.read(dve, (("cmp", kv), 0))
                    PJ.empty(lane, v.tensor_copy(ge[:, 0, kv, :], b[:, 0:4 * NC]), (("cmp", kv), 0))
                tt(ge[:, 1], ge[:, 0], ge[:, 0], ALU.mult)
                ts(ge[:, 1], ge[:, 1], 0.044715, 1.0, ALU.mult, ALU.add)
                tt(ge[:, 1], ge[:, 1], ge[:, 0], ALU.mult, E("ge_in"))
                dve.wait_ge(E("ge_sig").sem, 1)
                hv = HID.rearrange("p k f (g n) -> p (k f) g n", g=2)[:, :, :, 0:NC]
                gv = ge.rearrange("p i k (f g c) -> p i (k f) g c", f=2, g=2)
                tt(hv, gv[:, 0], gv[:, 2], ALU.mult, E("hid"))
                b = TP.read(dve, ("kc",))
                TP.empty(lane, v.tensor_copy(EP[:, 0, :], b[:, 0:2 * P]), ("kc",))
                b = TP.read(dve, ("vc",))
                TP.empty(lane, v.tensor_copy(EP[:, 1, 0:P], b[:, 0:2 * HD]), ("vc",))

                def output(a):
                    kind, t, g = GROUPS2[a]
                    b = TP.read(dve, ("o", a))
                    dve.wait_ge(E("p").sem, a + 1)
                    f = fac[:, a, :].rearrange("p (b a) -> p b a", a=2)
                    gt = gate[:, t, :].rearrange("p (g a b k) -> p g b a k", g=2, a=2, b=2)[:, g, :, :, "csw".index(kind)]
                    lane.settle()
                    lane.done(v.reciprocal(fac[:, a, :], den[:, a, :]))
                    tt(f, f, gt, ALU.mult)
                    if kind == "c":
                        ts(fac[:, a, :], fac[:, a, :], chip.rowv[:, t:t + 1], None, ALU.mult)
                    lane.settle()
                    dst = NS[:, t, g * 256:(g + 1) * 256]
                    out = dst if kind == "s" else TM[:, 0, :]
                    TP.empty(lane, v.tensor_tensor(out.rearrange("p (a b d) -> p b a d", a=2, b=2),
                                                   b[:, 0:256].rearrange("p (b a d) -> p b a d", a=2, b=2),
                                                   f.unsqueeze(3).to_broadcast([P, 2, 2, HD]), ALU.mult), ("o", a))
                    if kind != "s":
                        tt(dst, dst, TM[:, 0, :], ALU.add)

                G = len(GROUPS2)
                dve.wait_ge(E("gate").sem, 1)
                for k in range(G + 2):
                    if k < G:
                        kind, t, g = GROUPS2[k]
                        nk = keys(k)
                        dve.wait_ge(E("sc_full").sem, k + 1)
                        if k >= 2:
                            dve.wait_ge(E("pt_full").sem, k - 1)
                        p = sm[:, k % 2, :, 0:nk]
                        bias = (chip.cmpb if kind == "c" else chip.cbias)[:, t, 0:nk].unsqueeze(1).to_broadcast([P, 4, nk])
                        stt(p, scb[:, :, 0:nk], 0.125, bias, ALU.mult, ALU.add, E("sc_read"))
                        lane.settle()
                        lane.done(v.tensor_reduce(nmx[:, k, :], p, AX_X, ALU.max, negate=True), E("mx"))
                    if k - 2 >= 0:
                        output(k - 2)

                R10 = FT[:, F_R:F_R + 10, :]
                TP.drained(dve, ("f", 8))
                tt(DL[:, :, 1:S], R10[:, :, 0:S - 1], R10[:, :, 1:S], ALU.subtract)
                ts(DL[:, :, 0:1], R10[:, :, 0:1], -1.0, None, ALU.mult, settle=False)
                lane.settle()
                for c in range(10):
                    last = c == 9
                    stt(R10[:, c, :], DL[:, c, :], vec[:, V_MU + c:V_MU + c + 1], R10[:, c, :], ALU.mult, ALU.add,
                        E("shifted") if last else None, settle=last)
                Vf, Vn = chip.vfirst[:, :, :], FT[:, F_V:F_V + 2, :]
                tt(TM2[:, :, :], Vn, Vf, ALU.subtract)
                stt(Vf, TM2[:, :, :], vec[:, V_FLAG:V_FLAG + 1], Vf, ALU.mult, ALU.add)
                tt(TM2[:, :, :], Vf, Vn, ALU.subtract)
                TP.drained(dve, ("mv",))
                tt(TM2[:, :, :], TM2[:, :, :], BON[:, :, :], ALU.mult)
                tt(Vn, Vn, TM2[:, :, :], ALU.add)
                b = TP.read(dve, ("mz",))
                for c in range(2):
                    ins = v.tensor_scalar(LD[:, c, :], b[:, c * S:(c + 1) * S], vec[:, V_BA + c:V_BA + c + 1], None, ALU.add)
                    lane.done(ins) if c == 0 else TP.empty(lane, ins, ("mz",))
                stt(GQt[:, :, :], LD[:, 0:2, :], -1.0, LD[:, 0:2, :], ALU.mult, ALU.max, E("az"))
                for c in range(2):
                    ts(KK[:, c, :], FT[:, F_K + c, :], vec[:, V_KK + c:V_KK + c + 1], None, ALU.mult, settle=False)
                tt(TM2[:, :, :], KK[:, :, :], KK[:, :, :], ALU.mult, E("ksq"))
                dve.wait_ge(E("lnz").sem, 1)
                stt(LD[:, 0:2, :], LD[:, 0:2, :], 0.0, GQt[:, :, :], ALU.min, ALU.subtract)
                ts(LD[:, 0:2, :], LD[:, 0:2, :], 1.0 / 16, None, ALU.mult)
                TP.drained(dve, ("ma",))
                ts(LD[:, 2:4, :], LD[:, 2:4, :], -E_HALF, None, ALU.mult)
                lane.settle()
                for c in range(4):
                    lane.done(v.tensor_tensor_scan(CUM[:, c, :], chip.reset[:, :], LD[:, c, :], 0.0, ALU.mult, ALU.add))
                dve.wait_ge(E("gg_sig").sem, 1)
                tt(FT[:, F_GG:F_GG + 2, :], FT[:, F_GG:F_GG + 2, :], EN[:, :, :], ALU.mult)
                cv = CUM.rearrange("p c (k t) -> p c k t", t=CH)
                tt(EE.rearrange("p c (k t) -> p c k t", t=CH), cv[:, :, :, CH - 1:CH].to_broadcast([P, 4, 4, CH]), cv, ALU.subtract)
                tt(EM[:, :, :], CUM[:, 2:4, :], LD[:, 2:4, :], ALU.subtract, E("cum"))
                Kn, Rn = FT[:, F_K:F_K + 2, :], FT[:, F_R:F_R + 2, :]
                for c in range(2):
                    ts(BB[:, c, :], IC[:, c, :], 1.0, vec[:, V_KA + c:V_KA + c + 1], ALU.subtract, ALU.mult, settle=False)
                stt(Kn, BB[:, :, :], 1.0, Kn, ALU.add, ALU.mult)
                TP.drained(dve, ("kn",))
                ts(TM[:, :, :], TM[:, :, :], 1e-12, None, ALU.max)
                lane.settle()
                lane.done(v.reciprocal(TM[:, :, :], TM[:, :, :]))
                tt(KK[:, :, :], KK[:, :, :], TM[:, :, :], ALU.mult)
                for c in range(2):
                    stt(TM2[:, c, :], FT[:, F_R + c, :], vec[:, V_RK + c:V_RK + c + 1], FT[:, F_K + c, :], ALU.mult, ALU.mult,
                        E("rkr") if c else None)
                tt(BB[:, :, :], KK[:, :, :], IC[:, :, :], ALU.mult)
                b = TP.read(dve, ("bn",))
                TP.empty(lane, v.tensor_tensor(BON[:, :, :], both(b), Vn, ALU.mult), ("bn",))
                dve.wait_ge(E("exps").sem, 4)
                tt(BP[:, :, :], BB[:, :, :], EE[:, 2:4, :], ALU.mult)
                tt(KP[:, 0:2, :], FT[:, F_GK:F_GK + 2, :], EE[:, 0:2, :], ALU.mult, settle=False)
                tt(KP[:, 2:4, :], Kn, EE[:, 2:4, :], ALU.mult, settle=False)
                tt(GQt[:, :, :], FT[:, F_GQ:F_GQ + 2, :], EP[:, 0:2, :], ALU.mult, settle=False)
                stt(KK[:, :, :], KK[:, :, :], -1.0, EM[:, :, :], ALU.mult, ALU.mult)
                tt(BB[:, :, :], BB[:, :, :], EN[:, :, :], ALU.mult)
                tt(Kn, Kn, EN[:, :, :], ALU.mult)
                tt(Rn, Rn, EP[:, 2:4, :], ALU.mult)
                lane.settle()
                lane.done(v.memset(SC[:, :, :], 0.0), E("tilde"))

                def mask(m):
                    return masks[:, m, :].unsqueeze(1).to_broadcast([P, 8, P])

                def level(n, u):
                    w = 1 << n
                    return u.rearrange("p c (k h t) -> p (c k) h t", h=2, t=w)

                for n in range(LEVELS + 1):
                    if n < LEVELS:
                        w, nb = 1 << n, S // (2 << n) * 2
                        pn, cu = level(n, PN[:, n % 2]), level(n, CUM[:, 0:2, :])
                        q_, k_ = level(n, FT[:, F_GQ:F_GQ + 2, :]), level(n, FT[:, F_GK:F_GK + 2, :])
                        mid = cu[:, :, 0, w - 1:w].to_broadcast([P, nb, w])
                        if n >= 2:
                            dve.wait_ge(UB.filled.sem, UB.at[("g", n - 1)] + 1)
                        tt(pn[:, :, 0, :], mid, cu[:, :, 0, :], ALU.subtract)
                        tt(pn[:, :, 1, :], cu[:, :, 1, :], mid, ALU.subtract, E("pd"))
                    b = UB.read(dve, ("g", n))
                    lane.settle()
                    UB.empty(lane, v.copy_predicated(SC[:, :, :], mask(M_EYE if n == 0 else n - 1).bitcast(mybir.dt.int32), b), ("g", n))
                    if n < LEVELS:
                        dve.wait_ge(E("pe").sem, n + 1)
                        tt(pn[:, :, 0, :], pn[:, :, 0, :], k_[:, :, 0, :], ALU.mult)
                        tt(pn[:, :, 1, :], pn[:, :, 1, :], q_[:, :, 1, :], ALU.mult, E("pn"))
                for use, dst, m in (("AB", AB, M_STRICT), ("AK", AK, M_STRICT), ("RB", RB, M_INCL), ("RK", RK, M_INCL)):
                    b = UB.read(dve, use)
                    UB.empty(lane, v.tensor_tensor(dst[:, :, :], b, mask(m), ALU.mult), use)
                lane.done(v.tensor_copy(T_[:, :, :], chip.ident[:].unsqueeze(1).to_broadcast([P, 8, P])))
                lane.done(v.tensor_copy(TT[:, :, :], chip.ident[:].unsqueeze(1).to_broadcast([P, 8, P])))
                for n in range(LEVELS):
                    tt(BT[:, :, :], AB[:, :, :], mask(n), ALU.mult, E("bt"))
                    b = UB.read(dve, ("X", n))
                    dve.wait_ge(UB.filled.sem, UB.at[("XT", n)] + 1)
                    lane.settle()
                    UB.empty(lane, v.tensor_tensor(T_[:, :, :], b, T_[:, :, :], ALU.add), ("X", n))
                    b = UB.read(dve, ("XT", n))
                    UB.empty(lane, v.tensor_tensor(TT[:, :, :], b, TT[:, :, :], ALU.add), ("XT", n))
                lane.settle()
                lane.done(v.memset(SP[:, :, :], 0.0), E("state"))
                for i in range(4):
                    t, r = i // 2, slice(64 * (i % 2), 64 * (i % 2) + 64)
                    b = TP.read(dve, ("U", i))
                    TP.drained(dve, ("Q",)) if i == 0 else None
                    q_ = Qb.rearrange("p (a c t) d -> p c a t d", a=2, c=2)[r, :, :, t, :]
                    lane.settle()
                    TP.empty(lane, v.tensor_tensor(Us[r, t, :].rearrange("p (c a d) -> p c a d", c=2, a=2),
                                                   b[r, 0:256].rearrange("p (c a d) -> p c a d", c=2, a=2), q_, ALU.add), ("U", i))
                    if i < 3:
                        b = TP.read(dve, ("D", i))
                        for hf in range(2):
                            h = slice(64 * hf, 64 * hf + 64)
                            tt(SP[h, :, h], SP[h, :, h], EP[h, :, i * CH + CH - 1:i * CH + CH].to_broadcast([64, 4, 64]), ALU.mult,
                               settle=False)
                        lane.settle()
                        for hf in range(2):
                            h = slice(64 * hf, 64 * hf + 64)
                            ins = v.tensor_tensor(SP[h, :, h], b.rearrange("p (c n) -> p c n", c=4)[h, :, h], SP[h, :, h], ALU.add)
                            lane.done(ins) if hf == 0 else TP.empty(lane, ins, ("D", i))
                TP.drained(dve, ("I", 3))
                for t in range(NT):
                    b = TP.read(dve, ("Y", t))
                    TP.empty(lane, v.tensor_tensor(Y[:, t, :], b[:, :], Y[:, t, :], ALU.add), ("Y", t))
                yv = Y.rearrange("p t (h d) -> p t h d", d=HD)
                sv = CUM.rearrange("p (t m) (h d) -> p t (m h) d", t=NT, d=HD)
                lane.settle()
                lane.done(v.tensor_reduce(st[:, 0, :].rearrange("p (t h) -> p t h", t=NT), yv, AX_X, ALU.add))
                ts(st[:, 0, :], st[:, 0, :], 1.0 / HD, None, ALU.mult)
                tt(yv, yv, st[:, 0, :].rearrange("p (t h) -> p t h", t=NT).unsqueeze(3).to_broadcast([P, NT, 8, HD]), ALU.subtract)
                tt(sv, yv, yv, ALU.mult)
                lane.settle()
                lane.done(v.tensor_reduce(st[:, 1, :].rearrange("p (t h) -> p t h", t=NT), sv, AX_X, ALU.add))
                s1 = st[:, 1, :].rearrange("p (t m h) -> p t m h", t=NT, m=2)
                for m, eps in ((0, LN_EPS), (1, RWKV_GN_EPS)):
                    ts(s1[:, :, m, :], s1[:, :, m, :], 1.0 / HD, eps, ALU.mult, ALU.add, E("var") if m else None)
                dve.wait_ge(E("sd").sem, 1)
                lane.settle()
                lane.done(v.reciprocal(st[:, 0, :], st[:, 2, :]))
                tt(yv, yv, st[:, 0, :].rearrange("p (t h) -> p t h", t=NT).unsqueeze(3).to_broadcast([P, NT, 8, HD]), ALU.mult, E("normed"))
                for i in range(2):
                    b = TP.read(dve, ("y", i))
                    for c in range(2):
                        ch = 2 * i + c
                        ins = v.tensor_scalar(OT[:, ch, :], b[:, c * S:(c + 1) * S], vec[:, V_LNW + ch:V_LNW + ch + 1],
                                              vec[:, V_LNB + ch:V_LNB + ch + 1], ALU.mult, ALU.add)
                        lane.done(ins) if c == 0 else TP.empty(lane, ins, ("y", i))
                tt(OT[:, 0:2, :], OT[:, 0:2, :], FT[:, F_GG:F_GG + 2, :], ALU.mult, E("mixed"))
                tt(OT[:, 2:4, :], OT[:, 2:4, :], BON[:, :, :], ALU.add)
                tt(OT[:, 2:4, :], OT[:, 2:4, :], GT[:, :, :], ALU.mult, E("mixed"))

                def residual(s):
                    for j in range(2):
                        for t in range(NT):
                            b = PJ.read(dve, ((s, j), t))
                            xs = x[:, t, j * HALF:(j + 1) * HALF]
                            PJ.empty(lane, v.scalar_tensor_tensor(out=xs, in0=xs, scalar=ALPHA, in1=b[:, :],
                                                                  op0=ALU.mult, op1=ALU.add), ((s, j), t))

                def layer_norm(k):
                    lane.settle()
                    for t in range(NT):
                        for j in range(2):
                            lane.done(v.bn_stats(bn[:, t, j, :], x[:, t, j * HALF:(j + 1) * HALF]))
                    lane.settle()
                    for t in range(NT):
                        lane.done(v.bn_aggr(mv[:, t, :], bn[:, t, :, :].rearrange("p a b -> p (a b)")))
                    ts(mv[:, :, 1], mv[:, :, 1], LN_EPS, None, ALU.add, e=E("lnv"))
                    dve.wait_ge(E("lns").sem, k + 1)
                    lane.done(v.reciprocal(mv[:, :, 1], mv[:, :, 1]))
                    lane.settle()
                    for t in range(NT):
                        ts(x[:, t, :], x[:, t, :], mv[:, t, 0:1], mv[:, t, 1:2], ALU.subtract, ALU.mult, settle=False)
                    dve.wait_ge(E("ln_in").sem, 64)
                    for t in range(NT):
                        tt(x[:, t, :], x[:, t, :], ln[:, 2 * k, :], ALU.mult)
                        tt(x[:, t, :], x[:, t, :], ln[:, 2 * k + 1, :], ALU.add, E("x1") if k == 0 else None)

                residual("out")
                layer_norm(0)
                for j in range(6):
                    c0, w = fcols[j]
                    for t in range(NT):
                        b = PJ.read(dve, (("gt", j), t))
                        dve.wait_ge(E("sig").sem, 2 * j + t + 1)
                        PJ.empty(lane, v.tensor_tensor(sg[:, t, 0:w], b[:, 0:w], sg[:, t, 0:w], ALU.mult), (("gt", j), t))
                    lane.settle()
                    for t in range(NT):
                        b = PJ.read(dve, (("up", j), t))
                        lane.settle()
                        ins = v.tensor_tensor(H[:, t, c0:c0 + w], b[:, 0:w], sg[:, t, 0:w], ALU.mult)
                        PJ.empty(lane, ins, (("up", j), t))
                residual("dn")
                layer_norm(1)
                lane.settle()
          close_layer(nc, ctx.sems)


def layout(inputs):
    a = {k: np.ascontiguousarray(v) for k, v in inputs.items()}

    def by_feature(v):
        return np.ascontiguousarray(v.reshape(DEPTH, -1, P).transpose(0, 2, 1))

    a["vec1"] = np.concatenate([by_feature(a["norm_g"]), by_feature(a["mem_norm_g"])], axis=2)
    a["ident"] = np.eye(P, dtype=np.float32)
    tok = np.arange(S).reshape(NT, P).T
    a["cbias"] = np.where(np.arange(S)[None, None, :] <= tok[:, :, None], 0.0, NEG).astype(np.float32)

    def rope(theta, half):
        inv = np.float32(theta) ** (-np.arange(half, dtype=np.float32) / np.float32(half))
        ang = tok[:, :, None].astype(np.float32) * inv[None, None, :]
        c, s = np.cos(ang), np.sin(ang)
        return np.stack([np.concatenate([c, c], -1), np.concatenate([-s, s], -1)], axis=2).astype(np.float32)

    a["rope1"] = rope(500000.0, 8)
    a["rope2"] = rope(10000.0, 32)

    def at(v, size, off):
        out = np.zeros((DEPTH, size), np.float32)
        out[:, off:off + v.shape[1]] = v
        return out

    def late(v):
        return np.concatenate([np.zeros_like(v[:1]), v], axis=0)

    mu = a["rwkv_mu_2"]
    cols = [mu[:, 0:1024], at(mu[:, 1024:], P, P - 32), at(late(a["rwkv_mu_vres_2"]), P, P - 32), a["rwkv_w0_2"], a["rwkv_a0_2"],
            late(a["rwkv_v0_2"]), a["rwkv_k_k_2"], a["rwkv_k_a_2"], a["rwkv_r_k_2"].reshape(DEPTH, -1), a["gla_b_a_2"],
            a["gla_ln_w_2"], a["rwkv_ln_w_2"], a["gla_ln_b_2"], a["rwkv_ln_b_2"],
            np.repeat(np.array([[1.0], [0.0]], np.float32), P, axis=1)]
    a["vec2"] = np.concatenate([by_feature(v) for v in cols], axis=2)

    def rows(v, off):
        out = np.zeros((DEPTH, P, S), np.float32)
        out[:, off:off + v.shape[1]] = v
        return out

    g2 = a["rwkv_g2_2"]
    a["smallw"] = np.ascontiguousarray(np.stack([
        rows(a["gla_w_a2_2"], 0), rows(late(a["rwkv_v2_2"]), P - 32), rows(a["rwkv_w2_2"], 0), rows(a["rwkv_a2_2"], 64),
        g2[:, 0:P], rows(g2[:, P:], P - 32)], axis=2))
    a["pos"] = np.ascontiguousarray(np.stack([a["nsa_pos_k_2"], a["nsa_pos_v_2"]], axis=1)
                                    .reshape(DEPTH, 2, 2, 16, HD).transpose(0, 2, 4, 1, 3).reshape(DEPTH, P, 2, 16))
    for n in ("nsa_wk1_2", "nsa_wv1_2"):
        a[n] = np.ascontiguousarray(a[n].reshape(DEPTH, 2, 16, HD, 256).transpose(0, 1, 3, 2, 4).reshape(DEPTH, P, 16, 256))
    a["w_in_2"] = np.concatenate([a["w_in_2"], late(a["w_in_vres_2"])], axis=2)
    c = np.arange(P)
    ends = 16 * c + 31
    ok = (ends[None, None, :] <= tok[:, :, None]) & (c < 15)
    a["cmpb"] = np.where(ok, 0.0, NEG).astype(np.float32)
    a["rowv"] = (tok >= 31).astype(np.float32)
    a["ones"] = (c[:, None] // 64 == c[None, :] // 64).astype(np.float32)
    s_, t_ = c[:, None], c[None, :]
    same = s_ // 64 == t_ // 64
    m = [(s_ // (2 << n) == t_ // (2 << n)) & (s_ // (1 << n) % 2 == 0) & (t_ // (1 << n) % 2 == 1) for n in range(6)]
    m += [same & (s_ < t_), same & (s_ <= t_), s_ == t_]
    a["masks"] = np.ascontiguousarray(np.stack(m, axis=1).astype(np.float32))
    a["reset"] = np.repeat((np.arange(S)[None] % 64 != 0).astype(np.float32), P, axis=0)
    return {k: a[k] for k in USED}


USED = ["x", "mem", "vec1", "w_in", "w_mem_kv", "w_branch", "w_out", "ident", "cbias", "rope1", "final_g", "rope2", "vec2",
        "smallw", "pos", "nsa_wk1_2", "nsa_wk2_2", "nsa_wv1_2", "nsa_wv2_2", "w_in_2", "w_out_2", "ffn_w_gate_2", "ffn_w_up_2",
        "ffn_w_down_2", "ln1_w_2", "ln1_b_2", "ln2_w_2", "ln2_b_2", "cmpb", "rowv", "ones", "masks", "reset"]


def build(nc, A, out, first=DEPTH, second=DEPTH):
    with ExitStack() as ctx:
        chip = Chip(ctx, nc)
        with ExitStack() as c1:
            chip.memT = c1.enter_context(nc.sbuf_tensor("memT", [P, KC, S], F32))
            chip.rope1 = c1.enter_context(nc.sbuf_tensor("rope1s", [P, NT, 2, 16], F32))
            first_prologue(nc, chip, A)
            first_layers(nc, chip, A, first)

        def sb(name, shape):
            return ctx.enter_context(nc.sbuf_tensor(name, shape, F32))

        chip.vfirst = sb("vfirst", [P, 2, S])
        chip.rope2 = sb("rope2s", [P, NT, 2, HD])
        chip.cmpb = sb("cmpb", [P, NT, P])
        chip.rowv = sb("rowv", [P, NT])
        chip.ones = sb("ones", [P, P])
        chip.masks = sb("masks", [P, 9, P])
        chip.reset = sb("reset", [P, S])
        second_prologue(nc, chip, A)
        second_layers(nc, chip, A, second)
        with Scope() as c3:
            done = Count(c3, nc, "out_written")
            with nc.Block() as block:

                @block.sync
                def _(sp):
                    sp.dma_start(out.rearrange("(t p) d -> p t d", p=P), chip.x[:]).then_inc(done.sem, 16)
                    sp.wait_ge(done.sem, 16)


def kernel(**inputs):
    import concourse.bacc as _bacc
    from concourse.bass_utils import run_bass_kernel_spmd as _run

    nc = _bacc.Bacc("TRN2", target_bir_lowering=False, num_devices=1)
    arrays = layout({n: np.asarray(v) for n, v in inputs.items()})
    A = {n: nc.dram_tensor("in_" + n, a.shape, F32, kind="ExternalInput").ap() for n, a in arrays.items()}
    out = nc.dram_tensor("out", (S, D), F32, kind="ExternalOutput").ap()
    build(nc, A, out)
    r = _run(nc, [{"in_" + n: a for n, a in arrays.items()}], core_ids=[0])
    return r.results[0]["out"].reshape(1, S, D)
```

```python
from contextlib import ExitStack

import numpy as np
import concourse.bass as bass
from concourse import mybir

P = 128
F32 = mybir.dt.float32
F32R = mybir.dt.float32r
ALU = mybir.AluOpType
ACT = mybir.ActivationFunctionType
AX_X = mybir.AxisListType.X

D = 1024
S = 256
NT = S // P
KC = D // P
DEPTH = 2
HALF = 512
BR = 512
HD = 64
NEG = -1.0e30
TAKEN = -3.0e38
RMS_EPS = 1e-6
LN_EPS = 1e-5

AQ, AK, AV, AG, BQ, BK, BV, BG, IQ = [BR * i for i in range(9)]
IK = IQ + 512
IW = IK + 64
MQ = IW + 8
MG = MQ + BR
MIX = MG + BR
IN1 = MIX + 3 * D
TOPK = 64
RAW = 3
SPLIT = 4


class Count:

    def __init__(self, ctx, nc, name):
        self.sem = ctx.enter_context(nc.semaphore(name))
        ctx.sems.append(self.sem)
        self.n = 0


class Scope(ExitStack):

    def __init__(self):
        super().__init__()
        self.sems = []


class Lane:

    def __init__(self, ctx, nc, eng, name):
        self.eng = eng
        self.chain = Count(ctx, nc, name)
        self.open = {}

    def done(self, ins, signal=None):
        c = signal or self.chain
        ins.then_inc(c.sem, 1)
        c.n += 1
        self.open[c] = c.n

    def settle(self):
        for c, n in self.open.items():
            self.eng.wait_ge(c.sem, n)
        self.open = {}




class Weights:

    def __init__(self, ctx, nc, chip, banks, name, steps, plain=()):
        self.nc, self.chip, self.banks = nc, chip, banks
        self.items, self.first, self.last = [], {}, {}
        self.kth, self.split_items, used = {}, [], 0
        for s, parts, last_use in steps:
            self.first[s] = len(self.items)
            for n, (src, nk, w) in enumerate(parts):
                i = len(self.items)
                final = n == len(parts) - 1
                used += not final
                self.items.append((src, nk, w, last_use if final else used))
                if s not in plain:
                    self.kth[i] = len(self.split_items)
                    self.split_items.append(i)
            self.last[s] = len(self.items) - 1
        self.landed = [Count(ctx, nc, f"{name}_landed{i}") for i in range(RAW)]
        self.hi_ready, self.lo_ready, self.used = (Count(ctx, nc, f"{name}_{n}") for n in ("high_ready", "low_ready", "used"))
        self.to_split = 0

    def wait_used(self, eng, i):
        last = self.items[i][3]
        if isinstance(last, int):
            eng.wait_ge(self.used.sem, last)
        else:
            eng.wait_ge(self.banks.filled.sem, self.banks.at[last] + 1)

    def wait_landed(self, eng, i):
        eng.wait_ge(self.landed[i % RAW].sem, 16 * (i // RAW + 1))

    def raw(self, i):
        return self.chip.raw[:, i % RAW]

    def part(self, i, lo):
        return self.chip.parts[:, self.kth[i] % SPLIT, lo]

    def load(self, sp, l):
        for i, (src, nk, w, _) in enumerate(self.items):
            if i >= RAW:
                j = i - RAW
                if j in self.kth:
                    sp.wait_ge(self.lo_ready.sem, self.kth[j] + 1)
                else:
                    self.wait_used(sp, j)
            sp.dma_start(self.raw(i)[:, 0:nk, 0:w], src(l)).then_inc(self.landed[i % RAW].sem, 16)

    def high(self, act, upto):
        while self.to_split < len(self.items) and self.to_split <= upto:
            i = self.to_split
            self.to_split += 1
            if i not in self.kth:
                continue
            k, (_, nk, w, _) = self.kth[i], self.items[i]
            if k >= SPLIT:
                self.wait_used(act, self.split_items[k - SPLIT])
            self.wait_landed(act, i)
            self.nc.scalar.copy(self.part(i, 0)[:, 0:nk, 0:w], self.raw(i)[:, 0:nk, 0:w]).then_inc(self.hi_ready.sem, 1)

    def low(self, pool):
        for k, i in enumerate(self.split_items):
            _, nk, w, _ = self.items[i]
            pool.wait_ge(self.hi_ready.sem, k + 1)
            self.nc.gpsimd.tensor_tensor(self.part(i, 1)[:, 0:nk, 0:w], self.raw(i)[:, 0:nk, 0:w],
                                         self.part(i, 0)[:, 0:nk, 0:w], ALU.subtract).then_inc(self.lo_ready.sem, 1)

    def multiply(self, pe, s, n, hi, lo):
        i = self.first[s] + n
        _, nk, w, _ = self.items[i]
        pe.wait_ge(self.lo_ready.sem, self.kth[i] + 1)
        for t in range(NT):
            b = self.banks.aps[self.banks.at[(s, t)] % len(self.banks.aps)]
            if n == 0:
                self.banks.fill_ahead(pe, (s, t), t)
            final = i == self.last[s]
            for c in range(nk):
                k = 2 * n + c
                for m, (a, lo_w) in enumerate(((hi, 0), (hi, 1), (lo, 0))):
                    ins = pe.matmul(b[:, 0:w], a(k, t), self.part(i, lo_w)[:, c, 0:w],
                                    start=(k == 0 and m == 0), stop=(final and c == nk - 1 and m == 2))
            if final:
                self.banks.full(ins)
            elif t == NT - 1:
                ins.then_inc(self.used.sem, 1)


class Banks:

    def __init__(self, ctx, nc, name, aps, uses):
        self.aps = aps
        self.at = {u: i for i, u in enumerate(uses)}
        assert len(self.at) == len(uses)
        self.filled = Count(ctx, nc, name + "_filled")
        self.emptied = [Count(ctx, nc, f"{name}_emptied{i}") for i in range(len(aps))]

    def fill(self, pe, use):
        i, n = self.at[use], len(self.aps)
        assert self.filled.n == i, (use, i, self.filled.n)
        if i >= n:
            pe.wait_ge(self.emptied[i % n].sem, i // n)
        return self.aps[i % n]

    def fill_ahead(self, pe, use, ahead):
        i, n = self.at[use], len(self.aps)
        assert self.filled.n + ahead == i and ahead < n
        if i >= n:
            pe.wait_ge(self.emptied[i % n].sem, i // n)
        return self.aps[i % n]

    def full(self, ins):
        ins.then_inc(self.filled.sem, 1)
        self.filled.n += 1

    def read(self, eng, use):
        i = self.at[use]
        eng.wait_ge(self.filled.sem, i + 1)
        return self.aps[i % len(self.aps)]

    def taken(self, eng, use):
        i, n = self.at[use], len(self.aps)
        eng.wait_ge(self.emptied[i % n].sem, i // n + 1)

    def drained(self, eng, use):
        i, n = self.at[use], len(self.aps)
        for k in range(max(0, i - n + 1), i + 1):
            eng.wait_ge(self.emptied[k % n].sem, k // n + 1)

    def empty(self, lane, ins, use):
        i, n = self.at[use], len(self.aps)
        c = self.emptied[i % n]
        c.n = i // n
        lane.done(ins, c)


class Places:

    def __init__(self, ctx, nc):
        self.ctx, self.nc, self.offset = ctx, nc, {}

    def __call__(self, name, shape):
        self.offset[name] = -(-self.nc.sbuf_base // 32) * 32
        return self.ctx.enter_context(self.nc.sbuf_tensor(name, shape, F32))

    def over(self, name, place, shape, skip=0):
        return self.nc.alloc_sbuf_tensor_at(name, shape, F32R, offset=self.offset[place] + 4 * skip)


def close_layer(nc, sems):
    nc.all_engine_barrier()
    for s in sems:
        nc.gpsimd.sem_clear(s)
    nc.all_engine_barrier()


class Chip:

    def __init__(self, ctx, nc):
        def sb(name, shape, dtype=F32):
            return ctx.enter_context(nc.sbuf_tensor(name, shape, dtype))

        self.x = sb("x", [P, NT, D])
        self.xT = sb("xT", [P, KC, S], F32R)
        self.raw = sb("raw", [P, RAW, 2, HALF])
        self.parts = sb("parts", [P, SPLIT, 2, 2, HALF], F32R)
        self.ident = sb("ident", [P, P])
        self.cbias = sb("cbias", [P, NT, S])
        self.ps = ctx.enter_context(nc.psum_tensor("ps", [P, 8, HALF], F32))

    def bank(self, i):
        return self.ps[:, i, :]


def first_prologue(nc, chip, A):
    with Scope() as ctx:
        c_in = Count(ctx, nc, "consts_in")
        raw = ctx.enter_context(nc.sbuf_tensor("mem_raw", [P, NT, D], F32))
        junk = ctx.enter_context(nc.sbuf_tensor("mem_junk", [P, D], F32))
        ss = ctx.enter_context(nc.sbuf_tensor("mem_ss", [P, 3, NT], F32))
        tp = Banks(ctx, nc, "ptp", [chip.bank(2), chip.bank(3)], [("mem", i) for i in range(KC // 2)])
        sq, rt, sc = (Count(ctx, nc, n) for n in ("mem_squares", "mem_root", "mem_scaled"))
        block = ctx.enter_context(nc.Block())

        @block.sync
        def _(sp):
            for dst, src in ((chip.ident, A["ident"]), (chip.cbias, A["cbias"]), (chip.rope1, A["rope1"]),
                             (chip.x, A["x"].rearrange("b (t p) d -> p (b t) d", p=P)),
                             (raw, A["mem"].rearrange("b (t p) d -> p (b t) d", p=P))):
                sp.dma_start(dst[:], src).then_inc(c_in.sem, 16)

        @block.scalar
        def _(act):
            lane = Lane(ctx, nc, act, "act0")
            act.wait_ge(c_in.sem, 80)
            for t in range(NT):
                lane.done(nc.scalar.activation(junk[:], raw[:, t, :], ACT.Square, accum_out=ss[:, 0, t:t + 1]), sq)
                lane.settle()
            act.wait_ge(sc.sem, 1)
            lane.done(nc.scalar.activation(ss[:, 2, :], ss[:, 1, :], ACT.Sqrt), rt)

        @block.vector
        def _(dve):
            lane = Lane(ctx, nc, dve, "dve0")
            dve.wait_ge(sq.sem, 2)
            lane.done(nc.vector.tensor_scalar(ss[:, 1, :], ss[:, 0, :], 1.0 / D, RMS_EPS, ALU.mult, ALU.add), sc)
            dve.wait_ge(rt.sem, 1)
            lane.done(nc.vector.reciprocal(ss[:, 0, :], ss[:, 2, :]))
            lane.settle()
            for t in range(NT):
                lane.done(nc.vector.tensor_scalar(raw[:, t, :], raw[:, t, :], ss[:, 0, t:t + 1], None, ALU.mult), sc)
            for i in range(KC // 2):
                b = tp.read(dve, ("mem", i))
                tp.empty(lane, nc.vector.tensor_copy(chip.memT[:, 2 * i:2 * i + 2, :],
                                                     b[:, :].rearrange("p (c t) -> p c t", c=2)), ("mem", i))
            lane.settle()

        @block.tensor
        def _(pe):
            pe.wait_ge(sc.sem, 3)
            for i in range(KC // 2):
                b = tp.fill(pe, ("mem", i))
                for c in range(2):
                    for t in range(NT):
                        ins = pe.transpose(b[:, c * S + t * P:c * S + t * P + P],
                                           raw[:, t, (2 * i + c) * P:(2 * i + c + 1) * P], chip.ident[:])
                tp.full(ins)


IDX = [("i", t, g) for t in range(NT) for g in range(2)]
ATT = ([("a", t, g) for t in range(NT) for g in range(2)] + [("m", t, 0) for t in range(NT)]
       + [("b", t, g) for t in range(NT) for g in range(2)])
GROUPS1 = IDX + ATT


HEAD = [0, 2, 1, 3]


def nkeys(kind, t):
    return S if kind == "m" else P * (t + 1)


def first_layers(nc, chip, A, layers=DEPTH):
    ctx = Scope()
    with ctx:
        sb = Places(ctx, nc)
        H = sb("H", [P, NT, IN1])
        H_lo = sb.over("H_low", "H", [P, NT, IN1])
        M = sb("M", [P, NT, D])
        M_lo = sb.over("M_low", "M", [P, NT, D])
        QKT = sb("QKT", [P, 5, 4, S])
        ysT = sb.over("ysT", "QKT", [P, 12, S])
        ikT = sb("ikT", [P, S])
        mqT = sb("mqT", [P, 4, S])
        kmT = sb("kmT", [P, 4, S])
        KV = sb("KV", [P, NT, D])
        gv = sb("gv", [P, 2 * KC])
        sm = sb("sm", [P, 2, 4, S])
        PT = sb("PT", [P, 2, NT, 4, P])
        mn_hi = sb.over("mn_high", "sm", [P, KC, S])
        mn_lo = sb.over("mn_low", "PT", [P, KC, S])
        acc = sb("acc", [P, NT, S])
        bbias = sb("bbias", [P, NT, S])
        ra, rb = acc[:, :, :].rearrange("p t s -> p (t s)"), bbias[:, :, :].rearrange("p t s -> p (t s)")
        ikd = sb("ikd", [P, NT, P])
        wi = sb("wi", [P, NT, 8])
        m8 = sb("m8", [P, 8])
        st = sb("st", [P, 3, NT])
        nmx = sb("nmx", [P, len(ATT), 4])
        den = sb("den", [P, len(ATT), 4])
        rden = sb("rden", [P, len(ATT), 4])
        up = sm[:, 0, 0:2, :].rearrange("p a s -> p (a s)")
        hT = chip.xT
        x = chip.x

        w_in = A["w_in"]
        early = [8, 9, 10, 11, 4, 5, 6, 0, 1, 2]
        late = [3, 7] + list(range(12, 18))
        cols = [(j * HALF, HALF) for j in range(11)] + [(11 * HALF, MIX - 11 * HALF)] \
            + [(MIX + j * HALF, HALF) for j in range(6)]
        steps = ([("in", j) for j in early] + [("mem", 0), ("mem", 1)] + [("in", j) for j in late]
                 + [("up", h, n) for h in range(2) for n in range(3)] + [("out", 0), ("out", 1)])
        late_parts = [(("in", j), n) for j in late for n in range(KC // 2)]
        pj_uses = [(s, t) for s in steps for t in range(NT)]
        PJ = Banks(ctx, nc, "pj", [chip.bank(0), chip.bank(1)], pj_uses)
        tp_uses = [("h", i) for i in range(4)] + [("q", w, i) for w in (4, 0, 1, 2, 3) for i in range(2)] \
            + [("ik",), ("mq", 0), ("mq", 1), ("km", 0), ("km", 1)]
        tp_uses += [("o", i) for i in range(len(ATT))]
        tp_uses += [("y", i) for i in range(6)] + [("m", i) for i in range(4)]
        TP = Banks(ctx, nc, "tp", [chip.bank(2), chip.bank(3)], tp_uses)

        def chunks(ap, k0, nk, c0, w):
            return ap[k0 * P:(k0 + nk) * P, c0:c0 + w].rearrange("(c p) n -> p c n", p=P)

        g_in = Count(ctx, nc, "gains_in")
        h_sq, h_rt, h_sc, h_nm = (Count(ctx, nc, n) for n in ("h_squares", "h_root", "h_scaled", "h_normed"))
        mn_ok = Count(ctx, nc, "mn_ready")
        roped = Count(ctx, nc, "roped")
        sc_full, sc_read = Count(ctx, nc, "scores_full"), Count(ctx, nc, "scores_read")
        relu_ok, relu_used = Count(ctx, nc, "relu_ready"), Count(ctx, nc, "relu_used")
        mx_ok, p_ok = Count(ctx, nc, "max_ready"), Count(ctx, nc, "p_ready")
        pt_full, pt_ok = Count(ctx, nc, "pT_full"), Count(ctx, nc, "pT_ready")
        y_ok, g_free, g_sig, y_gated = (Count(ctx, nc, n) for n in ("y_ready", "g_free", "g_sigmoid", "y_gated"))
        m_ok = Count(ctx, nc, "m_ready")
        m_hi = Count(ctx, nc, "m_high")
        act_lane = Lane(ctx, nc, nc.scalar, "act1")
        dve_lane = Lane(ctx, nc, nc.vector, "dve1")
        scb = chip.ps[:, 4:6, :].rearrange("p a (b n) -> p (a b) n", b=2)
        ptb = chip.ps[:, 6:8, :]

        def smv(a, j):
            kind, t, g = ATT[a]
            return sm[:, a % 2, j, 0:nkeys(kind, t)]

        def turned(b, n=2):
            return b[:, 0:n * S].rearrange("p (c t) -> p c t", c=n)

        with nc.Fori(0, layers) as l:
            parts = []
            for s in steps:
                w = HALF
                if s[0] == "in":
                    c0, w = cols[s[1]]
                    name = "w_in"
                elif s[0] == "up":
                    name, c0 = "w_branch", s[1] * HALF
                else:
                    name, c0 = {"mem": "w_mem_kv", "out": "w_out"}[s[0]], s[1] * HALF
                if s[0] == "up":
                    src = [lambda l, q=q, c0=c0, n=s[2]: chunks(A["w_branch"][l, n], 2 * q, 2, c0, HALF) for q in range(2)]
                else:
                    src = [lambda l, q=q, c0=c0, w=w, n=name: chunks(A[n][l], 2 * q, 2, c0, w) for q in range(KC // 2)]
                parts.append((s, [(f, 2, w) for f in src], (s, NT - 1)))
            W = Weights(ctx, nc, chip, PJ, "w", parts)

            with nc.Block() as block:

                @block.sync
                def _(sp):
                    sp.dma_start(gv[:], A["vec1"][l]).then_inc(g_in.sem, 16)
                    W.load(sp, l)

                @block.gpsimd
                def _(pool):
                    W.low(pool)

                @block.tensor
                def _(pe):
                    def turn(use, srcs):
                        b = TP.fill(pe, use)
                        for k, src in enumerate(srcs):
                            ins = pe.transpose(b[:, k * P:(k + 1) * P], src, chip.ident[:])
                        TP.full(ins)

                    def hi_of(T):
                        return lambda k, t: T[:, k, t * P:(t + 1) * P]

                    def step_part(s, n):
                        hi, lo = hi_of(hT), lambda k, t: M_lo[:, t, k * P:(k + 1) * P]
                        if s[0] == "mem":
                            if (s[1], n) == (0, 0):
                                pe.wait_ge(mn_ok.sem, 1)
                            hi, lo = hi_of(mn_hi), hi_of(mn_lo)
                        elif s[0] == "up":
                            c0 = (AQ, BQ, MQ)[s[2]]
                            hi, lo = hi_of(ysT[:, 4 * s[2]:4 * s[2] + 4, :]), lambda k, t: H_lo[:, t, c0 + k * P:c0 + (k + 1) * P]
                        W.multiply(pe, s, n, hi, lo)

                    def step(s):
                        for n in range(W.last[s] - W.first[s] + 1):
                            step_part(s, n)

                    def scores(n):
                        kind, t, g = GROUPS1[n]
                        if n >= 1:
                            pe.wait_ge(sc_read.sem, n)
                        for s in (0, 2, 1, 3):
                            j = HEAD[s]
                            h = 4 * g + j
                            nk = S if kind == "i" else nkeys(kind, t)
                            r = slice(64 * (h % 2), 64 * (h % 2) + 64)
                            q, k = {"i": (QKT[r, 4, h // 2], ikT[r]), "a": (QKT[r, 0, h // 2], QKT[r, 1, h // 2]),
                                    "b": (QKT[r, 2, h // 2], QKT[r, 3, h // 2]), "m": (mqT[:, j % 4], kmT[:, j % 4])}[kind]
                            ins = pe.matmul(scb[:, s, 0:nk], q[:, t * P:(t + 1) * P], k[:, 0:nk],
                                            start=True, stop=True)
                        ins.then_inc(sc_full.sem, 1)

                    def turn_p(a):
                        kind, t, g = ATT[a]
                        pe.wait_ge(p_ok.sem, a + 1)
                        if a >= 1:
                            pe.wait_ge(pt_ok.sem, a)
                        for kt in range(nkeys(kind, t) // P):
                            for j in range(4):
                                ins = pe.transpose(ptb[:, kt, j * P:(j + 1) * P], smv(a, j)[:, kt * P:(kt + 1) * P],
                                                   chip.ident[:])
                        ins.then_inc(pt_full.sem, 1)

                    def values(a):
                        kind, t, g = ATT[a]
                        b = TP.fill(pe, ("o", a))
                        pe.wait_ge(pt_ok.sem, a + 1)
                        dv = P if kind == "m" else HD
                        for s in range(4):
                            n = nkeys(kind, t) // P
                            for kt in range(n):
                                j = HEAD[s]
                                h = 4 * g + j
                                v = {"a": H[:, kt, AV + h * HD:AV + (h + 1) * HD], "b": H[:, kt, BV + h * HD:BV + (h + 1) * HD],
                                     "m": KV[:, kt, BR + (j * P) % BR:BR + (j * P) % BR + P]}[kind]
                                ins = pe.matmul(b[:, s * dv:(s + 1) * dv], PT[:, a % 2, kt, s, :], v,
                                                start=(kt == 0), stop=(kt == n - 1))
                        TP.full(ins)

                    pe.wait_ge(h_nm.sem, NT)
                    for i in range(4):
                        turn(("h", i), [H[:, t, (2 * i + c) * P:(2 * i + c + 1) * P] for c in range(2) for t in range(NT)])
                    TP.drained(pe, ("h", 3))
                    for j in early:
                        step(("in", j))
                    for j in range(2):
                        step(("mem", j))
                    for w, c0 in ((4, IQ), (0, AQ), (1, AK), (2, BQ), (3, BK)):
                        pe.wait_ge(roped.sem, {4: 1, 0: 2, 1: 2, 2: 3, 3: 3}[w])
                        for i in range(2):
                            turn(("q", w, i), [H[:, t, c0 + (2 * i + c) * P:c0 + (2 * i + c + 1) * P]
                                               for c in range(2) for t in range(NT)])
                    pe.wait_ge(roped.sem, 4)
                    turn(("ik",), [ikd[:, t, :] for t in range(NT)])
                    for i in range(2):
                        turn(("mq", i), [H[:, t, MQ + (2 * i + c) * P:MQ + (2 * i + c + 1) * P] for c in range(2) for t in range(NT)])
                    PJ.drained(pe, (("mem", 1), 1))
                    for i in range(2):
                        turn(("km", i), [KV[:, t, (2 * i + c) * P:(2 * i + c + 1) * P] for c in range(2) for t in range(NT)])
                    for k in range(max(len(late_parts), len(GROUPS1) + 2)):
                        if k < len(late_parts):
                            step_part(*late_parts[k])
                        if k == 0:
                            TP.drained(pe, ("km", 1))
                        if k < len(GROUPS1):
                            scores(k)
                        a = k - len(IDX)
                        if 0 <= a - 1 < len(ATT):
                            turn_p(a - 1)
                        if 0 <= a - 2 < len(ATT):
                            values(a - 2)
                    pe.wait_ge(y_gated.sem, 6)
                    for i in range(6):
                        c0 = [AQ, BQ, MQ][i // 2] + (i % 2) * 256
                        turn(("y", i), [H[:, t, c0 + c * P:c0 + (c + 1) * P] for c in range(2) for t in range(NT)])
                    TP.drained(pe, ("y", 5))
                    for s in steps:
                        if s[0] == "up":
                            step(s)
                    pe.wait_ge(m_ok.sem, 4)
                    for i in range(4):
                        turn(("m", i), [M[:, t, (2 * i + c) * P:(2 * i + c + 1) * P] for c in range(2) for t in range(NT)])
                    TP.drained(pe, ("m", 3))
                    for h in range(2):
                        step(("out", h))

                @block.scalar
                def _(act):
                    lane = act_lane
                    for t in range(NT):
                        lane.done(nc.scalar.activation(H[:, 0, t * D:(t + 1) * D], x[:, t, :], ACT.Square,
                                                       accum_out=st[:, 0, t:t + 1]), h_sq)
                    W.high(act, SPLIT - 2)
                    act.wait_ge(h_sc.sem, 1)
                    lane.done(nc.scalar.activation(st[:, 2, :], st[:, 1, :], ACT.Sqrt), h_rt)
                    lane.settle()

                    def take(s, t):
                        b = PJ.read(act, (s, t))
                        if s[0] == "in":
                            c0, w = cols[s[1]]
                            PJ.empty(lane, nc.scalar.copy(H[:, t, c0:c0 + w], b[:, 0:w]), (s, t))
                        else:
                            PJ.empty(lane, nc.scalar.copy(KV[:, t, s[1] * HALF:(s[1] + 1) * HALF], b[:, 0:HALF]), (s, t))
                    def pace(s, n):
                        W.high(act, W.first[s] + n + SPLIT - 1)
                        if W.first[s] + n == W.last[s] and s[0] in ("in", "mem"):
                            for t in range(NT):
                                take(s, t)

                    for s in [("in", j) for j in early] + [("mem", 0), ("mem", 1)]:
                        for n in range(KC // 2):
                            if s == ("in", early[0]) and n == KC // 2 - 1:
                                TP.drained(act, ("h", 3))
                            pace(s, n)
                    for k in range(max(len(late_parts), len(GROUPS1) + 2)):
                        if k < len(late_parts):
                            pace(*late_parts[k])
                        a = k - len(IDX)
                        if 0 <= a - 1 < len(ATT):
                            kind, t, g = ATT[a - 1]
                            nk = nkeys(kind, t) // P
                            act.wait_ge(pt_full.sem, a)
                            if a - 1 >= 2:
                                act.wait_ge(TP.filled.sem, TP.at[("o", a - 3)] + 1)
                            lane.done(nc.scalar.copy(PT[:, (a - 1) % 2, 0:nk].rearrange("p k j s -> p (k j s)"),
                                                     ptb[:, 0:nk, :].rearrange("p k n -> p (k n)")), pt_ok)
                        if k < len(IDX):
                            act.wait_ge(sc_full.sem, k + 1)
                            if k >= 2:
                                act.wait_ge(relu_used.sem, k - 1)
                            lane.done(nc.scalar.activation(sm[:, k % 2], scb, ACT.Relu,
                                                           scale=float(HD) ** -0.5), sc_read)
                        elif a < len(ATT):
                            act.wait_ge(mx_ok.sem, a + 1)
                            for j in range(4):
                                lane.done(nc.scalar.activation(smv(a, j), smv(a, j), ACT.Exp, bias=nmx[:, a, j:j + 1],
                                                               accum_out=den[:, a, j:j + 1]),
                                          p_ok if j == 3 else None)
                    lane.settle()
                    act.wait_ge(g_free.sem, 3)
                    for t in range(NT):
                        lane.done(nc.scalar.activation(H[:, t, MIX:IN1], H[:, t, MIX:IN1], ACT.Sigmoid), g_sig)
                    for c0 in (AG, BG, MG):
                        lane.done(nc.scalar.activation(H[:, :, c0:c0 + BR], H[:, :, c0:c0 + BR], ACT.Sigmoid), g_sig)
                    lane.settle()
                    for s in steps:
                        if s[0] == "up":
                            for n in range(2):
                                pace(s, n)
                    for i in range(4):
                        b = TP.read(act, ("m", i))
                        lane.done(nc.scalar.copy(hT[:, 2 * i:2 * i + 2, :], turned(b)), m_hi)
                    for j in range(2):
                        for n in range(KC // 2):
                            pace(("out", j), n)

                @block.vector
                def _(dve):
                    lane = dve_lane
                    v = nc.vector

                    def by_tile(u):
                        return u.rearrange("p (t n) -> p t n", t=NT)

                    def low_of(k):
                        return M_lo[:, :, k * P:(k + 1) * P]

                    dve.wait_ge(h_sq.sem, NT)
                    lane.done(v.tensor_scalar(st[:, 1, :], st[:, 0, :], 1.0 / D, RMS_EPS, ALU.mult, ALU.add), h_sc)
                    dve.wait_ge(h_rt.sem, 1)
                    lane.done(v.reciprocal(st[:, 0, :], st[:, 2, :]))
                    lane.settle()
                    for t in range(NT):
                        lane.done(v.tensor_scalar(H[:, t, 0:D], x[:, t, :], st[:, 0, t:t + 1], None, ALU.mult), h_nm)
                    dve.wait_ge(g_in.sem, 16)
                    for i in range(4):
                        b = TP.read(dve, ("h", i))
                        lane.done(v.tensor_tensor(hT[:, 2 * i:2 * i + 2, :], turned(b),
                                                  gv[:, 2 * i:2 * i + 2].unsqueeze(2).to_broadcast([P, 2, S]), ALU.mult))
                        lane.settle()
                        for c in range(2):
                            k = 2 * i + c
                            ins = v.scalar_tensor_tensor(out=low_of(k), in0=by_tile(b[:, c * S:(c + 1) * S]), scalar=gv[:, k:k + 1],
                                                         in1=by_tile(hT[:, k, :]), op0=ALU.mult, op1=ALU.subtract)
                            lane.done(ins) if c == 0 else TP.empty(lane, ins, ("h", i))
                    lane.done(v.tensor_tensor(mn_hi[:, :, :], chip.memT[:, :, :],
                                              gv[:, KC:2 * KC].unsqueeze(2).to_broadcast([P, KC, S]), ALU.mult))
                    lane.settle()
                    for k in range(KC):
                        lane.done(v.scalar_tensor_tensor(out=mn_lo[:, k, :], in0=chip.memT[:, k, :], scalar=gv[:, KC + k:KC + k + 1],
                                                         in1=mn_hi[:, k, :], op0=ALU.mult, op1=ALU.subtract),
                                  mn_ok if k == KC - 1 else None)

                    def rope(c0, nh):
                        X = H[:, :, c0:c0 + nh * HD].rearrange("p t (h d) -> p t h d", d=HD)
                        n = NT * nh * 16
                        a_ = ra[:, 0:n].rearrange("p (t h d) -> p t h d", t=NT, d=16)
                        b_ = rb[:, 0:n].rearrange("p (t h d) -> p t h d", t=NT, d=16)
                        C = chip.rope1[:, :, 0, :]
                        Sn = chip.rope1[:, :, 1, :]
                        lane.done(v.tensor_tensor(a_, X[:, :, :, 0:16], C.unsqueeze(2).to_broadcast([P, NT, nh, 16]), ALU.mult))
                        lane.done(v.tensor_tensor(b_[:, :, :, 0:8], X[:, :, :, 8:16],
                                                  Sn[:, :, 0:8].unsqueeze(2).to_broadcast([P, NT, nh, 8]), ALU.mult))
                        lane.done(v.tensor_tensor(b_[:, :, :, 8:16], X[:, :, :, 0:8],
                                                  Sn[:, :, 8:16].unsqueeze(2).to_broadcast([P, NT, nh, 8]), ALU.mult))
                        lane.settle()
                        lane.done(v.tensor_tensor(X[:, :, :, 0:16], a_, b_, ALU.add), roped)
                        lane.settle()

                    PJ.drained(dve, (("in", 9), 1))
                    rope(IQ, 9)
                    lane.done(v.tensor_scalar(wi[:, :, :], H[:, :, IW:IW + 8], 8.0 ** -0.5, None, ALU.mult))
                    PJ.drained(dve, (("in", 1), 1))
                    rope(AQ, 16)
                    rope(BQ, 16)
                    lane.done(v.tensor_copy(ikd[:, :, 0:HD], H[:, :, IK:IK + HD]))
                    lane.settle()
                    lane.done(v.tensor_copy(ikd[:, :, HD:P], H[:, :, IK:IK + HD]), roped)
                    for w in (4, 0, 1, 2, 3):
                        for i in range(2):
                            b = TP.read(dve, ("q", w, i))
                            TP.empty(lane, v.tensor_copy(QKT[:, w, 2 * i:2 * i + 2, :], turned(b)), ("q", w, i))
                    b = TP.read(dve, ("ik",))
                    TP.empty(lane, v.tensor_copy(ikT[:, :], b[:, 0:S]), ("ik",))
                    for nm, dst in (("mq", mqT), ("km", kmT)):
                        for i in range(2):
                            b = TP.read(dve, (nm, i))
                            TP.empty(lane, v.tensor_copy(dst[:, 2 * i:2 * i + 2, :], turned(b)), (nm, i))

                    def top(t):
                        nk = P * (t + 1)
                        a_ = acc[:, t, 0:nk]
                        for _ in range(TOPK // 8):
                            lane.done(v.max(m8[:, :], a_))
                            lane.settle()
                            lane.done(v.match_replace(a_, m8[:, :], a_, TAKEN))
                            lane.settle()
                        lane.done(v.tensor_scalar(bbias[:, t, 0:nk], a_, TAKEN / 2, NEG, ALU.is_gt, ALU.mult))
                        lane.settle()
                        lane.done(v.tensor_tensor(bbias[:, t, 0:nk], bbias[:, t, 0:nk], chip.cbias[:, t, 0:nk], ALU.add))
                        lane.settle()

                    def output(a):
                        kind, t, g = ATT[a]
                        dv = P if kind == "m" else HD
                        b = TP.read(dve, ("o", a))
                        dve.wait_ge(p_ok.sem, a + 1)
                        lane.done(v.reciprocal(rden[:, a, :], den[:, a, :]))
                        lane.settle()
                        c0 = {"a": AQ, "b": BQ, "m": MQ}[kind] + g * 4 * dv
                        TP.empty(lane, v.tensor_tensor(H[:, t, c0:c0 + 4 * dv].rearrange("p (a b d) -> p b a d", a=2, b=2),
                                                       b[:, 0:4 * dv].rearrange("p (b a d) -> p b a d", a=2, b=2),
                                                       rden[:, a, :].rearrange("p (b a) -> p b a", a=2).unsqueeze(3)
                                                       .to_broadcast([P, 2, 2, dv]), ALU.mult), ("o", a))

                    for k in range(len(GROUPS1) + 2):
                        a = k - len(IDX)
                        if k < len(IDX):
                            _, t, g = IDX[k]
                            dve.wait_ge(sc_read.sem, k + 1)
                            for j in range(4):
                                prev = chip.cbias[:, t, :] if g == 0 and j == 0 else acc[:, t, :]
                                lane.settle()
                                lane.done(v.scalar_tensor_tensor(out=acc[:, t, :], in0=sm[:, k % 2, HEAD.index(j), :],
                                                                 scalar=wi[:, t, 4 * g + j:4 * g + j + 1], in1=prev,
                                                                 op0=ALU.mult, op1=ALU.add), relu_used if j == 3 else None)
                            lane.settle()
                        elif a < len(ATT):
                            kind, t, g = ATT[a]
                            nk = nkeys(kind, t)
                            dve.wait_ge(sc_full.sem, k + 1)
                            if a >= 2:
                                dve.wait_ge(pt_full.sem, a - 1)
                            s_ = sm[:, a % 2, :, 0:nk]
                            if kind == "m":
                                lane.done(v.tensor_scalar(s_, scb[:, :, 0:nk], float(P) ** -0.5, None, ALU.mult), sc_read)
                            else:
                                bias = (chip.cbias if kind == "a" else bbias)[:, t, 0:nk].unsqueeze(1).to_broadcast([P, 4, nk])
                                lane.done(v.scalar_tensor_tensor(out=s_, in0=scb[:, :, 0:nk],
                                                                 scalar=float(HD) ** -0.5, in1=bias,
                                                                 op0=ALU.mult, op1=ALU.add), sc_read)
                            lane.settle()
                            lane.done(v.tensor_reduce(nmx[:, a, :], s_, AX_X, ALU.max,
                                                      negate=True), mx_ok)
                            if a in (1, 3):
                                top(a // 2)
                        if 0 <= a - 2 < len(ATT):
                            output(a - 2)
                    lane.settle()
                    PJ.drained(dve, (("in", late[-1]), 1))
                    pairs = ((AQ, AG), (BQ, BG), (MQ, MG))
                    for c0, g0 in pairs:
                        lane.done(v.tensor_tensor(H[:, :, c0:c0 + BR], H[:, :, c0:c0 + BR], H[:, :, g0:g0 + BR], ALU.mult), g_free)
                    for n, (c0, g0) in enumerate(pairs):
                        dve.wait_ge(g_sig.sem, 3 + n)
                        for t in range(NT):
                            lane.done(v.tensor_tensor(H[:, t, c0:c0 + BR], H[:, t, c0:c0 + BR], H[:, t, g0:g0 + BR], ALU.mult),
                                      y_gated)
                    for i in range(6):
                        b = TP.read(dve, ("y", i))
                        hi = ysT[:, 2 * i:2 * i + 2, :]
                        lane.done(v.tensor_copy(hi, turned(b)))
                        lane.settle()
                        c0 = [AQ, BQ, MQ][i // 2] + (i % 2) * 256
                        TP.empty(lane, v.tensor_tensor(H_lo[:, :, c0:c0 + 256].rearrange("p t (c n) -> p c t n", c=2),
                                                       turned(b).rearrange("p c (t n) -> p c t n", t=NT),
                                                       hi.rearrange("p c (t n) -> p c t n", t=NT), ALU.subtract), ("y", i))
                    for s in steps:
                        if s[0] != "up":
                            continue
                        _, h, n = s
                        for t in range(NT):
                            b = PJ.read(dve, (s, t))
                            gate = H[:, t, MIX + n * D + h * HALF:MIX + n * D + (h + 1) * HALF]
                            dst = M[:, t, h * HALF:(h + 1) * HALF]
                            if n == 0:
                                PJ.empty(lane, v.tensor_tensor(dst, b[:, :], gate, ALU.mult), (s, t))
                            else:
                                lane.settle()
                                PJ.empty(lane, v.tensor_tensor(up, b[:, :], gate, ALU.mult), (s, t))
                                lane.settle()
                                lane.done(v.tensor_tensor(dst, dst, up, ALU.add), m_ok if n == 2 else None)
                    for i in range(4):
                        b = TP.read(dve, ("m", i))
                        dve.wait_ge(m_hi.sem, i + 1)
                        TP.empty(lane, v.tensor_tensor(M_lo[:, :, 2 * i * P:(2 * i + 2) * P].rearrange("p t (c n) -> p c t n", c=2),
                                                       turned(b).rearrange("p c (t n) -> p c t n", t=NT),
                                                       hT[:, 2 * i:2 * i + 2, :].rearrange("p c (t n) -> p c t n", t=NT),
                                                       ALU.subtract), ("m", i))
                    for h in range(2):
                        for t in range(NT):
                            b = PJ.read(dve, (("out", h), t))
                            xs = x[:, t, h * HALF:(h + 1) * HALF]
                            PJ.empty(lane, v.tensor_tensor(xs, b[:, :], xs, ALU.add), (("out", h), t))
                    lane.settle()
            close_layer(nc, ctx.sems)
GQ, GK, GV, GG, GLR = 0, 256, 512, 768, 1024
RR, RK_, RV, RWA, RG = 1040, 1296, 1552, 1808, 1936
NQ = 2096
NKC, NVC, NKS, NVS, NKW, NVW, NGT = [2608 + 128 * i for i in range(7)]
VRES = NGT + 24
IN2 = VRES + 32
FFN = 2816
FC = FFN // P
ALPHA = (2 * DEPTH) ** 0.25
WIN = [0, 128, 256, 384, 768, 896, 1024, 1040, 1168, 1296, 1424, 1552, 1680, 1808, 1936, NQ - P, IN2 - P]
F_GQ, F_GK, F_GG, F_LR, F_R, F_K, F_V, F_WA, F_G0, F_G1, F_VR = 0, 2, 4, 6, 7, 9, 11, 13, 14, 15, 16
V_MU, V_W0, V_A0, V_V0, V_KK, V_KA, V_RK, V_BA, V_LNW, V_LNB, V_FLAG = 0, 10, 12, 14, 16, 18, 20, 22, 24, 28, 32
NV2 = 33
CH = 64
LEVELS = 6
M_STRICT, M_INCL, M_EYE = 6, 7, 8
E_HALF = float(np.exp(-0.5))
RWKV_GN_EPS = 64e-5
NC = 15
GROUPS2 = [(k, t, g) for k in "swc" for t in range(NT) for g in range(2)]


def second_prologue(nc, chip, A):
    with Scope() as ctx:
        c_in = Count(ctx, nc, "consts2_in")
        s_sq, s_ms, s_rt, s_rs = (Count(ctx, nc, n) for n in ("fin_squares", "fin_mean", "fin_root", "fin_scaled"))
        fg = ctx.enter_context(nc.sbuf_tensor("final_gain", [P, D], F32))
        junk = ctx.enter_context(nc.sbuf_tensor("fin_junk", [P, D], F32))
        ss = ctx.enter_context(nc.sbuf_tensor("fin_ss", [P, 3, NT], F32))
        block = ctx.enter_context(nc.Block())

        @block.sync
        def _(sp):
            for dst, src in ((fg, A["final_g"].partition_broadcast(P)), (chip.rope2, A["rope2"]), (chip.cmpb, A["cmpb"]),
                             (chip.rowv, A["rowv"]), (chip.ones, A["ones"]), (chip.masks, A["masks"]), (chip.reset, A["reset"])):
                sp.dma_start(dst[:], src).then_inc(c_in.sem, 16)

        @block.scalar
        def _(act):
            lane = Lane(ctx, nc, act, "act_f")
            for t in range(NT):
                lane.done(nc.scalar.activation(junk[:], chip.x[:, t, :], ACT.Square, accum_out=ss[:, 0, t:t + 1]), s_sq)
                lane.settle()
            act.wait_ge(s_ms.sem, 1)
            lane.done(nc.scalar.activation(ss[:, 2, :], ss[:, 1, :], ACT.Sqrt), s_rt)

        @block.vector
        def _(dve):
            lane = Lane(ctx, nc, dve, "dve_f")
            lane.done(nc.vector.memset(chip.vfirst[:, :, :], 0.0))
            dve.wait_ge(s_sq.sem, NT)
            lane.done(nc.vector.tensor_scalar(ss[:, 1, :], ss[:, 0, :], 1.0 / D, RMS_EPS, ALU.mult, ALU.add), s_ms)
            dve.wait_ge(s_rt.sem, 1)
            lane.done(nc.vector.reciprocal(ss[:, 0, :], ss[:, 2, :]))
            dve.wait_ge(c_in.sem, 112)
            lane.settle()
            for t in range(NT):
                lane.done(nc.vector.scalar_tensor_tensor(out=chip.x[:, t, :], in0=chip.x[:, t, :], scalar=ss[:, 0, t:t + 1],
                                                         in1=fg[:, :], op0=ALU.mult, op1=ALU.mult), s_rs)
            lane.settle()


def second_layers(nc, chip, A, layers=DEPTH):
    ctx = Scope()
    with ctx:
        sb = Places(ctx, nc)
        x, xT, masks = chip.x, chip.xT, chip.masks
        H = sb("H2", [P, NT, IN2])
        H_lo = sb.over("H2_low", "H2", [P, NT, IN2])
        OT = xT
        FT = sb("FT", [P, len(WIN), S])
        LD = sb("LD", [P, 4, S])
        CUM = sb("CUM", [P, 4, S])
        EP = sb("EP", [P, 4, S])
        EE = sb("EE", [P, 4, S])
        EN = sb("EN", [P, 2, S])
        EM = LD[:, 2:4, :]
        IC = sb("IC", [P, 2, S])
        GT = sb("GT", [P, 2, S])
        BON = sb("BON", [P, 2, S])
        KK = sb("KK", [P, 2, S])
        BB = sb("BB", [P, 2, S])
        BP = sb("BP", [P, 2, S])
        DL = sb("DL", [P, 10, S])
        KP, GQt, TM, TM2 = DL[:, 0:4, :], DL[:, 4:6, :], DL[:, 6:8, :], DL[:, 8:10, :]
        BAt = H[:, :, 0:HALF]
        KPt = H[:, :, NQ:NQ + HALF]
        VT = H[:, :, NKC:NKC + S]
        Us = H[:, :, GG:GG + S]
        PTf = LD[:, 0:2, :]
        Wb = H[:, 0, NKS:NKS + 8 * CH].rearrange("p (u d) -> p u d", u=8)
        Qb = H[:, 1, NKS:NKS + 8 * CH].rearrange("p (u d) -> p u d", u=8)
        SP = sb("SP", [P, 4, P])
        NS = H[:, :, RR:RR + HALF]
        Y = H[:, :, RV:RV + HALF]
        HID = H[:, :, RV:RV + HALF].rearrange("p k (f n) -> p k f n", f=2)
        ge = H[:, :, GG:GG + 12 * NC].rearrange("p k (i n) -> p i k n", i=3)
        kcT = H[:, 0, 0:S].rearrange("p (g n) -> p g n", g=2)
        vcp = H[:, 1, 0:P].rearrange("p (g n) -> p g n", g=2)
        part_out = H[:, 0, S:2 * S]

        gate = sb("gate", [P, NT, 24])
        st = sb("st2", [P, 4, 16])
        vec = sb("vec2s", [P, NV2])
        posT = sb("posT", [P, 2, 16])
        sw = sb("smallw", [P, 6, S])
        w2k = sb("w2k", [P, 2, P])
        w2v = sb("w2v", [P, 2, HD])
        nmx = sb("nmx2", [P, len(GROUPS2), 4])
        den = sb("den2", [P, len(GROUPS2), 4])
        fac = sb("fac2", [P, len(GROUPS2), 4])
        bn = sb("bn", [P, NT, 2, 6])
        mv = sb("mv", [P, NT, 2])
        arena = sb("arena", [P, 10240])
        top_of = {}

        def carve(part, shape):
            n = int(np.prod(shape))
            o = top_of.get(part, 0)
            top_of[part] = o + n
            assert o + n <= 10240, part
            names = "abcd"[:len(shape)]
            return arena[:, o:o + n].rearrange(f"p ({' '.join(names)}) -> p {' '.join(names)}", **dict(zip(names, shape)))

        qT = carve("nsa", [4, S])
        DD = carve("nsa", [NT, 8, 2, HD])
        KT = carve("nsa", [8, S])
        sm = carve("nsa", [2, 4, S])
        PT = carve("nsa", [2, NT, 4 * P])
        BLK = carve("nsa", [2, 16, 2 * NC])
        AB, AK, RB, RK, SC = (carve("rec", [8, P]) for _ in range(5))
        T_, TT, BT, UU = (carve("rec", [8, P]) for _ in range(4))
        PN = carve("rec", [2, 2, S])
        x_lo = sb.over("x_low", "arena", [P, KC, S])
        x1_lo = sb.over("x1_low", "FT", [P, KC, S])
        carve("ffn", [FC, S])
        aT = sb.over("aT", "arena", [P, FC, S])
        ln = carve("ffn", [4, D])
        sg = EE.rearrange("p (t c) s -> p t (c s)", t=2)

        cols = [(j * HALF, min(HALF, IN2 - j * HALF)) for j in range(7)]
        fcols = [(j * HALF, min(HALF, FFN - j * HALF)) for j in range(6)]
        steps = ([("in", j) for j in range(7)] + [("cmp", kv) for kv in range(2)] + [("out", 0), ("out", 1)]
                 + [(k, j) for j in range(6) for k in ("gt", "up")] + [("dn", 0), ("dn", 1)])
        uses = []
        for s in steps:
            uses += [(s, t) for t in range(2)]
        PJ = Banks(ctx, nc, "pj2", [chip.bank(0), chip.bank(1)], uses)

        def chunks(ap, k0, nk, c0, w):
            return ap[k0 * P:(k0 + nk) * P, c0:c0 + w].rearrange("(c p) n -> p c n", p=P)

        parts = []
        for s in steps:
            if s[0] == "cmp":
                src = [(lambda l, n=("nsa_wk1_2", "nsa_wv1_2")[s[1]], i=i:
                        A[n][l, :, 4 * i:4 * i + 4, :].rearrange("p (c i) f -> p c (i f)", c=2), 2, HALF) for i in range(4)]
                parts.append((s, src, (s, 1)))
            else:
                name = {"in": "w_in_2", "out": "w_out_2", "gt": "ffn_w_gate_2", "up": "ffn_w_up_2", "dn": "ffn_w_down_2"}[s[0]]
                halves = [(0, HALF), (HALF, HALF)]
                c0, w = {"in": cols, "out": halves, "dn": halves, "gt": fcols, "up": fcols}[s[0]][s[1]]
                src = [(lambda l, n=name, q=q, c0=c0, w=w: chunks(A[n][l], 2 * q, 2, c0, w), 2, w)
                       for q in range((FC if s[0] == "dn" else KC) // 2)]
                parts.append((s, src, (s, NT - 1)))
        W = Weights(ctx, nc, chip, PJ, "w2", parts, plain=[("cmp", 0), ("cmp", 1)])

        tp = [("x", i) for i in range(4)] + [("f", i) for i in range(9)] + [("q", i) for i in range(2)] + [("d", i) for i in range(4)]
        tp += [("mv",), ("mw",), ("ma",), ("mg",), ("mz",), ("kn",), ("o", 0), ("o", 1), ("kc",), ("vc",)]
        tp += [("o", a) for a in range(2, len(GROUPS2))]
        tp += [("bn",), ("kp", 0), ("kp", 1), ("ba", 0), ("ba", 1), ("vt",), ("W",), ("Q",)]
        tp += [(k, i) for i in range(4) for k in ("U", "I", "D") if (k, i) != ("D", 3)] + [("Y", 0), ("Y", 1), ("y", 0), ("y", 1), ("n", 0), ("n", 1)]
        tp += [("x1", i) for i in range(4)] + [("a", i) for i in range(FC // 2)]
        TP = Banks(ctx, nc, "tp2", [chip.bank(2), chip.bank(3)], tp)
        pair0 = chip.ps[:, 4:6, :].rearrange("p a (b n) -> p (a b) n", b=4)
        pair1 = chip.ps[:, 6:8, :].rearrange("p a (b n) -> p (a b) n", b=4)
        UB = Banks(ctx, nc, "ub", [pair0, pair1], [("g", n) for n in range(LEVELS + 1)] + ["AB", "AK", "RB", "RK"])
        lb = [("X", 0, 0), ("X", 0, 1)]
        for n in range(1, LEVELS):
            lb += [("U", n, 0), ("U", n, 1)] + [(k, n, par) for par in range(2) for k in ("X", "XT") if (k, n) != ("X", LEVELS - 1)]
        LB = Banks(ctx, nc, "lb", [chip.bank(4 + i).rearrange("p (u n) -> p u n", u=4) for i in range(4)],
                   lb + [("P", par) for par in range(2)])
        scb = chip.ps[:, 4:6, :].rearrange("p a (b n) -> p (a b) n", b=2)
        ptb = chip.ps[:, 6:8, :]

        ev = {}

        def E(name):
            if name not in ev:
                ev[name] = Count(ctx, nc, "e_" + name)
            return ev[name]

        act_lane = Lane(ctx, nc, nc.scalar, "act2")
        dve_lane = Lane(ctx, nc, nc.vector, "dve2")
        HEADS = [(par, c, t) for par in range(2) for c in range(2) for t in range(NT)]

        def turned(b, n=2):
            return b[:, 0:n * S].rearrange("p (c t) -> p c t", c=n)

        def both(b):
            return b[:, :].rearrange("p (c t) -> p c t", c=2)

        def keys(g):
            return P * (GROUPS2[g][1] + 1) if GROUPS2[g][0] != "c" else P

        with nc.Fori(0, layers) as l:
          with nc.Block() as block:

            @block.sync
            def _(sp):
                for dst, src in ((vec[:], A["vec2"][l]), (sw[:], A["smallw"][l]), (posT[:], A["pos"][l]),
                                 (w2k[:, :, 0:HD], A["nsa_wk2_2"][l].rearrange("(c p) d -> p c d", p=P)),
                                 (w2k[:, :, HD:P], A["nsa_wk2_2"][l].rearrange("(c p) d -> p c d", p=P)),
                                 (w2v[:], A["nsa_wv2_2"][l].rearrange("(c p) d -> p c d", p=P))):
                    sp.dma_start(dst, src).then_inc(E("small_in").sem, 16)
                W.load(sp, l)

            @block.gpsimd
            def _(pool):
                W.low(pool)

            @block.tensor
            def _(pe):
                def turn(use, srcs):
                    b = TP.fill(pe, use)
                    for k, src in enumerate(srcs):
                        ins = pe.transpose(b[:, k * P:(k + 1) * P], src, chip.ident[:])
                    TP.full(ins)

                def product(s, hi, lo):
                    for n in range(W.last[s] - W.first[s] + 1):
                        W.multiply(pe, s, n, hi, lo)

                def by_feature(T):
                    return lambda k, t: T[:, k, t * P:(t + 1) * P]

                for i in range(4):
                    turn(("x", i), [x[:, t, (2 * i + c) * P:(2 * i + c + 1) * P] for c in range(2) for t in range(NT)])
                TP.drained(pe, ("x", 3))
                for j in range(7):
                    product(("in", j), by_feature(xT), by_feature(x_lo))
                PJ.drained(pe, (("in", 6), 1))
                for i in range(9):
                    w = WIN[2 * i:2 * i + 2]
                    turn(("f", i), [H[:, t, c0:c0 + P] for c0 in w for t in range(NT)])
                pe.wait_ge(E("roped").sem, 1)
                for i in range(2):
                    turn(("q", i), [H[:, t, NQ + (2 * i + c) * P:NQ + (2 * i + c + 1) * P] for c in range(2) for t in range(NT)])
                pe.wait_ge(E("dup").sem, 1)
                for i in range(4):
                    turn(("d", i), [DD[:, t, 2 * i + c, :, :].rearrange("p a b -> p (a b)") for c in range(2) for t in range(NT)])
                def compress(kv):
                    s = ("cmp", kv)
                    b = [PJ.fill_ahead(pe, (s, f), f) for f in range(2)]
                    pe.wait_ge(E("blk").sem, kv + 1)
                    for i in range(16):
                        item = W.first[s] + i // 4
                        if i % 4 == 0:
                            W.wait_landed(pe, item)
                        slot = W.raw(item).rearrange("p c (i f) -> p (c i) f", i=2)
                        for f in range(2):
                            ins = pe.matmul(b[f][:, 0:2 * NC], slot[:, i % 4, f * P:(f + 1) * P], BLK[:, kv, i, :],
                                            start=(i == 0), stop=(i == 15))
                            if i == 15:
                                PJ.full(ins)
                        if i in (3, 7, 11):
                            ins.then_inc(W.used.sem, 1)

                compress(0)
                def small(use, w, rhs, start=True, stop=True):
                    b = TP.aps[TP.at[use] % 2]
                    for c in range(2):
                        ins = pe.matmul(b[:, c * S:(c + 1) * S], sw[:, w, c * P:(c + 1) * P], rhs, start=start, stop=stop)
                    return ins

                TP.fill(pe, ("mv",))
                pe.wait_ge(E("small_in").sem, 96)
                pe.wait_ge(E("shifted").sem, 1)
                TP.full(small(("mv",), 1, FT[:, F_VR, :]))
                TP.fill(pe, ("mw",))
                pe.wait_ge(E("ranks").sem, 1)
                TP.full(small(("mw",), 2, TM[:, 0, :]))
                TP.fill(pe, ("ma",))
                TP.full(small(("ma",), 3, FT[:, F_WA, :]))
                b = TP.fill(pe, ("mg",))
                pe.wait_ge(E("ranks").sem, 3)
                for c in range(2):
                    for k in range(2):
                        ins = pe.matmul(b[:, c * S:(c + 1) * S], sw[:, 4 + k, c * P:(c + 1) * P], FT[:, F_G0 + k, :],
                                        start=(k == 0), stop=(k == 1))
                TP.full(ins)
                TP.fill(pe, ("mz",))
                TP.full(small(("mz",), 0, FT[:, F_LR, :]))
                compress(1)

                def compressed():
                    b = TP.fill(pe, ("kc",))
                    pe.wait_ge(E("hid").sem, 1)
                    for f in range(2):
                        ins = pe.matmul(b[:, 0:2 * P], w2k[:, f, :], HID[:, 0, f, :], start=(f == 0), stop=(f == 1))
                    TP.full(ins)
                    b = TP.fill(pe, ("vc",))
                    for g in range(2):
                        for f in range(2):
                            ins = pe.matmul(b[:, g * HD:(g + 1) * HD], HID[:, 1, f, g * P:(g + 1) * P], w2v[:, f, :],
                                            start=(f == 0), stop=(f == 1))
                    TP.full(ins)

                def scores(a):
                    kind, t, g = GROUPS2[a]
                    if a >= 1:
                        pe.wait_ge(E("sc_read").sem, a)
                    if kind == "c":
                        TP.drained(pe, ("vc",))
                    for s in (0, 2, 1, 3):
                        h = 4 * g + HEAD[s]
                        r = slice(64 * (h % 2), 64 * (h % 2) + 64)
                        k = {"s": KT[r, g], "w": KT[r, 2 + g], "c": kcT[r, g]}[kind]
                        ins = pe.matmul(scb[:, s, 0:keys(a)], qT[r, h // 2, t * P:(t + 1) * P], k[:, 0:keys(a)],
                                        start=True, stop=True)
                    ins.then_inc(E("sc_full").sem, 1)

                def turn_p(a):
                    pe.wait_ge(E("p").sem, a + 1)
                    if a >= 1:
                        pe.wait_ge(E("pt").sem, a)
                    for kt in range(keys(a) // P):
                        for s in range(4):
                            ins = pe.transpose(ptb[:, kt, s * P:(s + 1) * P], sm[:, a % 2, s, kt * P:(kt + 1) * P], chip.ident[:])
                    ins.then_inc(E("pt_full").sem, 1)

                def values(a):
                    kind, t, g = GROUPS2[a]
                    b = TP.fill(pe, ("o", a))
                    pe.wait_ge(E("pt").sem, a + 1)
                    n = keys(a) // P
                    for s in range(4):
                        for kt in range(n):
                            v = vcp[:, g, :] if kind == "c" else H[:, kt, {"s": NVS, "w": NVW}[kind] + g * HD:][:, 0:HD]
                            ins = pe.matmul(b[:, s * HD:(s + 1) * HD], PT[:, a % 2, kt, s * P:(s + 1) * P], v,
                                            start=(kt == 0), stop=(kt == n - 1))
                    TP.full(ins)

                TP.drained(pe, ("d", 3))
                G = len(GROUPS2)
                for k in range(G + 2):
                    if k == 2:
                        b = TP.fill(pe, ("kn",))
                        pe.wait_ge(E("ksq").sem, 1)
                        TP.full(pe.matmul(b[:, :], chip.ones[:], TM2.rearrange("p c s -> p (c s)"), start=True, stop=True))
                    if k == 4:
                        compressed()
                    if k < G:
                        scores(k)
                    if 0 <= k - 1 < G:
                        turn_p(k - 1)
                    if 0 <= k - 2 < G:
                        values(k - 2)

                b = TP.fill(pe, ("bn",))
                pe.wait_ge(E("rkr").sem, 1)
                TP.full(pe.matmul(b[:, :], chip.ones[:], TM2.rearrange("p c s -> p (c s)"), start=True, stop=True))

                def units(use, L, R):
                    b = UB.fill(pe, use)
                    for n in range(4):
                        for par in range(2):
                            r = slice(64 * par, 64 * par + 64)
                            c, t = n // 2, n % 2
                            ins = pe.matmul(b[:, 4 * par + n, :], L[r, c, t * P:(t + 1) * P], R[r, c, t * P:(t + 1) * P],
                                            start=True, stop=True)
                    UB.full(ins)

                units(("g", 0), FT[:, F_GK:F_GK + 2, :], FT[:, F_GQ:F_GQ + 2, :])
                for n in range(LEVELS):
                    pe.wait_ge(E("pn").sem, n + 1)
                    units(("g", n + 1), PN[:, n % 2], PN[:, n % 2])
                pe.wait_ge(E("tilde").sem, 1)
                units("AB", BB, KK)
                units("AK", FT[:, F_K:F_K + 2, :], KK)
                units("RB", BB, FT[:, F_R:F_R + 2, :])
                units("RK", FT[:, F_K:F_K + 2, :], FT[:, F_R:F_R + 2, :])
                for t in range(NT):
                    turn(("kp", t), [KP[:, c, t * P:(t + 1) * P] for c in range(4)])
                for t in range(NT):
                    turn(("ba", t), [BP[:, 0, t * P:(t + 1) * P], BP[:, 1, t * P:(t + 1) * P],
                                     KK[:, 0, t * P:(t + 1) * P], KK[:, 1, t * P:(t + 1) * P]])
                turn(("vt",), [FT[:, F_V + c, t * P:(t + 1) * P] for t in range(NT) for c in range(2)])
                b = TP.fill(pe, ("W",))
                TP.drained(pe, ("vt",))
                for u, (par, c, t) in enumerate(HEADS):
                    ins = pe.matmul(b[:, u * CH:(u + 1) * CH], AK[:, u, :], VT[:, t, (2 * c + par) * HD:(2 * c + par + 1) * HD],
                                    start=True, stop=True)
                TP.full(ins)

                def four(use, par, L, R):
                    b = LB.fill(pe, use)
                    for u in range(4):
                        ins = pe.matmul(b[:, u, :], L[:, 4 * par + u, :], R[:, 4 * par + u, :], start=True, stop=True)
                    LB.full(ins)

                UB.drained(pe, "RK")
                pe.wait_ge(E("bt").sem, 1)
                for par in range(2):
                    b = LB.fill(pe, ("X", 0, par))
                    for u in range(4):
                        ins = pe.transpose(b[:, u, :], BT[:, 4 * par + u, :], chip.ident[:])
                    LB.full(ins)
                for n in range(1, LEVELS):
                    pe.wait_ge(E("bt").sem, n + 1)
                    for par in range(2):
                        LB.taken(pe, ("X", n - 1, par))
                        four(("U", n, par), par, BT, T_)
                    for par in range(2):
                        LB.taken(pe, ("U", n, par))
                        if n == 1:
                            pe.wait_ge(E("tt1").sem, 1)
                        else:
                            LB.taken(pe, ("XT", n - 1, par))
                        if n < LEVELS - 1:
                            four(("X", n, par), par, TT, UU)
                        four(("XT", n, par), par, UU, TT)
                for par in range(2):
                    LB.taken(pe, ("XT", LEVELS - 1, par))
                b = TP.fill(pe, ("Q",))
                TP.drained(pe, ("W",))
                for u in range(8):
                    ins = pe.matmul(b[:, u * CH:(u + 1) * CH], TT[:, u, :], Wb[:, u, :], start=True, stop=True)
                TP.full(ins)
                for par in range(2):
                    b = LB.fill(pe, ("P", par))
                    for n in range(4):
                        c, t = n // 2, n % 2
                        ins = pe.matmul(b[:, n, :], BAt[:, t, 256 + c * P:256 + (c + 1) * P], TT[:, 4 * par + n, :],
                                        start=True, stop=True)
                    LB.full(ins)
                LB.drained(pe, ("P", 1))
                for i in range(4):
                    t, r = i // 2, slice(64 * (i % 2), 64 * (i % 2) + 64)
                    pe.wait_ge(E("state").sem, 1)
                    if i:
                        TP.drained(pe, ("D", i - 1))
                    b = TP.fill(pe, ("U", i))
                    for c in range(2):
                        ins = pe.matmul(b[:, c * P:(c + 1) * P], PTf[:, c, t * P:(t + 1) * P], SP[:, 2 + c, :], start=True, stop=True)
                    TP.full(ins)
                    b = TP.fill(pe, ("I", i))
                    for c in range(4):
                        q = GQt[:, c] if c < 2 else FT[:, F_R + c - 2]
                        ins = pe.matmul(b[:, c * P:(c + 1) * P], q[:, t * P:(t + 1) * P], SP[:, c, :], start=True, stop=True)
                    TP.full(ins)
                    if i == 3:
                        continue
                    b = TP.fill(pe, ("D", i))
                    TP.drained(pe, ("U", i))
                    for c in range(4):
                        v = H[r, t, GV + c * P:GV + (c + 1) * P] if c < 2 else VT[r, t, (c - 2) * P:(c - 1) * P]
                        ins = pe.matmul(b[:, c * P:(c + 1) * P], KPt[r, t, c * P:(c + 1) * P], v, start=True, stop=(c < 2))
                        if c >= 2:
                            ins = pe.matmul(b[:, c * P:(c + 1) * P], BAt[r, t, (c - 2) * P:(c - 1) * P],
                                            Us[r, t, (c - 2) * P:(c - 1) * P], start=False, stop=True)
                    TP.full(ins)
                for t in range(NT):
                    b = TP.fill(pe, ("Y", t))
                    for c in range(2):
                        for par in range(2):
                            u, h = 4 * par + 2 * c + t, 2 * c + par
                            pe.matmul(b[:, h * HD:(h + 1) * HD], SC[:, u, :], H[:, t, GV + h * HD:GV + (h + 1) * HD],
                                      start=True, stop=True)
                            o = b[:, 256 + h * HD:256 + (h + 1) * HD]
                            pe.matmul(o, RK[:, u, :], VT[:, t, h * HD:(h + 1) * HD], start=True, stop=False)
                            ins = pe.matmul(o, RB[:, u, :], Us[:, t, h * HD:(h + 1) * HD], start=False, stop=True)
                    TP.full(ins)
                pe.wait_ge(E("normed").sem, 1)
                for i in range(2):
                    turn(("y", i), [Y[:, t, (2 * i + c) * P:(2 * i + c + 1) * P] for c in range(2) for t in range(NT)])
                for i in range(2):
                    turn(("n", i), [NS[:, t, (2 * i + c) * P:(2 * i + c + 1) * P] for c in range(2) for t in range(NT)])
                pe.wait_ge(E("mixed").sem, 2)
                TP.drained(pe, ("n", 1))
                for j in range(2):
                    product(("out", j), by_feature(OT), by_feature(x_lo))
                pe.wait_ge(E("x1").sem, NT)
                for i in range(4):
                    turn(("x1", i), [x[:, t, (2 * i + c) * P:(2 * i + c + 1) * P] for c in range(2) for t in range(NT)])
                TP.drained(pe, ("x1", 3))

                def turn_acts(j):
                    c0, w = fcols[j]
                    PJ.drained(pe, (("up", j), 1))
                    for i in range(c0 // 256, (c0 + w) // 256):
                        turn(("a", i), [H[:, t, (2 * i + c) * P:(2 * i + c + 1) * P] for c in range(2) for t in range(NT)])

                for j in range(6):
                    product(("gt", j), by_feature(xT), by_feature(x1_lo))
                    if j >= 1:
                        turn_acts(j - 1)
                    product(("up", j), by_feature(xT), by_feature(x1_lo))
                turn_acts(5)
                TP.drained(pe, ("a", FC // 2 - 1))
                for j in range(2):
                    product(("dn", j), by_feature(aT), lambda k, t: H_lo[:, t, k * P:(k + 1) * P])

            @block.scalar
            def _(act):
                lane = act_lane
                sc = nc.scalar
                for i in range(4):
                    b = TP.read(act, ("x", i))
                    lane.done(sc.copy(xT[:, 2 * i:2 * i + 2, :], turned(b)), E("x_high"))

                def pace(s, read=lambda: None):
                    for i in range(W.first[s], W.last[s] + 1):
                        W.high(act, i + SPLIT - 1)
                    read()

                def take_in(j):
                    for t in range(NT):
                        b = PJ.read(act, (("in", j), t))
                        c0, w = cols[j]
                        PJ.empty(lane, sc.copy(H[:, t, c0:c0 + w], b[:, 0:w]), (("in", j), t))

                W.high(act, SPLIT - 2)
                for j in range(7):
                    pace(("in", j), lambda: take_in(j))
                for i in range(9):
                    b = TP.read(act, ("f", i))
                    n = len(WIN[2 * i:2 * i + 2])
                    TP.empty(lane, sc.activation(FT[:, 2 * i:2 * i + n, :], turned(b, n), ACT.Copy,
                                                 scale=0.125 if i == 0 else 1.0), ("f", i))
                for i in range(2):
                    b = TP.read(act, ("q", i))
                    TP.empty(lane, sc.copy(qT[:, 2 * i:2 * i + 2, :], turned(b)), ("q", i))
                for i in range(4):
                    b = TP.read(act, ("d", i))
                    TP.empty(lane, sc.copy(KT[:, 2 * i:2 * i + 2, :], turned(b)), ("d", i))
                lane.settle()
                lane.done(sc.activation(gate[:, :, :], H[:, :, NGT:NGT + 24], ACT.Sigmoid), E("gate"))
                act.wait_ge(E("shifted").sem, 1)
                lane.done(sc.activation(TM[:, 0, :], FT[:, F_WA, :], ACT.Tanh), E("ranks"))
                for k in range(2):
                    lane.done(sc.activation(FT[:, F_G0 + k, :], FT[:, F_G0 + k, :], ACT.Sigmoid), E("ranks"))
                b = TP.read(act, ("mv",))
                for c in range(2):
                    ins = sc.activation(BON[:, c, :], b[:, c * S:(c + 1) * S], ACT.Sigmoid, bias=vec[:, V_V0 + c:V_V0 + c + 1])
                    lane.done(ins) if c == 0 else TP.empty(lane, ins, ("mv",))
                b = TP.read(act, ("mw",))
                for c in range(2):
                    ins = sc.activation(LD[:, 2 + c, :], b[:, c * S:(c + 1) * S], ACT.Sigmoid, bias=vec[:, V_W0 + c:V_W0 + c + 1])
                    lane.done(ins) if c == 0 else TP.empty(lane, ins, ("mw",))
                b = TP.read(act, ("ma",))
                for c in range(2):
                    ins = sc.activation(IC[:, c, :], b[:, c * S:(c + 1) * S], ACT.Sigmoid, bias=vec[:, V_A0 + c:V_A0 + c + 1])
                    lane.done(ins) if c == 0 else TP.empty(lane, ins, ("ma",))
                b = TP.read(act, ("mg",))
                TP.empty(lane, sc.copy(GT[:, :, :], both(b)), ("mg",))
                lane.done(sc.activation(EN[:, :, :], FT[:, F_GG:F_GG + 2, :], ACT.Sigmoid), E("gg_sig"))
                act.wait_ge(E("az").sem, 1)
                lane.done(sc.activation(GQt[:, :, :], GQt[:, :, :], ACT.Exp, scale=-1.0))
                lane.settle()
                lane.done(sc.activation(GQt[:, :, :], GQt[:, :, :], ACT.Ln, bias=1.0), E("lnz"))
                act.wait_ge(E("ge_in").sem, 1)
                lane.done(sc.activation(ge[:, 2], ge[:, 1], ACT.Sigmoid, scale=2.0 * 0.7978845608028654), E("ge_sig"))
                G = len(GROUPS2)
                for a in range(G + 1):
                    if a == 0:
                        act.wait_ge(E("cum").sem, 1)
                        lane.done(sc.activation(EP[:, :, :], CUM[:, :, :], ACT.Exp), E("exps"))
                        lane.done(sc.activation(EE[:, :, :], EE[:, :, :], ACT.Exp), E("exps"))
                    if a == 1:
                        lane.done(sc.activation(EN[:, :, :], CUM[:, 2:4, :], ACT.Exp, scale=-1.0), E("exps"))
                        lane.done(sc.activation(EM[:, :, :], EM[:, :, :], ACT.Exp), E("exps"))
                    if a == 2:
                        b = TP.read(act, ("kn",))
                        TP.empty(lane, sc.activation(TM, both(b), ACT.Sqrt), ("kn",))
                    if a >= 1:
                        act.wait_ge(E("pt_full").sem, a)
                        if a - 1 >= 2:
                            act.wait_ge(TP.filled.sem, TP.at[("o", a - 3)] + 1)
                        n = keys(a - 1) // P
                        lane.done(sc.copy(PT[:, (a - 1) % 2, 0:n, :], ptb[:, 0:n, :]), E("pt"))
                    if a < G:
                        act.wait_ge(E("mx").sem, a + 1)
                        for s in range(4):
                            p = sm[:, a % 2, s, 0:keys(a)]
                            lane.done(sc.activation(p, p, ACT.Exp, bias=nmx[:, a, s:s + 1], accum_out=den[:, a, s:s + 1]),
                                      E("p") if s == 3 else None)
                for n in range(LEVELS):
                    act.wait_ge(E("pd").sem, n + 1)
                    lane.done(sc.activation(PN[:, n % 2], PN[:, n % 2], ACT.Exp), E("pe"))
                for use, dst in ((("kp", 0), KPt[:, 0]), (("kp", 1), KPt[:, 1]), (("ba", 0), BAt[:, 0]), (("ba", 1), BAt[:, 1]),
                                 (("vt",), VT)):
                    b = TP.read(act, use)
                    TP.empty(lane, sc.copy(dst, both(b) if use == ("vt",) else b[:, :]), use)
                b = TP.read(act, ("W",))
                TP.empty(lane, sc.copy(Wb[:, :, :].rearrange("p u d -> p (u d)"), b[:, :]), ("W",))
                for n in range(1, LEVELS):
                    for par in range(2):
                        b = LB.read(act, ("U", n, par))
                        if n >= 2:
                            act.wait_ge(LB.filled.sem, LB.at[("XT", n - 1, par)] + 1)
                        LB.empty(lane, sc.copy(UU[:, 4 * par:4 * par + 4, :], b), ("U", n, par))
                b = TP.read(act, ("Q",))
                TP.empty(lane, sc.copy(Qb[:, :, :].rearrange("p u d -> p (u d)"), b[:, :]), ("Q",))
                for par in range(2):
                    r = slice(64 * par, 64 * par + 64)
                    b = LB.read(act, ("P", par))
                    LB.empty(lane, sc.copy(PTf[r, :, :].rearrange("p c s -> p (c s)"), b[r, :, :].rearrange("p u n -> p (u n)")), ("P", par))
                for i in range(4):
                    r = slice(64 * (i % 2), 64 * (i % 2) + 64)
                    b = TP.read(act, ("I", i))
                    TP.empty(lane, sc.copy(Y[r, i // 2, :], b[r, :]), ("I", i))
                W.high(act, W.first[("out", 0)] + SPLIT - 2)
                act.wait_ge(E("var").sem, 1)
                lane.done(sc.activation(st[:, 2, :], st[:, 1, :], ACT.Sqrt), E("sd"))
                TP.drained(act, ("Y", 1))
                for k, n in enumerate(("ln1_w_2", "ln1_b_2", "ln2_w_2", "ln2_b_2")):
                    act.dma_start(ln[:, k, :], A[n][l].partition_broadcast(P)).then_inc(E("ln_in").sem, 16)
                for i in range(2):
                    b = TP.read(act, ("n", i))
                    lane.done(sc.copy(OT[:, 4 + 2 * i:6 + 2 * i, :], turned(b)), E("n_high"))
                for j in range(2):
                    pace(("out", j))
                for k in range(2):
                    act.wait_ge(E("lnv").sem, k + 1)
                    lane.done(sc.activation(mv[:, :, 1], mv[:, :, 1], ACT.Sqrt), E("lns"))
                    if k == 0:
                        for i in range(4):
                            b = TP.read(act, ("x1", i))
                            lane.done(sc.copy(xT[:, 2 * i:2 * i + 2, :], turned(b)), E("x1_high"))

                        def turned_acts(j):
                            c0, w = fcols[j]
                            for i in range(c0 // 256, (c0 + w) // 256):
                                b = TP.read(act, ("a", i))
                                lane.done(sc.copy(aT[:, 2 * i:2 * i + 2, :], turned(b)), E("a_high"))

                        def sigmoids(j):
                            for t in range(NT):
                                b = PJ.read(act, (("gt", j), t))
                                if j >= 1:
                                    PJ.drained(act, (("up", j - 1), t))
                                w = fcols[j][1]
                                lane.done(sc.activation(sg[:, t, 0:w], b[:, 0:w], ACT.Sigmoid), E("sig"))
                            if j >= 1:
                                turned_acts(j - 1)
                        for j in range(6):
                            pace(("gt", j), lambda: sigmoids(j))
                            pace(("up", j))
                        turned_acts(5)
                        for j in range(2):
                            pace(("dn", j))

            @block.vector
            def _(dve):
                lane = dve_lane
                v = nc.vector

                def tt(out, a, b, op, e=None, settle=True):
                    if settle:
                        lane.settle()
                    lane.done(v.tensor_tensor(out, a, b, op), e)

                def ts(out, a, s1, s2, o1, o2=None, e=None, settle=True):
                    if settle:
                        lane.settle()
                    ins = v.tensor_scalar(out, a, s1, s2, o1, o2) if o2 is not None else v.tensor_scalar(out, a, s1, None, o1)
                    lane.done(ins, e)

                def stt(out, a, s, b, o0, o1, e=None, settle=True):
                    if settle:
                        lane.settle()
                    lane.done(v.scalar_tensor_tensor(out=out, in0=a, scalar=s, in1=b, op0=o0, op1=o1), e)

                def low(dst, use, hi, i, e):
                    b = TP.read(dve, use)
                    dve.wait_ge(E(e).sem, i + 1)
                    TP.empty(lane, v.tensor_tensor(dst, turned(b), hi, ALU.subtract), use)

                for i in range(4):
                    low(x_lo[:, 2 * i:2 * i + 2, :], ("x", i), xT[:, 2 * i:2 * i + 2, :], i, "x_high")
                PJ.drained(dve, (("in", 6), 1))
                ra = sm.rearrange("p a b s -> p (a b s)")[:, 0:NT * 512].rearrange("p (t h d) -> p t h d", t=NT, d=HD)
                rb = PT.rearrange("p a b s -> p (a b s)")[:, 0:NT * 512].rearrange("p (t h d) -> p t h d", t=NT, d=HD)

                def rope(X, a_, b_, C, Sn, shape, e=None):
                    def bc(w):
                        for _ in shape[1:-1] if len(shape) == 4 else shape[1:-1]:
                            w = w.unsqueeze(len(w.shape) - 1)
                        return w
                    n = len(shape)
                    lo, hi = (slice(None),) * (n - 1) + (slice(0, 32),), (slice(None),) * (n - 1) + (slice(32, 64),)
                    c_, s_ = C, Sn
                    while len(c_.shape) < n:
                        c_, s_ = c_.unsqueeze(len(c_.shape) - 1), s_.unsqueeze(len(s_.shape) - 1)
                    half = shape[:-1] + [32]
                    tt(a_, X, c_.to_broadcast(shape), ALU.mult)
                    tt(b_[lo], X[hi], s_[(slice(None),) * (n - 1) + (slice(0, 32),)].to_broadcast(half), ALU.mult, settle=False)
                    tt(b_[hi], X[lo], s_[(slice(None),) * (n - 1) + (slice(32, 64),)].to_broadcast(half), ALU.mult, settle=False)
                    tt(X, a_, b_, ALU.add, e)

                rope(H[:, :, NQ:NQ + 512].rearrange("p t (h d) -> p t h d", d=HD), ra, rb,
                     chip.rope2[:, :, 0, :], chip.rope2[:, :, 1, :], [P, NT, 8, HD], E("roped"))
                for t in range(NT):
                    rope(H[:, t, NKC:NKC + 768].rearrange("p (k o d) -> p k o d", k=3, o=4)[:, :, 0:2, :],
                         ra[:, t, 0:6, :].rearrange("p (k g) d -> p k g d", k=3), rb[:, t, 0:6, :].rearrange("p (k g) d -> p k g d", k=3),
                         chip.rope2[:, t, 0, :], chip.rope2[:, t, 1, :], [P, 3, 2, HD])
                lane.settle()
                for n, c0 in enumerate((NKS, NKW, NKC, NVC)):
                    for t in range(NT):
                        src = H[:, t, c0:c0 + P].rearrange("p (g d) -> p g d", g=2).unsqueeze(2).to_broadcast([P, 2, 2, HD])
                        last = (n, t) == (3, 1)
                        if last:
                            lane.settle()
                        lane.done(v.tensor_copy(DD[:, t, 2 * n:2 * n + 2, :, :], src), E("dup") if last else None)
                TP.drained(dve, ("d", 3))
                dve.wait_ge(E("small_in").sem, 96)
                for kv in range(2):
                    for g in range(2):
                        for hf in range(2):
                            r = slice(64 * hf, 64 * hf + 64)
                            src = KT[r, 4 + 2 * kv + g, :]
                            src = src[:, 16 * hf:16 * hf + 16 * NC].rearrange("p (c i) -> p i c", i=16)
                            last = (g, hf) == (1, 1)
                            tt(BLK[r, kv, :, g * NC:(g + 1) * NC], src, posT[r, kv, :].unsqueeze(2).to_broadcast([64, 16, NC]),
                               ALU.add, E("blk") if last else None, settle=last)
                def output(a):
                    kind, t, g = GROUPS2[a]
                    b = TP.read(dve, ("o", a))
                    dve.wait_ge(E("p").sem, a + 1)
                    f = fac[:, a, :].rearrange("p (b a) -> p b a", a=2)
                    gt = gate[:, t, :].rearrange("p (g a b k) -> p g b a k", g=2, a=2, b=2)[:, g, :, :, "csw".index(kind)]
                    lane.settle()
                    lane.done(v.reciprocal(fac[:, a, :], den[:, a, :]))
                    tt(f, f, gt, ALU.mult)
                    if kind == "c":
                        ts(fac[:, a, :], fac[:, a, :], chip.rowv[:, t:t + 1], None, ALU.mult)
                    lane.settle()
                    dst = NS[:, t, g * 256:(g + 1) * 256]
                    out = dst if kind == "s" else part_out
                    TP.empty(lane, v.tensor_tensor(out.rearrange("p (a b d) -> p b a d", a=2, b=2),
                                                   b[:, 0:256].rearrange("p (b a d) -> p b a d", a=2, b=2),
                                                   f.unsqueeze(3).to_broadcast([P, 2, 2, HD]), ALU.mult), ("o", a))
                    if kind != "s":
                        tt(dst, dst, part_out, ALU.add)

                R10 = FT[:, F_R:F_R + 10, :]
                TP.drained(dve, ("f", 8))
                tt(DL[:, :, 1:S], R10[:, :, 0:S - 1], R10[:, :, 1:S], ALU.subtract)
                ts(DL[:, :, 0:1], R10[:, :, 0:1], -1.0, None, ALU.mult, settle=False)
                lane.settle()
                for c in range(10):
                    last = c == 9
                    stt(R10[:, c, :], DL[:, c, :], vec[:, V_MU + c:V_MU + c + 1], R10[:, c, :], ALU.mult, ALU.add,
                        E("shifted") if last else None, settle=last)
                lane.done(v.memset(HID[:, :, :, :], 0.0))

                def take_hidden(kv):
                    for f in range(2):
                        b = PJ.read(dve, (("cmp", kv), f))
                        PJ.empty(lane, v.tensor_copy(ge[:, 0, kv, f * 2 * NC:(f + 1) * 2 * NC], b[:, 0:2 * NC]), (("cmp", kv), f))

                take_hidden(0)
                Vf, Vn = chip.vfirst[:, :, :], FT[:, F_V:F_V + 2, :]
                tt(TM2[:, :, :], Vn, Vf, ALU.subtract)
                stt(Vf, TM2[:, :, :], vec[:, V_FLAG:V_FLAG + 1], Vf, ALU.mult, ALU.add)
                tt(TM2[:, :, :], Vf, Vn, ALU.subtract)
                TP.drained(dve, ("mv",))
                tt(TM2[:, :, :], TM2[:, :, :], BON[:, :, :], ALU.mult)
                tt(Vn, Vn, TM2[:, :, :], ALU.add)
                b = TP.read(dve, ("mz",))
                for c in range(2):
                    ins = v.tensor_scalar(LD[:, c, :], b[:, c * S:(c + 1) * S], vec[:, V_BA + c:V_BA + c + 1], None, ALU.add)
                    lane.done(ins) if c == 0 else TP.empty(lane, ins, ("mz",))
                stt(GQt[:, :, :], LD[:, 0:2, :], -1.0, LD[:, 0:2, :], ALU.mult, ALU.max, E("az"))
                for c in range(2):
                    ts(KK[:, c, :], FT[:, F_K + c, :], vec[:, V_KK + c:V_KK + c + 1], None, ALU.mult, settle=False)
                tt(TM2[:, :, :], KK[:, :, :], KK[:, :, :], ALU.mult, E("ksq"))
                dve.wait_ge(E("lnz").sem, 1)
                stt(LD[:, 0:2, :], LD[:, 0:2, :], 0.0, GQt[:, :, :], ALU.min, ALU.subtract)
                ts(LD[:, 0:2, :], LD[:, 0:2, :], 1.0 / 16, None, ALU.mult)
                TP.drained(dve, ("ma",))
                ts(LD[:, 2:4, :], LD[:, 2:4, :], -E_HALF, None, ALU.mult)
                lane.settle()
                for c in range(4):
                    lane.done(v.tensor_tensor_scan(CUM[:, c, :], chip.reset[:, :], LD[:, c, :], 0.0, ALU.mult, ALU.add))
                dve.wait_ge(E("gg_sig").sem, 1)
                tt(FT[:, F_GG:F_GG + 2, :], FT[:, F_GG:F_GG + 2, :], EN[:, :, :], ALU.mult)
                cv = CUM.rearrange("p c (k t) -> p c k t", t=CH)
                tt(EE.rearrange("p c (k t) -> p c k t", t=CH), cv[:, :, :, CH - 1:CH].to_broadcast([P, 4, 4, CH]), cv, ALU.subtract)
                tt(EM[:, :, :], CUM[:, 2:4, :], LD[:, 2:4, :], ALU.subtract, E("cum"))
                Kn, Rn = FT[:, F_K:F_K + 2, :], FT[:, F_R:F_R + 2, :]
                for c in range(2):
                    ts(BB[:, c, :], IC[:, c, :], 1.0, vec[:, V_KA + c:V_KA + c + 1], ALU.subtract, ALU.mult, settle=False)
                stt(Kn, BB[:, :, :], 1.0, Kn, ALU.add, ALU.mult)
                take_hidden(1)
                tt(ge[:, 1], ge[:, 0], ge[:, 0], ALU.mult)
                ts(ge[:, 1], ge[:, 1], 0.044715, 1.0, ALU.mult, ALU.add)
                tt(ge[:, 1], ge[:, 1], ge[:, 0], ALU.mult, E("ge_in"))
                dve.wait_ge(E("ge_sig").sem, 1)
                for kv in range(2):
                    h_, s_ = (ge[:, i, kv, :].rearrange("p (f g n) -> p f g n", f=2, g=2) for i in (0, 2))
                    tt(HID[:, kv, :, :].rearrange("p f (g n) -> p f g n", g=2)[:, :, :, 0:NC], h_, s_, ALU.mult,
                       E("hid") if kv else None, settle=kv == 0)

                def compressed():
                    b = TP.read(dve, ("kc",))
                    TP.empty(lane, v.tensor_copy(H[:, 0, 0:S], b[:, 0:2 * P]), ("kc",))
                    b = TP.read(dve, ("vc",))
                    TP.empty(lane, v.tensor_copy(H[:, 1, 0:P], b[:, 0:2 * HD]), ("vc",))

                def keys_normalised():
                    TP.drained(dve, ("kn",))
                    ts(TM, TM, 1e-12, None, ALU.max)
                    lane.settle()
                    lane.done(v.reciprocal(TM, TM))
                    tt(KK[:, :, :], KK[:, :, :], TM, ALU.mult)

                def bonus():
                    for c in range(2):
                        stt(TM2[:, c, :], FT[:, F_R + c, :], vec[:, V_RK + c:V_RK + c + 1], FT[:, F_K + c, :], ALU.mult, ALU.mult,
                            E("rkr") if c else None)
                    tt(BB[:, :, :], KK[:, :, :], IC[:, :, :], ALU.mult)

                def to_the_end():
                    dve.wait_ge(E("exps").sem, 4)
                    tt(BP[:, :, :], BB[:, :, :], EE[:, 2:4, :], ALU.mult)
                    tt(KP[:, 0:2, :], FT[:, F_GK:F_GK + 2, :], EE[:, 0:2, :], ALU.mult, settle=False)
                    tt(KP[:, 2:4, :], Kn, EE[:, 2:4, :], ALU.mult, settle=False)

                def from_the_start_1():
                    tt(GQt[:, :, :], FT[:, F_GQ:F_GQ + 2, :], EP[:, 0:2, :], ALU.mult)
                    stt(KK[:, :, :], KK[:, :, :], -1.0, EM[:, :, :], ALU.mult, ALU.mult)

                def from_the_start_2():
                    tt(BB[:, :, :], BB[:, :, :], EN[:, :, :], ALU.mult)
                    tt(Kn, Kn, EN[:, :, :], ALU.mult)
                    tt(Rn, Rn, EP[:, 2:4, :], ALU.mult, E("tilde"))

                with_group = {3: keys_normalised, 5: bonus, 6: to_the_end, 7: from_the_start_1, 8: from_the_start_2}
                G = len(GROUPS2)
                dve.wait_ge(E("gate").sem, 1)
                for k in range(G + 2):
                    if k == 4:
                        compressed()
                    if k < G:
                        kind, t, g = GROUPS2[k]
                        nk = keys(k)
                        dve.wait_ge(E("sc_full").sem, k + 1)
                        if k >= 2:
                            dve.wait_ge(E("pt_full").sem, k - 1)
                        p = sm[:, k % 2, :, 0:nk]
                        bias = (chip.cmpb if kind == "c" else chip.cbias)[:, t, 0:nk].unsqueeze(1).to_broadcast([P, 4, nk])
                        stt(p, scb[:, :, 0:nk], 0.125, bias, ALU.mult, ALU.add, E("sc_read"))
                        lane.settle()
                        lane.done(v.tensor_reduce(nmx[:, k, :], p, AX_X, ALU.max, negate=True), E("mx"))
                    if k - 2 >= 0:
                        output(k - 2)
                    if k in with_group:
                        with_group[k]()

                def mask(m):
                    return masks[:, m, :].unsqueeze(1).to_broadcast([P, 8, P])

                b = TP.read(dve, ("bn",))
                TP.empty(lane, v.tensor_tensor(BON[:, :, :], both(b), Vn, ALU.mult), ("bn",))

                def level(n, u):
                    w = 1 << n
                    return u.rearrange("p c (k h t) -> p (c k) h t", h=2, t=w)

                def parts(n):
                    w = 1 << n
                    return [level(n, u) for u in (PN[:, n % 2], CUM[:, 0:2, :], FT[:, F_GQ:F_GQ + 2, :], FT[:, F_GK:F_GK + 2, :])]

                def decays(n):
                    w = 1 << n
                    pn, cu, _, _ = parts(n)
                    mid = cu[:, :, 0, w - 1:w].to_broadcast([P, S // w, w])
                    if n >= 2:
                        dve.wait_ge(UB.filled.sem, UB.at[("g", n - 1)] + 1)
                    tt(pn[:, :, 0, :], mid, cu[:, :, 0, :], ALU.subtract)
                    tt(pn[:, :, 1, :], cu[:, :, 1, :], mid, ALU.subtract, E("pd"), settle=False)

                decays(0)
                for n in range(LEVELS + 1):
                    if n < LEVELS:
                        pn, _, q_, k_ = parts(n)
                        dve.wait_ge(E("pe").sem, n + 1)
                        tt(pn[:, :, 0, :], pn[:, :, 0, :], k_[:, :, 0, :], ALU.mult)
                        tt(pn[:, :, 1, :], pn[:, :, 1, :], q_[:, :, 1, :], ALU.mult, E("pn"), settle=False)
                    if n + 1 < LEVELS:
                        decays(n + 1)
                    b = UB.read(dve, ("g", n))
                    lane.settle()
                    if n == 0:
                        UB.empty(lane, v.tensor_tensor(SC[:, :, :], b, mask(M_EYE), ALU.mult), ("g", n))
                    else:
                        UB.empty(lane, v.copy_predicated(SC[:, :, :], mask(n - 1).bitcast(mybir.dt.int32), b), ("g", n))
                for use, dst, m in (("AB", AB, M_STRICT), ("AK", AK, M_STRICT), ("RB", RB, M_INCL), ("RK", RK, M_INCL)):
                    b = UB.read(dve, use)
                    UB.empty(lane, v.tensor_tensor(dst[:, :, :], b, mask(m), ALU.mult), use)
                    if use == "AB":
                        tt(BT[:, :, :], AB[:, :, :], mask(0), ALU.mult, E("bt"))
                tt(TT[:, :, :], BT[:, :, :], chip.ident[:].unsqueeze(1).to_broadcast([P, 8, P]), ALU.add, E("tt1"))
                for n in range(LEVELS):
                    if n + 1 < LEVELS:
                        dve.wait_ge(LB.filled.sem, LB.at[("U", n, 1) if n else ("X", 0, 1)] + 1)
                        tt(BT[:, :, :], AB[:, :, :], mask(n + 1), ALU.mult, E("bt"))
                    for par in range(2):
                        four = slice(4 * par, 4 * par + 4)
                        if n < LEVELS - 1:
                            b = LB.read(dve, ("X", n, par))
                            lane.settle()
                            LB.empty(lane, v.tensor_tensor(T_[:, four, :], b, T_[:, four, :] if n else
                                                           chip.ident[:].unsqueeze(1).to_broadcast([P, 4, P]), ALU.add), ("X", n, par))
                        if n:
                            b = LB.read(dve, ("XT", n, par))
                            lane.settle()
                            LB.empty(lane, v.tensor_tensor(TT[:, four, :], b, TT[:, four, :], ALU.add), ("XT", n, par))
                lane.settle()
                lane.done(v.memset(SP[:, :, :], 0.0), E("state"))
                for i in range(4):
                    t, r = i // 2, slice(64 * (i % 2), 64 * (i % 2) + 64)
                    b = TP.read(dve, ("U", i))
                    TP.drained(dve, ("Q",)) if i == 0 else None
                    q_ = Qb.rearrange("p (a c t) d -> p c a t d", a=2, c=2)[r, :, :, t, :]
                    lane.settle()
                    TP.empty(lane, v.tensor_tensor(Us[r, t, :].rearrange("p (c a d) -> p c a d", c=2, a=2),
                                                   b[r, 0:256].rearrange("p (c a d) -> p c a d", c=2, a=2), q_, ALU.add), ("U", i))
                    if i < 3:
                        b = TP.read(dve, ("D", i))
                        for hf in range(2):
                            h = slice(64 * hf, 64 * hf + 64)
                            tt(SP[h, :, h], SP[h, :, h], EP[h, :, i * CH + CH - 1:i * CH + CH].to_broadcast([64, 4, 64]), ALU.mult,
                               settle=False)
                        lane.settle()
                        for hf in range(2):
                            h = slice(64 * hf, 64 * hf + 64)
                            ins = v.tensor_tensor(SP[h, :, h], b.rearrange("p (c n) -> p c n", c=4)[h, :, h], SP[h, :, h], ALU.add)
                            lane.done(ins) if hf == 0 else TP.empty(lane, ins, ("D", i))
                TP.drained(dve, ("I", 3))
                for t in range(NT):
                    b = TP.read(dve, ("Y", t))
                    TP.empty(lane, v.tensor_tensor(Y[:, t, :], b[:, :], Y[:, t, :], ALU.add), ("Y", t))
                yv = Y.rearrange("p t (h d) -> p t h d", d=HD)
                sv = CUM.rearrange("p (t m) (h d) -> p t (m h) d", t=NT, d=HD)
                lane.settle()
                lane.done(v.tensor_reduce(st[:, 0, :].rearrange("p (t h) -> p t h", t=NT), yv, AX_X, ALU.add))
                ts(st[:, 0, :], st[:, 0, :], 1.0 / HD, None, ALU.mult)
                tt(yv, yv, st[:, 0, :].rearrange("p (t h) -> p t h", t=NT).unsqueeze(3).to_broadcast([P, NT, 8, HD]), ALU.subtract)
                tt(sv, yv, yv, ALU.mult)
                lane.settle()
                lane.done(v.tensor_reduce(st[:, 1, :].rearrange("p (t h) -> p t h", t=NT), sv, AX_X, ALU.add))
                s1 = st[:, 1, :].rearrange("p (t m h) -> p t m h", t=NT, m=2)
                for m, eps in ((0, LN_EPS), (1, RWKV_GN_EPS)):
                    ts(s1[:, :, m, :], s1[:, :, m, :], 1.0 / HD, eps, ALU.mult, ALU.add, E("var") if m else None)
                dve.wait_ge(E("sd").sem, 1)
                lane.settle()
                lane.done(v.reciprocal(st[:, 0, :], st[:, 2, :]))
                tt(yv, yv, st[:, 0, :].rearrange("p (t h) -> p t h", t=NT).unsqueeze(3).to_broadcast([P, NT, 8, HD]), ALU.mult, E("normed"))
                for i in range(2):
                    b = TP.read(dve, ("y", i))
                    for c in range(2):
                        ch = 2 * i + c
                        dst = (TM, TM2)[i][:, c, :]
                        ins = v.tensor_scalar(dst, b[:, c * S:(c + 1) * S], vec[:, V_LNW + ch:V_LNW + ch + 1],
                                              vec[:, V_LNB + ch:V_LNB + ch + 1], ALU.mult, ALU.add)
                        lane.done(ins) if c == 0 else TP.empty(lane, ins, ("y", i))
                for hi, lo, val, g in ((OT[:, 0:2, :], x_lo[:, 0:2, :], TM, FT[:, F_GG:F_GG + 2, :]),
                                       (OT[:, 2:4, :], x_lo[:, 2:4, :], TM2, GT)):
                    if val is TM2:
                        tt(val[:, :, :], val[:, :, :], BON[:, :, :], ALU.add)
                    tt(val[:, :, :], val[:, :, :], g if val is TM else g[:, :, :], ALU.mult)
                    lane.settle()
                    lane.done(v.tensor_copy(hi, val[:, :, :]))
                    tt(lo, val[:, :, :], hi, ALU.subtract, E("mixed"))
                for i in range(2):
                    low(x_lo[:, 4 + 2 * i:6 + 2 * i, :], ("n", i), OT[:, 4 + 2 * i:6 + 2 * i, :], i, "n_high")

                def residual(s):
                    for j in range(2):
                        for t in range(NT):
                            b = PJ.read(dve, ((s, j), t))
                            xs = x[:, t, j * HALF:(j + 1) * HALF]
                            PJ.empty(lane, v.scalar_tensor_tensor(out=xs, in0=xs, scalar=ALPHA, in1=b[:, :],
                                                                  op0=ALU.mult, op1=ALU.add), ((s, j), t))

                def layer_norm(k):
                    lane.settle()
                    for t in range(NT):
                        for j in range(2):
                            lane.done(v.bn_stats(bn[:, t, j, :], x[:, t, j * HALF:(j + 1) * HALF]))
                    lane.settle()
                    for t in range(NT):
                        lane.done(v.bn_aggr(mv[:, t, :], bn[:, t, :, :].rearrange("p a b -> p (a b)")))
                    ts(mv[:, :, 1], mv[:, :, 1], LN_EPS, None, ALU.add, e=E("lnv"))
                    dve.wait_ge(E("lns").sem, k + 1)
                    lane.done(v.reciprocal(mv[:, :, 1], mv[:, :, 1]))
                    lane.settle()
                    for t in range(NT):
                        ts(x[:, t, :], x[:, t, :], mv[:, t, 0:1], mv[:, t, 1:2], ALU.subtract, ALU.mult, settle=False)
                    dve.wait_ge(E("ln_in").sem, 64)
                    for t in range(NT):
                        tt(x[:, t, :], x[:, t, :], ln[:, 2 * k, :], ALU.mult)
                        tt(x[:, t, :], x[:, t, :], ln[:, 2 * k + 1, :], ALU.add, E("x1") if k == 0 else None)

                residual("out")
                layer_norm(0)
                for i in range(4):
                    low(x1_lo[:, 2 * i:2 * i + 2, :], ("x1", i), xT[:, 2 * i:2 * i + 2, :], i, "x1_high")

                def low_acts(j):
                    c0, w = fcols[j]
                    for i in range(c0 // 256, (c0 + w) // 256):
                        b = TP.read(dve, ("a", i))
                        dve.wait_ge(E("a_high").sem, i + 1)
                        TP.empty(lane, v.tensor_tensor(
                            H_lo[:, :, 2 * i * P:(2 * i + 2) * P].rearrange("p t (c n) -> p c t n", c=2),
                            turned(b).rearrange("p c (t n) -> p c t n", t=NT),
                            aT[:, 2 * i:2 * i + 2, :].rearrange("p c (t n) -> p c t n", t=NT), ALU.subtract), ("a", i))

                for j in range(6):
                    c0, w = fcols[j]
                    for t in range(NT):
                        b = PJ.read(dve, (("gt", j), t))
                        dve.wait_ge(E("sig").sem, 2 * j + t + 1)
                        PJ.empty(lane, v.tensor_tensor(sg[:, t, 0:w], b[:, 0:w], sg[:, t, 0:w], ALU.mult), (("gt", j), t))
                    if j >= 1:
                        low_acts(j - 1)
                    lane.settle()
                    for t in range(NT):
                        b = PJ.read(dve, (("up", j), t))
                        lane.settle()
                        ins = v.tensor_tensor(H[:, t, c0:c0 + w], b[:, 0:w], sg[:, t, 0:w], ALU.mult)
                        PJ.empty(lane, ins, (("up", j), t))
                low_acts(5)
                residual("dn")
                layer_norm(1)
                lane.settle()
          close_layer(nc, ctx.sems)


def layout(inputs):
    a = {k: np.ascontiguousarray(v) for k, v in inputs.items()}

    def by_feature(v):
        return np.ascontiguousarray(v.reshape(DEPTH, -1, P).transpose(0, 2, 1))

    a["vec1"] = np.concatenate([by_feature(a["norm_g"]), by_feature(a["mem_norm_g"])], axis=2)
    a["ident"] = np.eye(P, dtype=np.float32)
    tok = np.arange(S).reshape(NT, P).T
    a["cbias"] = np.where(np.arange(S)[None, None, :] <= tok[:, :, None], 0.0, NEG).astype(np.float32)

    def rope(theta, half):
        inv = np.float32(theta) ** (-np.arange(half, dtype=np.float32) / np.float32(half))
        ang = tok[:, :, None].astype(np.float32) * inv[None, None, :]
        c, s = np.cos(ang), np.sin(ang)
        return np.stack([np.concatenate([c, c], -1), np.concatenate([-s, s], -1)], axis=2).astype(np.float32)

    a["rope1"] = rope(500000.0, 8)
    a["rope2"] = rope(10000.0, 32)

    def at(v, size, off):
        out = np.zeros((DEPTH, size), np.float32)
        out[:, off:off + v.shape[1]] = v
        return out

    def late(v):
        return np.concatenate([np.zeros_like(v[:1]), v], axis=0)

    mu = a["rwkv_mu_2"]
    cols = [mu[:, 0:1024], at(mu[:, 1024:], P, P - 32), at(late(a["rwkv_mu_vres_2"]), P, P - 32), a["rwkv_w0_2"], a["rwkv_a0_2"],
            late(a["rwkv_v0_2"]), a["rwkv_k_k_2"], a["rwkv_k_a_2"], a["rwkv_r_k_2"].reshape(DEPTH, -1), a["gla_b_a_2"],
            a["gla_ln_w_2"], a["rwkv_ln_w_2"], a["gla_ln_b_2"], a["rwkv_ln_b_2"],
            np.repeat(np.array([[1.0], [0.0]], np.float32), P, axis=1)]
    a["vec2"] = np.concatenate([by_feature(v) for v in cols], axis=2)

    def rows(v, off):
        out = np.zeros((DEPTH, P, S), np.float32)
        out[:, off:off + v.shape[1]] = v
        return out

    g2 = a["rwkv_g2_2"]
    a["smallw"] = np.ascontiguousarray(np.stack([
        rows(a["gla_w_a2_2"], 0), rows(late(a["rwkv_v2_2"]), P - 32), rows(a["rwkv_w2_2"], 0), rows(a["rwkv_a2_2"], 64),
        g2[:, 0:P], rows(g2[:, P:], P - 32)], axis=2))
    a["pos"] = np.ascontiguousarray(np.stack([a["nsa_pos_k_2"], a["nsa_pos_v_2"]], axis=1)
                                    .reshape(DEPTH, 2, 2, 16, HD).transpose(0, 2, 4, 1, 3).reshape(DEPTH, P, 2, 16))
    for n in ("nsa_wk1_2", "nsa_wv1_2"):
        a[n] = np.ascontiguousarray(a[n].reshape(DEPTH, 2, 16, HD, 256).transpose(0, 1, 3, 2, 4).reshape(DEPTH, P, 16, 256))
    a["w_in_2"] = np.concatenate([a["w_in_2"], late(a["w_in_vres_2"])], axis=2)
    c = np.arange(P)
    ends = 16 * c + 31
    ok = (ends[None, None, :] <= tok[:, :, None]) & (c < 15)
    a["cmpb"] = np.where(ok, 0.0, NEG).astype(np.float32)
    a["rowv"] = (tok >= 31).astype(np.float32)
    a["ones"] = (c[:, None] // 64 == c[None, :] // 64).astype(np.float32)
    s_, t_ = c[:, None], c[None, :]
    same = s_ // 64 == t_ // 64
    m = [(s_ // (2 << n) == t_ // (2 << n)) & (s_ // (1 << n) % 2 == 0) & (t_ // (1 << n) % 2 == 1) for n in range(6)]
    m += [same & (s_ < t_), same & (s_ <= t_), s_ == t_]
    a["masks"] = np.ascontiguousarray(np.stack(m, axis=1).astype(np.float32))
    a["reset"] = np.repeat((np.arange(S)[None] % 64 != 0).astype(np.float32), P, axis=0)
    return {k: a[k] for k in USED}


USED = ["x", "mem", "vec1", "w_in", "w_mem_kv", "w_branch", "w_out", "ident", "cbias", "rope1", "final_g", "rope2", "vec2",
        "smallw", "pos", "nsa_wk1_2", "nsa_wk2_2", "nsa_wv1_2", "nsa_wv2_2", "w_in_2", "w_out_2", "ffn_w_gate_2", "ffn_w_up_2",
        "ffn_w_down_2", "ln1_w_2", "ln1_b_2", "ln2_w_2", "ln2_b_2", "cmpb", "rowv", "ones", "masks", "reset"]


def build(nc, A, out, first=DEPTH, second=DEPTH):
    with ExitStack() as ctx:
        chip = Chip(ctx, nc)
        with ExitStack() as c1:
            chip.memT = c1.enter_context(nc.sbuf_tensor("memT", [P, KC, S], F32))
            chip.rope1 = c1.enter_context(nc.sbuf_tensor("rope1s", [P, NT, 2, 16], F32))
            first_prologue(nc, chip, A)
            first_layers(nc, chip, A, first)

        def sb(name, shape):
            return ctx.enter_context(nc.sbuf_tensor(name, shape, F32))

        chip.vfirst = sb("vfirst", [P, 2, S])
        chip.rope2 = sb("rope2s", [P, NT, 2, HD])
        chip.cmpb = sb("cmpb", [P, NT, P])
        chip.rowv = sb("rowv", [P, NT])
        chip.ones = sb("ones", [P, P])
        chip.masks = sb("masks", [P, 9, P])
        chip.reset = sb("reset", [P, S])
        second_prologue(nc, chip, A)
        second_layers(nc, chip, A, second)
        with Scope() as c3:
            done = Count(c3, nc, "out_written")
            with nc.Block() as block:

                @block.sync
                def _(sp):
                    sp.dma_start(out.rearrange("(t p) d -> p t d", p=P), chip.x[:]).then_inc(done.sem, 16)
                    sp.wait_ge(done.sem, 16)


def kernel(**inputs):
    import concourse.bacc as _bacc
    from concourse.bass_utils import run_bass_kernel_spmd as _run

    nc = _bacc.Bacc("TRN2", target_bir_lowering=False, num_devices=1)
    arrays = layout({n: np.asarray(v) for n, v in inputs.items()})
    A = {n: nc.dram_tensor("in_" + n, a.shape, F32, kind="ExternalInput").ap() for n, a in arrays.items()}
    out = nc.dram_tensor("out", (S, D), F32, kind="ExternalOutput").ap()
    build(nc, A, out)
    r = _run(nc, [{"in_" + n: a for n, a in arrays.items()}], core_ids=[0])
    return r.results[0]["out"].reshape(1, S, D)
```

```python
from contextlib import ExitStack

import numpy as np
import concourse.bass as bass
from concourse import mybir

P = 128
F32 = mybir.dt.float32
F32R = mybir.dt.float32r
ALU = mybir.AluOpType
ACT = mybir.ActivationFunctionType
AX_X = mybir.AxisListType.X

D = 1024
S = 256
NT = S // P
KC = D // P
DEPTH = 2
HALF = 512
BR = 512
HD = 64
NEG = -1.0e30
TAKEN = -3.0e38
RMS_EPS = 1e-6
LN_EPS = 1e-5

AQ, AK, AV, AG, BQ, BK, BV, BG, IQ = [BR * i for i in range(9)]
IK = IQ + 512
IW = IK + 64
MQ = IW + 8
MG = MQ + BR
MIX = MG + BR
IN1 = MIX + 3 * D
TOPK = 64
RAW = 3
SPLIT = 4


class Count:

    def __init__(self, ctx, nc, name):
        self.sem = ctx.enter_context(nc.semaphore(name))
        ctx.sems.append(self.sem)
        self.n = 0


class Scope(ExitStack):

    def __init__(self):
        super().__init__()
        self.sems = []


class Lane:

    def __init__(self, ctx, nc, eng, name):
        self.eng = eng
        self.chain = Count(ctx, nc, name)
        self.open = {}

    def done(self, ins, signal=None):
        c = signal or self.chain
        ins.then_inc(c.sem, 1)
        c.n += 1
        self.open[c] = c.n

    def settle(self):
        for c, n in self.open.items():
            self.eng.wait_ge(c.sem, n)
        self.open = {}




class Weights:

    def __init__(self, ctx, nc, chip, banks, name, steps, plain=(), shared={}):
        self.shared = shared
        self.nc, self.chip, self.banks = nc, chip, banks
        self.items, self.first, self.last = [], {}, {}
        self.kth, self.split_items, used = {}, [], 0
        for s, parts, last_use in steps:
            self.first[s] = len(self.items)
            for n, (src, nk, w) in enumerate(parts):
                i = len(self.items)
                final = n == len(parts) - 1 and last_use is not None
                used += not final
                self.items.append((src, nk, w, (self.sums(s)[0], last_use) if final else used))
                if s not in plain:
                    self.kth[i] = len(self.split_items)
                    self.split_items.append(i)
            self.last[s] = len(self.items) - 1
        self.landed = [Count(ctx, nc, f"{name}_landed{i}") for i in range(RAW)]
        self.hi_ready, self.lo_ready, self.used = (Count(ctx, nc, f"{name}_{n}") for n in ("high_ready", "low_ready", "used"))
        self.to_split = 0

    def sums(self, s):
        return self.shared.get(s, (self.banks, s, 0, True, True))

    def wait_used(self, eng, i):
        last = self.items[i][3]
        if isinstance(last, int):
            eng.wait_ge(self.used.sem, last)
        else:
            banks, use = last
            eng.wait_ge(banks.filled.sem, banks.at[use] + 1)

    def wait_landed(self, eng, i):
        eng.wait_ge(self.landed[i % RAW].sem, 16 * (i // RAW + 1))

    def raw(self, i):
        return self.chip.raw[:, i % RAW]

    def part(self, i, lo):
        return self.chip.parts[:, self.kth[i] % SPLIT, lo]

    def load(self, sp, l, start, stop):
        for i in range(start, stop):
            src, nk, w, _ = self.items[i]
            if i >= RAW:
                j = i - RAW
                if j in self.kth:
                    sp.wait_ge(self.lo_ready.sem, self.kth[j] + 1)
                else:
                    self.wait_used(sp, j)
            sp.dma_start(self.raw(i)[:, 0:nk, 0:w], src(l)).then_inc(self.landed[i % RAW].sem, 16)

    def high(self, act, upto):
        while self.to_split < len(self.items) and self.to_split <= upto:
            i = self.to_split
            self.to_split += 1
            if i not in self.kth:
                continue
            k, (_, nk, w, _) = self.kth[i], self.items[i]
            if k >= SPLIT:
                self.wait_used(act, self.split_items[k - SPLIT])
            self.wait_landed(act, i)
            self.nc.scalar.copy(self.part(i, 0)[:, 0:nk, 0:w], self.raw(i)[:, 0:nk, 0:w]).then_inc(self.hi_ready.sem, 1)

    def low(self, pool):
        for k, i in enumerate(self.split_items):
            _, nk, w, _ = self.items[i]
            pool.wait_ge(self.hi_ready.sem, k + 1)
            self.nc.gpsimd.tensor_tensor(self.part(i, 1)[:, 0:nk, 0:w], self.raw(i)[:, 0:nk, 0:w],
                                         self.part(i, 0)[:, 0:nk, 0:w], ALU.subtract).then_inc(self.lo_ready.sem, 1)

    def multiply(self, pe, s, n, hi, lo, tiles=range(NT), parts_in=None):
        banks, name, k0, opens, closes = self.sums(s)
        i = self.first[s] + n
        _, nk, w, _ = self.items[i]
        early = n == 0
        if parts_in is not None:
            parts_in[0]()
        pe.wait_ge((self.hi_ready if early else self.lo_ready).sem, self.kth[i] + 1)
        products = [(c, a, lo_w) for c in range(nk) for a, lo_w in ((hi, 0), (lo, 0), (hi, 1))]
        if parts_in is not None:
            products = [(c, a, lo_w) for a, lo_w in ((hi, 0), (hi, 1), (lo, 0)) for c in range(nk)]
        elif early:
            products.sort(key=lambda p: p[2])
        for t in tiles:
            use = banks.at[(name, t)]
            b = banks.aps[use % len(banks.aps)]
            if n == 0 and opens:
                banks.fill_ahead(pe, (name, t), use - banks.filled.n)
            final = i == self.last[s] and closes
            for p, (c, a, lo_w) in enumerate(products):
                if early and t == tiles[0] and p == (2 * nk if parts_in is None else nk):
                    pe.wait_ge(self.lo_ready.sem, self.kth[i] + 1)
                if parts_in is not None and t == tiles[0] and p == 2 * nk:
                    parts_in[1]()
                ins = pe.matmul(b[:, 0:w], a(k0 + 2 * n + c, t), self.part(i, lo_w)[:, c, 0:w],
                                start=(opens and n == p == 0), stop=(final and p == len(products) - 1))
            if final:
                banks.full(ins)
            elif t == NT - 1:
                ins.then_inc(self.used.sem, 1)


class Banks:

    def __init__(self, ctx, nc, name, aps, uses):
        self.aps = aps
        self.at = {u: i for i, u in enumerate(uses)}
        assert len(self.at) == len(uses)
        self.filled = Count(ctx, nc, name + "_filled")
        self.emptied = [Count(ctx, nc, f"{name}_emptied{i}") for i in range(len(aps))]

    def fill(self, pe, use):
        i, n = self.at[use], len(self.aps)
        assert self.filled.n == i, (use, i, self.filled.n)
        if i >= n:
            pe.wait_ge(self.emptied[i % n].sem, i // n)
        return self.aps[i % n]

    def fill_ahead(self, pe, use, ahead):
        i, n = self.at[use], len(self.aps)
        assert self.filled.n + ahead == i and ahead < n
        if i >= n:
            pe.wait_ge(self.emptied[i % n].sem, i // n)
        return self.aps[i % n]

    def full(self, ins):
        ins.then_inc(self.filled.sem, 1)
        self.filled.n += 1

    def read(self, eng, use):
        i = self.at[use]
        eng.wait_ge(self.filled.sem, i + 1)
        return self.aps[i % len(self.aps)]

    def taken(self, eng, use):
        i, n = self.at[use], len(self.aps)
        eng.wait_ge(self.emptied[i % n].sem, i // n + 1)

    def drained(self, eng, use):
        i, n = self.at[use], len(self.aps)
        for k in range(max(0, i - n + 1), i + 1):
            eng.wait_ge(self.emptied[k % n].sem, k // n + 1)

    def empty(self, lane, ins, use):
        i, n = self.at[use], len(self.aps)
        c = self.emptied[i % n]
        c.n = i // n
        lane.done(ins, c)


class Places:

    def __init__(self, ctx, nc):
        self.ctx, self.nc, self.offset = ctx, nc, {}

    def __call__(self, name, shape):
        self.offset[name] = -(-self.nc.sbuf_base // 32) * 32
        return self.ctx.enter_context(self.nc.sbuf_tensor(name, shape, F32))

    def over(self, name, place, shape, skip=0):
        return self.nc.alloc_sbuf_tensor_at(name, shape, F32R, offset=self.offset[place] + 4 * skip)


def close_layer(nc, sems):
    nc.all_engine_barrier()
    engines = (nc.gpsimd, nc.sync, nc.scalar, nc.vector, nc.tensor)
    for i, s in enumerate(sems):
        engines[i % len(engines)].sem_clear(s)
    nc.all_engine_barrier()


class Chip:

    def __init__(self, ctx, nc):
        def sb(name, shape, dtype=F32):
            return ctx.enter_context(nc.sbuf_tensor(name, shape, dtype))

        self.x = sb("x", [P, NT, D])
        self.xT = sb("xT", [P, KC, S], F32R)
        self.raw = sb("raw", [P, RAW, 2, HALF])
        self.parts = sb("parts", [P, SPLIT, 2, 2, HALF], F32R)
        self.ident = sb("ident", [P, P])
        self.cbias = sb("cbias", [P, NT, S])
        self.ps = ctx.enter_context(nc.psum_tensor("ps", [P, 8, HALF], F32))

    def bank(self, i):
        return self.ps[:, i, :]


def first_prologue(nc, chip, A):
    with Scope() as ctx:
        c_in, m_in = Count(ctx, nc, "consts_in"), Count(ctx, nc, "memory_in")
        raw = ctx.enter_context(nc.sbuf_tensor("mem_raw", [P, NT, D], F32))
        junk = ctx.enter_context(nc.sbuf_tensor("mem_junk", [P, D], F32))
        ss = ctx.enter_context(nc.sbuf_tensor("mem_ss", [P, 3, NT], F32))
        tp = Banks(ctx, nc, "ptp", [chip.bank(2), chip.bank(3)], [("mem", i) for i in range(KC // 2)])
        sq, rt, sc = (Count(ctx, nc, n) for n in ("mem_squares", "mem_root", "mem_scaled"))
        block = ctx.enter_context(nc.Block())

        @block.sync
        def _(sp):
            sp.dma_start(raw[:], A["mem"].rearrange("b (t p) d -> p (b t) d", p=P)).then_inc(m_in.sem, 16)
            sp.dma_start(chip.ident[:], A["ident"]).then_inc(m_in.sem, 16)
            for dst, src in ((chip.x, A["x"].rearrange("b (t p) d -> p (b t) d", p=P)), (chip.cbias, A["cbias"]),
                             (chip.rope1, A["rope1"])):
                sp.dma_start(dst[:], src).then_inc(c_in.sem, 16)
            sp.wait_ge(c_in.sem, 48)

        @block.scalar
        def _(act):
            lane = Lane(ctx, nc, act, "act0")
            act.wait_ge(m_in.sem, 32)
            for t in range(NT):
                lane.done(nc.scalar.activation(junk[:], raw[:, t, :], ACT.Square, accum_out=ss[:, 0, t:t + 1]), sq)
                lane.settle()
            act.wait_ge(sc.sem, 1)
            lane.done(nc.scalar.activation(ss[:, 2, :], ss[:, 1, :], ACT.Sqrt), rt)

        @block.vector
        def _(dve):
            lane = Lane(ctx, nc, dve, "dve0")
            dve.wait_ge(sq.sem, 2)
            lane.done(nc.vector.tensor_scalar(ss[:, 1, :], ss[:, 0, :], 1.0 / D, RMS_EPS, ALU.mult, ALU.add), sc)
            dve.wait_ge(rt.sem, 1)
            lane.done(nc.vector.reciprocal(ss[:, 0, :], ss[:, 2, :]))
            lane.settle()
            for t in range(NT):
                lane.done(nc.vector.tensor_scalar(raw[:, t, :], raw[:, t, :], ss[:, 0, t:t + 1], None, ALU.mult), sc)
            for i in range(KC // 2):
                b = tp.read(dve, ("mem", i))
                tp.empty(lane, nc.vector.tensor_copy(chip.memT[:, 2 * i:2 * i + 2, :],
                                                     b[:, :].rearrange("p (c t) -> p c t", c=2)), ("mem", i))
            lane.settle()

        @block.tensor
        def _(pe):
            pe.wait_ge(sc.sem, 3)
            for i in range(KC // 2):
                b = tp.fill(pe, ("mem", i))
                for c in range(2):
                    for t in range(NT):
                        ins = pe.transpose(b[:, c * S + t * P:c * S + t * P + P],
                                           raw[:, t, (2 * i + c) * P:(2 * i + c + 1) * P], chip.ident[:])
                tp.full(ins)


IDX = [("i", t, g) for t in range(NT) for g in range(2)]
ATT = ([("a", t, g) for t in range(NT) for g in range(2)] + [("m", t, 0) for t in range(NT)]
       + [("b", t, g) for t in range(NT) for g in range(2)])
GROUPS1 = IDX + ATT


HEAD = [0, 2, 1, 3]


def nkeys(kind, t):
    return S if kind == "m" else P * (t + 1)


def first_layers(nc, chip, A, layers=DEPTH):
    ctx = Scope()
    with ctx:
        sb = Places(ctx, nc)
        H = sb("H", [P, NT, IN1])
        H_lo = sb.over("H_low", "H", [P, NT, IN1])
        M = sb("M", [P, NT, D])
        M_lo = sb.over("M_low", "M", [P, NT, D])
        QKT = sb("QKT", [P, 5, 4, S])
        ysT = sb.over("ysT", "QKT", [P, 12, S])
        ikT = sb("ikT", [P, S])
        mqT = sb("mqT", [P, 4, S])
        kmT = sb("kmT", [P, 4, S])
        KV = sb("KV", [P, NT, D])
        gv = sb("gv", [P, 2 * KC])
        sm = sb("sm", [P, 2, 4, S])
        PT = sb("PT", [P, 2, NT, 4, P])
        mn_hi = sb.over("mn_high", "sm", [P, KC, S])
        mn_lo = sb.over("mn_low", "PT", [P, KC, S])
        acc = sb("acc", [P, NT, S])
        bbias = sb("bbias", [P, NT, S])
        ra, rb = acc[:, :, :].rearrange("p t s -> p (t s)"), bbias[:, :, :].rearrange("p t s -> p (t s)")
        ikd = sb("ikd", [P, NT, P])
        wi = sb("wi", [P, NT, 8])
        m8 = sb("m8", [P, 8])
        st = sb("st", [P, 3, NT])
        nmx = sb("nmx", [P, len(ATT), 4])
        den = sb("den", [P, len(ATT), 4])
        rden = sb("rden", [P, len(ATT), 4])
        up = sm[:, 0, 0:2, :].rearrange("p a s -> p (a s)")
        hT = chip.xT
        x = chip.x

        w_in = A["w_in"]
        early = [8, 9, 10, 11, 4, 5, 6, 0, 1, 2]
        late = [3, 7] + list(range(12, 18))
        third = -(-(MIX - IK) // 6) * 2
        cols = [(j * HALF, HALF) for j in range(9)] + [(IK + j * third, min(third, MIX - IK - j * third)) for j in range(3)] \
            + [(MIX + j * HALF, HALF) for j in range(6)]
        steps = ([("mem", 0), ("mem", 1)] + [("in", j) for j in early + late]
                 + [("up", h, n) for h in range(2) for n in range(3)] + [("out", 0), ("out", 1)])
        pairs = ((AQ, AG, AK), (BQ, BG, BK), (MQ, MG, IQ))
        tail = len(GROUPS1) + 2
        late_parts = [(("in", j), n) for j in late for n in range(KC // 2)]
        pj_uses = [(s, t) for s in steps for t in range(NT)]
        PJ = Banks(ctx, nc, "pj", [chip.bank(0), chip.bank(1)], pj_uses)
        tp_uses = [("h", i) for i in range(4)] + [("q", w, i) for w in (4, 0, 1, 2, 3) for i in range(2)] \
            + [("ik",), ("mq", 0), ("mq", 1), ("km", 0), ("km", 1)]
        tp_uses += [("o", i) for i in range(len(ATT))]
        tp_uses += [("y", i) for i in range(6)] + [("m", i) for i in range(4)]
        TP = Banks(ctx, nc, "tp", [chip.bank(2), chip.bank(3)], tp_uses)

        tail_steps = [s for s, n in late_parts[tail:] if n == KC // 2 - 1]
        assert len(late_parts) - tail >= 5
        n_mixed = cols[tail_steps[0][1]][0] - MIX

        def chunks(ap, k0, nk, c0, w):
            return ap[k0 * P:(k0 + nk) * P, c0:c0 + w].rearrange("(c p) n -> p c n", p=P)

        g_in = Count(ctx, nc, "gains_in")
        h_sq, h_rt, h_sc, h_nm = (Count(ctx, nc, n) for n in ("h_squares", "h_root", "h_scaled", "h_normed"))
        mn_ok = Count(ctx, nc, "mn_ready")
        roped = Count(ctx, nc, "roped")
        sc_full, sc_read = Count(ctx, nc, "scores_full"), Count(ctx, nc, "scores_read")
        relu_ok, relu_used = Count(ctx, nc, "relu_ready"), Count(ctx, nc, "relu_used")
        mx_ok, p_ok = Count(ctx, nc, "max_ready"), Count(ctx, nc, "p_ready")
        pt_full, pt_ok = Count(ctx, nc, "pT_full"), Count(ctx, nc, "pT_ready")
        g_sig, y_gated, mix_sig = (Count(ctx, nc, n) for n in ("g_sigmoid", "y_gated", "mix_sigmoid"))
        m_ok = Count(ctx, nc, "m_ready")
        m_hi, y_hi = Count(ctx, nc, "m_high"), Count(ctx, nc, "y_high")
        act_lane = Lane(ctx, nc, nc.scalar, "act1")
        dve_lane = Lane(ctx, nc, nc.vector, "dve1")
        scb = chip.ps[:, 4:6, :].rearrange("p a (b n) -> p (a b) n", b=2)
        ptb = chip.ps[:, 6:8, :]

        def smv(a, j):
            kind, t, g = ATT[a]
            return sm[:, a % 2, j, 0:nkeys(kind, t)]

        def turned(b, n=2):
            return b[:, 0:n * S].rearrange("p (c t) -> p c t", c=n)

        with nc.Fori(0, layers) as l:
            parts = []
            for s in steps:
                w = HALF
                if s[0] == "in":
                    c0, w = cols[s[1]]
                    name = "w_in"
                elif s[0] == "up":
                    name, c0 = "w_branch", s[1] * HALF
                else:
                    name, c0 = {"mem": "w_mem_kv", "out": "w_out"}[s[0]], s[1] * HALF
                if s[0] == "up":
                    src = [lambda l, q=q, c0=c0, n=s[2]: chunks(A["w_branch"][l, n], 2 * q, 2, c0, HALF) for q in range(2)]
                else:
                    src = [lambda l, q=q, c0=c0, w=w, n=name: chunks(A[n][l], 2 * q, 2, c0, w) for q in range(KC // 2)]
                parts.append((s, [(f, 2, w) for f in src], (s, NT - 1)))
            W = Weights(ctx, nc, chip, PJ, "w", parts)

            with nc.Block() as block:

                @block.sync
                def _(sp):
                    sp.dma_start(gv[:], A["vec1"][l]).then_inc(g_in.sem, 16)
                    W.load(sp, l, 0, len(W.items))

                @block.gpsimd
                def _(pool):
                    W.low(pool)

                @block.tensor
                def _(pe):
                    def turn(use, srcs):
                        b = TP.fill(pe, use)
                        for k, src in enumerate(srcs):
                            ins = pe.transpose(b[:, k * P:(k + 1) * P], src, chip.ident[:])
                        TP.full(ins)

                    def hi_of(T):
                        return lambda k, t: T[:, k, t * P:(t + 1) * P]

                    def step_part(s, n, parts_in=None):
                        hi, lo = hi_of(hT), lambda k, t: M_lo[:, t, k * P:(k + 1) * P]
                        if s[0] == "mem":
                            if s[1] == 0:
                                pe.wait_ge(mn_ok.sem, n + 1)
                            hi, lo = hi_of(mn_hi), hi_of(mn_lo)
                        elif s[0] == "up":
                            c0 = (AQ, BQ, MQ)[s[2]]
                            hi, lo = hi_of(ysT[:, 4 * s[2]:4 * s[2] + 4, :]), lambda k, t: H_lo[:, t, c0 + k * P:c0 + (k + 1) * P]
                        W.multiply(pe, s, n, hi, lo, parts_in=parts_in)

                    def step(s):
                        for n in range(W.last[s] - W.first[s] + 1):
                            step_part(s, n)

                    def scores(n):
                        kind, t, g = GROUPS1[n]
                        if n >= 1:
                            pe.wait_ge(sc_read.sem, n)
                        for s in (0, 2, 1, 3):
                            j = HEAD[s]
                            h = 4 * g + j
                            nk = S if kind == "i" else nkeys(kind, t)
                            r = slice(64 * (h % 2), 64 * (h % 2) + 64)
                            q, k = {"i": (QKT[r, 4, h // 2], ikT[r]), "a": (QKT[r, 0, h // 2], QKT[r, 1, h // 2]),
                                    "b": (QKT[r, 2, h // 2], QKT[r, 3, h // 2]), "m": (mqT[:, j % 4], kmT[:, j % 4])}[kind]
                            ins = pe.matmul(scb[:, s, 0:nk], q[:, t * P:(t + 1) * P], k[:, 0:nk],
                                            start=True, stop=True)
                        ins.then_inc(sc_full.sem, 1)

                    def turn_p(a):
                        kind, t, g = ATT[a]
                        pe.wait_ge(p_ok.sem, a + 1)
                        if a >= 1:
                            pe.wait_ge(pt_ok.sem, a)
                        for kt in range(nkeys(kind, t) // P):
                            for j in range(4):
                                ins = pe.transpose(ptb[:, kt, j * P:(j + 1) * P], smv(a, j)[:, kt * P:(kt + 1) * P],
                                                   chip.ident[:])
                        ins.then_inc(pt_full.sem, 1)

                    def values(a):
                        kind, t, g = ATT[a]
                        b = TP.fill(pe, ("o", a))
                        pe.wait_ge(pt_ok.sem, a + 1)
                        dv = P if kind == "m" else HD
                        for s in range(4):
                            n = nkeys(kind, t) // P
                            for kt in range(n):
                                j = HEAD[s]
                                h = 4 * g + j
                                v = {"a": H[:, kt, AV + h * HD:AV + (h + 1) * HD], "b": H[:, kt, BV + h * HD:BV + (h + 1) * HD],
                                     "m": KV[:, kt, BR + (j * P) % BR:BR + (j * P) % BR + P]}[kind]
                                ins = pe.matmul(b[:, s * dv:(s + 1) * dv], PT[:, a % 2, kt, s, :], v,
                                                start=(kt == 0), stop=(kt == n - 1))
                        TP.full(ins)

                    step(("mem", 0))
                    pe.wait_ge(h_nm.sem, NT)
                    for i in range(4):
                        turn(("h", i), [H[:, t, (2 * i + c) * P:(2 * i + c + 1) * P] for c in range(2) for t in range(NT)])
                    step(("mem", 1))
                    TP.drained(pe, ("h", 3))
                    for j in early:
                        step(("in", j))
                    for w, c0 in ((4, IQ), (0, AQ), (1, AK), (2, BQ), (3, BK)):
                        pe.wait_ge(roped.sem, {4: 1, 0: 2, 1: 2, 2: 3, 3: 3}[w])
                        for i in range(2):
                            turn(("q", w, i), [H[:, t, c0 + (2 * i + c) * P:c0 + (2 * i + c + 1) * P]
                                               for c in range(2) for t in range(NT)])
                    pe.wait_ge(roped.sem, 4)
                    turn(("ik",), [ikd[:, t, :] for t in range(NT)])
                    for i in range(2):
                        turn(("mq", i), [H[:, t, MQ + (2 * i + c) * P:MQ + (2 * i + c + 1) * P] for c in range(2) for t in range(NT)])
                    PJ.drained(pe, (("mem", 1), 1))
                    for i in range(2):
                        turn(("km", i), [KV[:, t, (2 * i + c) * P:(2 * i + c + 1) * P] for c in range(2) for t in range(NT)])
                    for k in range(max(len(late_parts), len(GROUPS1) + 2)):
                        if k == len(late_parts) - 1:
                            pe.wait_ge(y_gated.sem, 6)
                            for i in range(6):
                                c0 = [AQ, BQ, MQ][i // 2] + (i % 2) * 256
                                turn(("y", i), [H[:, t, c0 + c * P:c0 + (c + 1) * P] for c in range(2) for t in range(NT)])
                        if k < len(late_parts):
                            step_part(*late_parts[k])
                        if k == 0:
                            TP.drained(pe, ("km", 1))
                        if k < len(GROUPS1):
                            scores(k)
                        a = k - len(IDX)
                        if 0 <= a - 1 < len(ATT):
                            turn_p(a - 1)
                        if 0 <= a - 2 < len(ATT):
                            values(a - 2)
                    TP.drained(pe, ("y", 5))

                    def turn_m(h):
                        pe.wait_ge(m_ok.sem, NT * (h + 1))
                        for i in (2 * h, 2 * h + 1):
                            turn(("m", i), [M[:, t, (2 * i + c) * P:(2 * i + c + 1) * P] for c in range(2) for t in range(NT)])

                    def m_parts(i):
                        return lambda: pe.wait_ge(m_hi.sem, i + 1), lambda: TP.taken(pe, ("m", i))

                    for s in steps:
                        if s[0] == "up":
                            step(s)
                            if s == ("up", 1, 0):
                                turn_m(0)
                    for n in range(2):
                        step_part(("out", 0), n, m_parts(n))
                    turn_m(1)
                    for n in range(2, 4):
                        step_part(("out", 0), n, m_parts(n))
                    step(("out", 1))

                @block.scalar
                def _(act):
                    lane = act_lane
                    for t in range(NT):
                        lane.done(nc.scalar.activation(H[:, 0, t * D:(t + 1) * D], x[:, t, :], ACT.Square,
                                                       accum_out=st[:, 0, t:t + 1]), h_sq)
                        W.high(act, t)
                    W.high(act, SPLIT - 2)
                    act.wait_ge(h_sc.sem, 1)
                    lane.done(nc.scalar.activation(st[:, 2, :], st[:, 1, :], ACT.Sqrt), h_rt)
                    lane.settle()

                    def take(s, t):
                        b = PJ.read(act, (s, t))
                        if s[0] == "in":
                            c0, w = cols[s[1]]
                            if s in tail_steps:
                                PJ.empty(lane, nc.scalar.activation(H[:, t, c0:c0 + w], b[:, 0:w], ACT.Sigmoid), (s, t))
                            else:
                                PJ.empty(lane, nc.scalar.copy(H[:, t, c0:c0 + w], b[:, 0:w]), (s, t))
                        else:
                            PJ.empty(lane, nc.scalar.copy(KV[:, t, s[1] * HALF:(s[1] + 1) * HALF], b[:, 0:HALF]), (s, t))
                    def pace(s, n):
                        W.high(act, W.first[s] + n + SPLIT - 1)
                        if W.first[s] + n == W.last[s] and s[0] in ("in", "mem"):
                            for t in range(NT):
                                take(s, t)

                    for s in [("mem", 0), ("mem", 1)] + [("in", j) for j in early]:
                        for n in range(KC // 2):
                            if s == ("in", early[0]) and n == KC // 2 - 1:
                                TP.drained(act, ("h", 3))
                            pace(s, n)
                    for k in range(max(len(late_parts), len(GROUPS1) + 2)):
                        if k >= tail:
                            n = k - tail
                            if n < 3:
                                _, g0, s0 = pairs[n]
                                if n == 0:
                                    lane.settle()
                                lane.done(nc.scalar.activation(H[:, :, s0:s0 + BR], H[:, :, g0:g0 + BR], ACT.Sigmoid), g_sig)
                            elif n < 5:
                                t = n - 3
                                lane.done(nc.scalar.activation(H[:, t, MIX:MIX + n_mixed], H[:, t, MIX:MIX + n_mixed], ACT.Sigmoid), mix_sig)
                        if k == len(late_parts) - 1:
                            for i in range(6):
                                b = TP.read(act, ("y", i))
                                lane.done(nc.scalar.copy(ysT[:, 2 * i:2 * i + 2, :], turned(b)), y_hi)
                        if k < len(late_parts):
                            pace(*late_parts[k])
                        a = k - len(IDX)
                        if 0 <= a - 1 < len(ATT):
                            kind, t, g = ATT[a - 1]
                            nk = nkeys(kind, t) // P
                            act.wait_ge(pt_full.sem, a)
                            if a - 1 >= 2:
                                act.wait_ge(TP.filled.sem, TP.at[("o", a - 3)] + 1)
                            lane.done(nc.scalar.copy(PT[:, (a - 1) % 2, 0:nk].rearrange("p k j s -> p (k j s)"),
                                                     ptb[:, 0:nk, :].rearrange("p k n -> p (k n)")), pt_ok)
                        if k < len(IDX):
                            act.wait_ge(sc_full.sem, k + 1)
                            if k >= 2:
                                act.wait_ge(relu_used.sem, k - 1)
                            lane.done(nc.scalar.activation(sm[:, k % 2], scb, ACT.Relu,
                                                           scale=float(HD) ** -0.5), sc_read)
                        elif a < len(ATT):
                            act.wait_ge(mx_ok.sem, a + 1)
                            for j in range(4):
                                lane.done(nc.scalar.activation(smv(a, j), smv(a, j), ACT.Exp, bias=nmx[:, a, j:j + 1],
                                                               accum_out=den[:, a, j:j + 1]),
                                          p_ok if j == 3 else None)
                    lane.settle()
                    def m_high(h):
                        for i in (2 * h, 2 * h + 1):
                            b = TP.read(act, ("m", i))
                            lane.done(nc.scalar.copy(hT[:, 2 * i:2 * i + 2, :], turned(b)), m_hi)

                    for s in steps:
                        if s[0] == "up":
                            for n in range(2):
                                pace(s, n)
                            if s == ("up", 1, 0):
                                m_high(0)
                    for n in range(2):
                        pace(("out", 0), n)
                    m_high(1)
                    for j, n in ((0, 2), (0, 3), (1, 0), (1, 1), (1, 2), (1, 3)):
                        pace(("out", j), n)

                @block.vector
                def _(dve):
                    lane = dve_lane
                    v = nc.vector

                    def by_tile(u):
                        return u.rearrange("p (t n) -> p t n", t=NT)

                    def low_of(k):
                        return M_lo[:, :, k * P:(k + 1) * P]

                    dve.wait_ge(g_in.sem, 16)
                    for i in range(4):
                        two = slice(2 * i, 2 * i + 2)
                        lane.done(v.tensor_tensor(mn_hi[:, two, :], chip.memT[:, two, :],
                                                  gv[:, KC + 2 * i:KC + 2 * i + 2].unsqueeze(2).to_broadcast([P, 2, S]), ALU.mult))
                        lane.settle()
                        for k in (2 * i, 2 * i + 1):
                            lane.done(v.scalar_tensor_tensor(out=mn_lo[:, k, :], in0=chip.memT[:, k, :], scalar=gv[:, KC + k:KC + k + 1],
                                                             in1=mn_hi[:, k, :], op0=ALU.mult, op1=ALU.subtract),
                                      mn_ok if k % 2 else None)
                    dve.wait_ge(h_sq.sem, NT)
                    lane.done(v.tensor_scalar(st[:, 1, :], st[:, 0, :], 1.0 / D, RMS_EPS, ALU.mult, ALU.add), h_sc)
                    dve.wait_ge(h_rt.sem, 1)
                    lane.done(v.reciprocal(st[:, 0, :], st[:, 2, :]))
                    lane.settle()
                    for t in range(NT):
                        lane.done(v.tensor_scalar(H[:, t, 0:D], x[:, t, :], st[:, 0, t:t + 1], None, ALU.mult), h_nm)
                    for i in range(4):
                        b = TP.read(dve, ("h", i))
                        lane.done(v.tensor_tensor(hT[:, 2 * i:2 * i + 2, :], turned(b),
                                                  gv[:, 2 * i:2 * i + 2].unsqueeze(2).to_broadcast([P, 2, S]), ALU.mult))
                        lane.settle()
                        for c in range(2):
                            k = 2 * i + c
                            ins = v.scalar_tensor_tensor(out=low_of(k), in0=by_tile(b[:, c * S:(c + 1) * S]), scalar=gv[:, k:k + 1],
                                                         in1=by_tile(hT[:, k, :]), op0=ALU.mult, op1=ALU.subtract)
                            lane.done(ins) if c == 0 else TP.empty(lane, ins, ("h", i))
                    def rope(c0, nh):
                        X = H[:, :, c0:c0 + nh * HD].rearrange("p t (h d) -> p t h d", d=HD)
                        n = NT * nh * 16
                        a_ = ra[:, 0:n].rearrange("p (t h d) -> p t h d", t=NT, d=16)
                        b_ = rb[:, 0:n].rearrange("p (t h d) -> p t h d", t=NT, d=16)
                        C = chip.rope1[:, :, 0, :]
                        Sn = chip.rope1[:, :, 1, :]
                        lane.done(v.tensor_tensor(a_, X[:, :, :, 0:16], C.unsqueeze(2).to_broadcast([P, NT, nh, 16]), ALU.mult))
                        lane.done(v.tensor_tensor(b_[:, :, :, 0:8], X[:, :, :, 8:16],
                                                  Sn[:, :, 0:8].unsqueeze(2).to_broadcast([P, NT, nh, 8]), ALU.mult))
                        lane.done(v.tensor_tensor(b_[:, :, :, 8:16], X[:, :, :, 0:8],
                                                  Sn[:, :, 8:16].unsqueeze(2).to_broadcast([P, NT, nh, 8]), ALU.mult))
                        lane.settle()
                        lane.done(v.tensor_tensor(X[:, :, :, 0:16], a_, b_, ALU.add), roped)
                        lane.settle()

                    PJ.drained(dve, (("in", 9), 1))
                    rope(IQ, 9)
                    lane.done(v.tensor_scalar(wi[:, :, :], H[:, :, IW:IW + 8], 8.0 ** -0.5, None, ALU.mult))
                    PJ.drained(dve, (("in", 1), 1))
                    rope(AQ, 16)
                    rope(BQ, 16)
                    lane.done(v.tensor_copy(ikd[:, :, 0:HD], H[:, :, IK:IK + HD]))
                    lane.settle()
                    lane.done(v.tensor_copy(ikd[:, :, HD:P], H[:, :, IK:IK + HD]), roped)
                    for w in (4, 0, 1, 2, 3):
                        for i in range(2):
                            b = TP.read(dve, ("q", w, i))
                            TP.empty(lane, v.tensor_copy(QKT[:, w, 2 * i:2 * i + 2, :], turned(b)), ("q", w, i))
                    b = TP.read(dve, ("ik",))
                    TP.empty(lane, v.tensor_copy(ikT[:, :], b[:, 0:S]), ("ik",))
                    for nm, dst in (("mq", mqT), ("km", kmT)):
                        for i in range(2):
                            b = TP.read(dve, (nm, i))
                            TP.empty(lane, v.tensor_copy(dst[:, 2 * i:2 * i + 2, :], turned(b)), (nm, i))

                    def top(t):
                        nk = P * (t + 1)
                        a_ = acc[:, t, 0:nk]
                        for _ in range(TOPK // 8):
                            lane.done(v.max(m8[:, :], a_))
                            lane.settle()
                            lane.done(v.match_replace(a_, m8[:, :], a_, TAKEN))
                            lane.settle()
                        lane.done(v.tensor_scalar(bbias[:, t, 0:nk], a_, TAKEN / 2, NEG, ALU.is_gt, ALU.mult))
                        lane.settle()
                        lane.done(v.tensor_tensor(bbias[:, t, 0:nk], bbias[:, t, 0:nk], chip.cbias[:, t, 0:nk], ALU.add))
                        lane.settle()

                    def output(a):
                        kind, t, g = ATT[a]
                        dv = P if kind == "m" else HD
                        b = TP.read(dve, ("o", a))
                        dve.wait_ge(p_ok.sem, a + 1)
                        lane.done(v.reciprocal(rden[:, a, :], den[:, a, :]))
                        lane.settle()
                        c0 = {"a": AQ, "b": BQ, "m": MQ}[kind] + g * 4 * dv
                        TP.empty(lane, v.tensor_tensor(H[:, t, c0:c0 + 4 * dv].rearrange("p (a b d) -> p b a d", a=2, b=2),
                                                       b[:, 0:4 * dv].rearrange("p (b a d) -> p b a d", a=2, b=2),
                                                       rden[:, a, :].rearrange("p (b a) -> p b a", a=2).unsqueeze(3)
                                                       .to_broadcast([P, 2, 2, dv]), ALU.mult), ("o", a))

                    for k in range(len(GROUPS1) + 2):
                        a = k - len(IDX)
                        if k < len(IDX):
                            _, t, g = IDX[k]
                            dve.wait_ge(sc_read.sem, k + 1)
                            for j in range(4):
                                prev = chip.cbias[:, t, :] if g == 0 and j == 0 else acc[:, t, :]
                                lane.settle()
                                lane.done(v.scalar_tensor_tensor(out=acc[:, t, :], in0=sm[:, k % 2, HEAD.index(j), :],
                                                                 scalar=wi[:, t, 4 * g + j:4 * g + j + 1], in1=prev,
                                                                 op0=ALU.mult, op1=ALU.add), relu_used if j == 3 else None)
                            lane.settle()
                        elif a < len(ATT):
                            kind, t, g = ATT[a]
                            nk = nkeys(kind, t)
                            dve.wait_ge(sc_full.sem, k + 1)
                            if a >= 2:
                                dve.wait_ge(pt_full.sem, a - 1)
                            s_ = sm[:, a % 2, :, 0:nk]
                            if kind == "m":
                                lane.done(v.tensor_scalar(s_, scb[:, :, 0:nk], float(P) ** -0.5, None, ALU.mult), sc_read)
                            else:
                                bias = (chip.cbias if kind == "a" else bbias)[:, t, 0:nk].unsqueeze(1).to_broadcast([P, 4, nk])
                                lane.done(v.scalar_tensor_tensor(out=s_, in0=scb[:, :, 0:nk],
                                                                 scalar=float(HD) ** -0.5, in1=bias,
                                                                 op0=ALU.mult, op1=ALU.add), sc_read)
                            lane.settle()
                            lane.done(v.tensor_reduce(nmx[:, a, :], s_, AX_X, ALU.max,
                                                      negate=True), mx_ok)
                            if a in (1, 3):
                                top(a // 2)
                        if 0 <= a - 2 < len(ATT):
                            output(a - 2)
                    lane.settle()
                    for n, (c0, g0, s0) in enumerate(pairs):
                        dve.wait_ge(g_sig.sem, n + 1)
                        lane.done(v.tensor_tensor(H[:, :, g0:g0 + BR], H[:, :, g0:g0 + BR], H[:, :, s0:s0 + BR], ALU.mult))
                        lane.settle()
                        for t in range(NT):
                            lane.done(v.tensor_tensor(H[:, t, c0:c0 + BR], H[:, t, c0:c0 + BR], H[:, t, g0:g0 + BR], ALU.mult),
                                      y_gated)
                    for i in range(6):
                        b = TP.read(dve, ("y", i))
                        hi = ysT[:, 2 * i:2 * i + 2, :]
                        dve.wait_ge(y_hi.sem, i + 1)
                        c0 = [AQ, BQ, MQ][i // 2] + (i % 2) * 256
                        TP.empty(lane, v.tensor_tensor(H_lo[:, :, c0:c0 + 256].rearrange("p t (c n) -> p c t n", c=2),
                                                       turned(b).rearrange("p c (t n) -> p c t n", t=NT),
                                                       hi.rearrange("p c (t n) -> p c t n", t=NT), ALU.subtract), ("y", i))
                    PJ.drained(dve, (("in", late[-1]), 1))
                    dve.wait_ge(mix_sig.sem, NT)

                    def m_low(h):
                        for i in (2 * h, 2 * h + 1):
                            b = TP.read(dve, ("m", i))
                            dve.wait_ge(m_hi.sem, i + 1)
                            TP.empty(lane, v.tensor_tensor(M_lo[:, :, 2 * i * P:(2 * i + 2) * P].rearrange("p t (c n) -> p c t n", c=2),
                                                           turned(b).rearrange("p c (t n) -> p c t n", t=NT),
                                                           hT[:, 2 * i:2 * i + 2, :].rearrange("p c (t n) -> p c t n", t=NT),
                                                           ALU.subtract), ("m", i))

                    for s in steps:
                        if s[0] != "up":
                            continue
                        _, h, n = s
                        for t in range(NT):
                            b = PJ.read(dve, (s, t))
                            gate = H[:, t, MIX + n * D + h * HALF:MIX + n * D + (h + 1) * HALF]
                            dst = M[:, t, h * HALF:(h + 1) * HALF]
                            if n == 0:
                                PJ.empty(lane, v.tensor_tensor(dst, b[:, :], gate, ALU.mult), (s, t))
                            else:
                                lane.settle()
                                PJ.empty(lane, v.tensor_tensor(up, b[:, :], gate, ALU.mult), (s, t))
                                lane.settle()
                                lane.done(v.tensor_tensor(dst, dst, up, ALU.add), m_ok if n == 2 else None)
                        if (h, n) == (1, 0):
                            m_low(0)
                    m_low(1)
                    for h in range(2):
                        for t in range(NT):
                            b = PJ.read(dve, (("out", h), t))
                            xs = x[:, t, h * HALF:(h + 1) * HALF]
                            PJ.empty(lane, v.tensor_tensor(xs, b[:, :], xs, ALU.add), (("out", h), t))
                    lane.settle()
            close_layer(nc, ctx.sems)
GQ, GK, GV, GG, GLR = 0, 256, 512, 768, 1024
RR, RK_, RV, RWA, RG = 1040, 1296, 1552, 1808, 1936
VRES = 2096
NQ = VRES + 32
NKC, NVC, NKS, NVS, NKW, NVW, NGT = [NQ + 512 + 128 * i for i in range(7)]
IN2 = NGT + 24
FFN = 2816
FC = FFN // P
ALPHA = (2 * DEPTH) ** 0.25
WIN = [0, 128, 256, 384, 768, 896, 1024, 1040, 1168, 1296, 1424, 1552, 1680, 1808, 1936, VRES - P, NQ - P]
F_GQ, F_GK, F_GG, F_LR, F_R, F_K, F_V, F_WA, F_G0, F_G1, F_VR = 0, 2, 4, 6, 7, 9, 11, 13, 14, 15, 16
V_MU, V_W0, V_A0, V_V0, V_KK, V_KA, V_RK, V_BA, V_LNW, V_LNB, V_FLAG = 0, 10, 12, 14, 16, 18, 20, 22, 24, 28, 32
NV2 = 33
CH = 64
LEVELS = 6
M_STRICT, M_INCL, M_EYE = 6, 7, 8
E_HALF = float(np.exp(-0.5))
RWKV_GN_EPS = 64e-5
NC = 15
GROUPS2 = [(k, t, g) for k in "swc" for t in range(NT) for g in range(2)]


def second_prologue(nc, chip, A):
    with Scope() as ctx:
        c_in, g_in = Count(ctx, nc, "consts2_in"), Count(ctx, nc, "final_gain_in")
        s_sq, s_ms, s_rt, s_rs = (Count(ctx, nc, n) for n in ("fin_squares", "fin_mean", "fin_root", "fin_scaled"))
        fg = ctx.enter_context(nc.sbuf_tensor("final_gain", [P, D], F32))
        junk = ctx.enter_context(nc.sbuf_tensor("fin_junk", [P, D], F32))
        ss = ctx.enter_context(nc.sbuf_tensor("fin_ss", [P, 3, NT], F32))
        block = ctx.enter_context(nc.Block())

        @block.sync
        def _(sp):
            sp.dma_start(fg[:], A["final_g"].partition_broadcast(P)).then_inc(g_in.sem, 16)
            for dst, src in ((chip.rope2, A["rope2"]), (chip.cmpb, A["cmpb"]),
                             (chip.rowv, A["rowv"]), (chip.ones, A["ones"]), (chip.masks, A["masks"]), (chip.reset, A["reset"])):
                sp.dma_start(dst[:], src).then_inc(c_in.sem, 16)
            sp.wait_ge(c_in.sem, 96)

        @block.scalar
        def _(act):
            lane = Lane(ctx, nc, act, "act_f")
            for t in range(NT):
                lane.done(nc.scalar.activation(junk[:], chip.x[:, t, :], ACT.Square, accum_out=ss[:, 0, t:t + 1]), s_sq)
                lane.settle()
            act.wait_ge(s_ms.sem, 1)
            lane.done(nc.scalar.activation(ss[:, 2, :], ss[:, 1, :], ACT.Sqrt), s_rt)

        @block.vector
        def _(dve):
            lane = Lane(ctx, nc, dve, "dve_f")
            lane.done(nc.vector.memset(chip.vfirst[:, :, :], 0.0))
            dve.wait_ge(s_sq.sem, NT)
            lane.done(nc.vector.tensor_scalar(ss[:, 1, :], ss[:, 0, :], 1.0 / D, RMS_EPS, ALU.mult, ALU.add), s_ms)
            dve.wait_ge(s_rt.sem, 1)
            lane.done(nc.vector.reciprocal(ss[:, 0, :], ss[:, 2, :]))
            dve.wait_ge(g_in.sem, 16)
            lane.settle()
            for t in range(NT):
                lane.done(nc.vector.scalar_tensor_tensor(out=chip.x[:, t, :], in0=chip.x[:, t, :], scalar=ss[:, 0, t:t + 1],
                                                         in1=fg[:, :], op0=ALU.mult, op1=ALU.mult), s_rs)
            lane.settle()


def second_layers(nc, chip, A, layers=DEPTH):
    ctx = Scope()
    with ctx:
        sb = Places(ctx, nc)
        x, xT, masks = chip.x, chip.xT, chip.masks
        H = sb("H2", [P, NT, IN2])
        H_lo = sb.over("H2_low", "H2", [P, NT, IN2])
        OT = xT
        FT = sb("FT", [P, len(WIN), S])
        LD = sb("LD", [P, 4, S])
        CUM = sb("CUM", [P, 4, S])
        EP = sb("EP", [P, 4, S])
        EE = sb("EE", [P, 4, S])
        EN = sb("EN", [P, 2, S])
        EM = LD[:, 2:4, :]
        IC = sb("IC", [P, 2, S])
        GT = sb("GT", [P, 2, S])
        BON = sb("BON", [P, 2, S])
        KK = sb("KK", [P, 2, S])
        BB = sb("BB", [P, 2, S])
        BP = sb("BP", [P, 2, S])
        DL = sb("DL", [P, 10, S])
        VAL = DL[:, 6:10, :]
        KP, GQt, TM, TM2 = DL[:, 0:4, :], DL[:, 4:6, :], DL[:, 6:8, :], DL[:, 8:10, :]
        BAt = H[:, :, 0:HALF]
        KPt = H[:, :, NQ:NQ + HALF]
        VT = H[:, :, NKC:NKC + S]
        Us = H[:, :, GG:GG + S]
        PTf = LD[:, 0:2, :]
        Wb = H[:, 0, NKS:NKS + 8 * CH].rearrange("p (u d) -> p u d", u=8)
        Qb = H[:, 1, NKS:NKS + 8 * CH].rearrange("p (u d) -> p u d", u=8)
        SP = sb("SP", [P, 4, P])
        NS = H[:, :, RR:RR + HALF]
        Y = H[:, :, RV:RV + HALF]
        HID = H[:, :, RV:RV + HALF].rearrange("p k (f n) -> p k f n", f=2)
        ge = [KP[:, 0:2, :], KP[:, 2:4, :], BP[:, :, :]]
        kcT = H[:, 0, 0:S].rearrange("p (g n) -> p g n", g=2)
        vcp = H[:, 1, 0:P].rearrange("p (g n) -> p g n", g=2)
        part_out = H[:, 0, S:2 * S]

        gate = sb("gate", [P, NT, 24])
        st = sb("st2", [P, 4, 16])
        vec = sb("vec2s", [P, NV2])
        posT = sb("posT", [P, 2, 16])
        sw = sb("smallw", [P, 6, S])
        w2k = sb("w2k", [P, 2, P])
        w2v = sb("w2v", [P, 2, HD])
        nmx = sb("nmx2", [P, len(GROUPS2), 4])
        den = sb("den2", [P, len(GROUPS2), 4])
        fac = sb("fac2", [P, len(GROUPS2), 4])
        bn = sb("bn", [P, NT, 2, 6])
        mv = sb("mv", [P, NT, 2])
        arena = sb("arena", [P, 10240])
        top_of = {}

        def carve(part, shape):
            n = int(np.prod(shape))
            o = top_of.get(part, 0)
            top_of[part] = o + n
            assert o + n <= 10240, part
            names = "abcd"[:len(shape)]
            return arena[:, o:o + n].rearrange(f"p ({' '.join(names)}) -> p {' '.join(names)}", **dict(zip(names, shape)))

        qT = carve("nsa", [4, S])
        KT = carve("nsa", [8, S])
        sm = carve("nsa", [2, 4, S])
        PT = carve("nsa", [2, NT, 4 * P])
        DD = PT.rearrange("p a k n -> p (a k n)").rearrange("p (t s a d) -> p t s a d", t=NT, s=8, a=2)
        BLK = carve("nsa", [2, 16, 2 * NC])
        AB, AK, RB, RK, SC = (carve("rec", [8, P]) for _ in range(5))
        T_, TT, BT, UU = (carve("rec", [8, P]) for _ in range(4))
        PN = carve("rec", [2, 2, S])
        x_lo = sb.over("x_low", "arena", [P, KC, S])
        x1_lo = sb.over("x1_low", "FT", [P, KC, S])
        carve("ffn", [FC, S])
        aT = sb.over("aT", "arena", [P, FC, S])
        ln = carve("ffn", [4, D])
        sg = EE.rearrange("p (t c) s -> p t (c s)", t=2)

        MIXED = -(-NQ // HALF)
        cols = [(j * HALF, min(HALF, IN2 - j * HALF)) for j in range(7)]
        fcols = [(j * HALF, min(HALF, FFN - j * HALF)) for j in range(6)]
        steps = ([("in", j) for j in range(7)] + [("cmp", kv) for kv in range(2)]
                 + [(k, j) for k in ("out_nsa", "out_mix") for j in range(2)]
                 + [(k, j) for j in range(6) for k in ("gt", "up")] + [("dn", 0), ("dn", 1)])
        uses = []
        for s in steps:
            if s[0][:3] != "out":
                uses += [(s, 0)] if s[0] == "cmp" else [(s, t) for t in range(NT)]
        PJ = Banks(ctx, nc, "pj2", [chip.bank(0), chip.bank(1)], uses)

        def chunks(ap, k0, nk, c0, w):
            return ap[k0 * P:(k0 + nk) * P, c0:c0 + w].rearrange("(c p) n -> p c n", p=P)

        parts = []
        for s in steps:
            if s[0] == "cmp":
                src = [(lambda l, n=("nsa_wk1_2", "nsa_wv1_2")[s[1]], i=i:
                        A[n][l, :, 4 * i:4 * i + 4, :].rearrange("p (c i) f -> p c (i f)", c=2), 2, HALF) for i in range(4)]
                parts.append((s, src, (s, 0)))
            elif s[0][:3] == "out":
                k0 = 4 if s[0] == "out_nsa" else 0
                parts.append((s, [(lambda l, q=q, c0=s[1] * HALF: chunks(A["w_out_2"][l], q, 2, c0, HALF), 2, HALF)
                                  for q in (k0, k0 + 2)], None if k0 else (("out", s[1]), NT - 1)))
            else:
                name = {"in": "w_in_2", "gt": "ffn_w_gate_2", "up": "ffn_w_up_2", "dn": "ffn_w_down_2"}[s[0]]
                halves = [(0, HALF), (HALF, HALF)]
                c0, w = {"in": cols, "dn": halves, "gt": fcols, "up": fcols}[s[0]][s[1]]
                src = [(lambda l, n=name, q=q, c0=c0, w=w: chunks(A[n][l], 2 * q, 2, c0, w), 2, w)
                       for q in range((FC if s[0] == "dn" else KC) // 2)]
                parts.append((s, src, (s, NT - 1)))
        OB = Banks(ctx, nc, "ob", [chip.bank(4 + i) for i in range(4)], [(("out", j), t) for t in range(NT) for j in range(2)])
        shared = {(k, j): (OB, ("out", j), k0, k0 > 0, k0 == 0) for k, k0 in (("out_nsa", 4), ("out_mix", 0)) for j in range(2)}
        W = Weights(ctx, nc, chip, PJ, "w2", parts, plain=[("cmp", 0), ("cmp", 1)], shared=shared)

        tp = [("x", i) for i in range(4)] + [("f", i) for i in range(9)] + [("mv",), ("mw",), ("ma",), ("mg",), ("mz",)]
        tp += [("q", i) for i in range(2)] + [("d", i) for i in range(4)] + [("kn",)]
        tp += [("o", a) for a in range(5)] + [("hd",), ("kc",), ("vc",)]
        tp += [("o", a) for a in range(5, len(GROUPS2))]
        tp += [("bn",), ("kp", 0), ("kp", 1), ("ba", 0), ("ba", 1), ("vt",), ("W",), ("Q",)]
        tp += [("n", 0), ("n", 1)] + [(k, i) for i in range(2) for k in ("U", "I", "D")] + [("Y", 0)]
        tp += [(k, i) for i in range(2, 4) for k in ("U", "I", "D") if (k, i) != ("D", 3)] + [("Y", 1), ("y", 0), ("y", 1)]
        tp += [("x1", t, i) for t in range(NT) for i in range(2)] + [("a", i) for i in range(FC // 2)]
        TP = Banks(ctx, nc, "tp2", [chip.bank(2), chip.bank(3)], tp)
        pair0 = chip.ps[:, 4:6, :].rearrange("p a (b n) -> p (a b) n", b=4)
        pair1 = chip.ps[:, 6:8, :].rearrange("p a (b n) -> p (a b) n", b=4)
        UB = Banks(ctx, nc, "ub", [pair0, pair1], [("g", n) for n in range(LEVELS + 1)] + ["AB", "AK", "RB", "RK"])
        lb = [("X", 0, 0), ("X", 0, 1)]
        for n in range(1, LEVELS):
            lb += [("U", n, 0), ("U", n, 1)] + [(k, n, par) for par in range(2) for k in ("X", "XT") if (k, n) != ("X", LEVELS - 1)]
        LB = Banks(ctx, nc, "lb", [chip.bank(4 + i).rearrange("p (u n) -> p u n", u=4) for i in range(4)],
                   lb + [("P", par) for par in range(2)])
        scb = chip.ps[:, 4:6, :].rearrange("p a (b n) -> p (a b) n", b=2)
        ptb = chip.ps[:, 6:8, :]

        ev = {}

        def E(name):
            if name not in ev:
                ev[name] = Count(ctx, nc, "e_" + name)
            return ev[name]

        act_lane = Lane(ctx, nc, nc.scalar, "act2")
        dve_lane = Lane(ctx, nc, nc.vector, "dve2")
        HEADS = [(par, c, t) for par in range(2) for c in range(2) for t in range(NT)]

        def turned(b, n=2):
            return b[:, 0:n * S].rearrange("p (c t) -> p c t", c=n)

        def both(b):
            return b[:, :].rearrange("p (c t) -> p c t", c=2)

        def keys(g):
            return P * (GROUPS2[g][1] + 1) if GROUPS2[g][0] != "c" else P

        with nc.Fori(0, layers) as l:
          with nc.Block() as block:

            @block.sync
            def _(sp):
                W.load(sp, l, 0, RAW)
                for dst, src in ((vec[:], A["vec2"][l]), (sw[:], A["smallw"][l]), (posT[:], A["pos"][l]),
                                 (w2k[:, :, 0:HD], A["nsa_wk2_2"][l].rearrange("(c p) d -> p c d", p=P)),
                                 (w2k[:, :, HD:P], A["nsa_wk2_2"][l].rearrange("(c p) d -> p c d", p=P)),
                                 (w2v[:], A["nsa_wv2_2"][l].rearrange("(c p) d -> p c d", p=P))):
                    sp.dma_start(dst, src).then_inc(E("small_in").sem, 16)
                W.load(sp, l, RAW, len(W.items))

            @block.gpsimd
            def _(pool):
                W.low(pool)

            @block.tensor
            def _(pe):
                def turn(use, srcs):
                    b = TP.fill(pe, use)
                    for k, src in enumerate(srcs):
                        ins = pe.transpose(b[:, k * P:(k + 1) * P], src, chip.ident[:])
                    TP.full(ins)

                def product(s, hi, lo, apart=0, parts_in=lambda n: None):
                    n_items = W.last[s] - W.first[s] + 1
                    for n in range(n_items - apart):
                        W.multiply(pe, s, n, hi, lo, parts_in=parts_in(n))
                    for t in range(NT):
                        for n in range(n_items - apart, n_items):
                            W.multiply(pe, s, n, hi, lo, [t], parts_in=parts_in(n) if t == 0 else None)

                def by_feature(T):
                    return lambda k, t: T[:, k, t * P:(t + 1) * P]

                for i in range(4):
                    turn(("x", i), [x[:, t, (2 * i + c) * P:(2 * i + c + 1) * P] for c in range(2) for t in range(NT)])
                for j in range(MIXED):
                    product(("in", j), by_feature(xT), by_feature(x_lo), parts_in=lambda n: None if j else (
                        lambda: pe.wait_ge(E("x_high").sem, n + 1), lambda: TP.taken(pe, ("x", n))))
                PJ.drained(pe, (("in", MIXED - 1), 1))
                for i in range(9):
                    w = WIN[2 * i:2 * i + 2]
                    turn(("f", i), [H[:, t, c0:c0 + P] for c0 in w for t in range(NT)])
                product(("in", MIXED), by_feature(xT), by_feature(x_lo))

                def small(use, w, rhs, start=True, stop=True):
                    b = TP.aps[TP.at[use] % 2]
                    for c in range(2):
                        ins = pe.matmul(b[:, c * S:(c + 1) * S], sw[:, w, c * P:(c + 1) * P], rhs, start=start, stop=stop)
                    return ins

                TP.fill(pe, ("mv",))
                pe.wait_ge(E("small_in").sem, 96)
                pe.wait_ge(E("shifted").sem, 1)
                TP.full(small(("mv",), 1, FT[:, F_VR, :]))
                TP.fill(pe, ("mw",))
                pe.wait_ge(E("ranks").sem, 1)
                TP.full(small(("mw",), 2, TM[:, 0, :]))
                TP.fill(pe, ("ma",))
                TP.full(small(("ma",), 3, FT[:, F_WA, :]))
                b = TP.fill(pe, ("mg",))
                pe.wait_ge(E("ranks").sem, 3)
                for c in range(2):
                    for k in range(2):
                        ins = pe.matmul(b[:, c * S:(c + 1) * S], sw[:, 4 + k, c * P:(c + 1) * P], FT[:, F_G0 + k, :],
                                        start=(k == 0), stop=(k == 1))
                TP.full(ins)
                TP.fill(pe, ("mz",))
                TP.full(small(("mz",), 0, FT[:, F_LR, :]))
                for j in range(MIXED + 1, len(cols)):
                    product(("in", j), by_feature(xT), by_feature(x_lo), apart=4 if j == len(cols) - 1 else 0)
                pe.wait_ge(E("roped").sem, 1)
                for i in range(2):
                    turn(("q", i), [H[:, t, NQ + (2 * i + c) * P:NQ + (2 * i + c + 1) * P] for c in range(2) for t in range(NT)])
                pe.wait_ge(E("dup").sem, 1)
                for i in range(4):
                    turn(("d", i), [DD[:, t, 2 * i + c, :, :].rearrange("p a b -> p (a b)") for c in range(2) for t in range(NT)])
                def compress(kv, i):
                    s = ("cmp", kv)
                    b = PJ.fill(pe, (s, 0)) if i == 0 else PJ.aps[PJ.at[(s, 0)] % 2]
                    if i == 0:
                        pe.wait_ge(E("blk").sem, kv + 1)
                    item = W.first[s] + i // 4
                    if i % 4 == 0:
                        W.wait_landed(pe, item)
                    slot = W.raw(item).rearrange("p c (i f) -> p (c i) f", i=2)
                    ins = pe.matmul(b[0:2 * NC, 0:S], BLK[:, kv, i, :], slot[:, i % 4, :], start=(i == 0), stop=(i == 15))
                    if i in (3, 7, 11):
                        ins.then_inc(W.used.sem, 1)
                    if i == 15:
                        PJ.full(ins)

                def hidden():
                    b = TP.fill(pe, ("hd",))
                    pe.wait_ge(E("gelu").sem, 1)
                    for n in range(4):
                        ins = pe.transpose(b[:, n * 2 * NC:(n + 1) * 2 * NC], ge[0][0:2 * NC, n // 2, (n % 2) * P:(n % 2) * P + P],
                                           chip.ident[0:2 * NC, 0:2 * NC])
                    TP.full(ins)

                def compressed():
                    b = TP.fill(pe, ("kc",))
                    TP.taken(pe, ("hd",))
                    for f in range(2):
                        ins = pe.matmul(b[:, 0:2 * P], w2k[:, f, :], HID[:, 0, f, :], start=(f == 0), stop=(f == 1))
                    TP.full(ins)
                    b = TP.fill(pe, ("vc",))
                    for g in range(2):
                        for f in range(2):
                            ins = pe.matmul(b[:, g * HD:(g + 1) * HD], HID[:, 1, f, g * P:(g + 1) * P], w2v[:, f, :],
                                            start=(f == 0), stop=(f == 1))
                    TP.full(ins)

                def scores(a):
                    kind, t, g = GROUPS2[a]
                    if a >= 1:
                        pe.wait_ge(E("sc_read").sem, a)
                    if kind == "c":
                        TP.drained(pe, ("vc",))
                    for s in (0, 2, 1, 3):
                        h = 4 * g + HEAD[s]
                        r = slice(64 * (h % 2), 64 * (h % 2) + 64)
                        k = {"s": KT[r, g], "w": KT[r, 2 + g], "c": kcT[r, g]}[kind]
                        ins = pe.matmul(scb[:, s, 0:keys(a)], qT[r, h // 2, t * P:(t + 1) * P], k[:, 0:keys(a)],
                                        start=True, stop=True)
                    ins.then_inc(E("sc_full").sem, 1)

                def turn_p(a):
                    pe.wait_ge(E("p").sem, a + 1)
                    if a >= 1:
                        pe.wait_ge(E("pt").sem, a)
                    for kt in range(keys(a) // P):
                        for s in range(4):
                            ins = pe.transpose(ptb[:, kt, s * P:(s + 1) * P], sm[:, a % 2, s, kt * P:(kt + 1) * P], chip.ident[:])
                    ins.then_inc(E("pt_full").sem, 1)

                def values(a):
                    kind, t, g = GROUPS2[a]
                    b = TP.fill(pe, ("o", a))
                    pe.wait_ge(E("pt").sem, a + 1)
                    n = keys(a) // P
                    for s in range(4):
                        for kt in range(n):
                            v = vcp[:, g, :] if kind == "c" else H[:, kt, {"s": NVS, "w": NVW}[kind] + g * HD:][:, 0:HD]
                            ins = pe.matmul(b[:, s * HD:(s + 1) * HD], PT[:, a % 2, kt, s * P:(s + 1) * P], v,
                                            start=(kt == 0), stop=(kt == n - 1))
                    TP.full(ins)

                TP.drained(pe, ("d", 3))
                G = len(GROUPS2)
                for k in range(G + 2):
                    if k == 2:
                        b = TP.fill(pe, ("kn",))
                        pe.wait_ge(E("ksq").sem, 1)
                        TP.full(pe.matmul(b[:, :], chip.ones[:], TM2.rearrange("p c s -> p (c s)"), start=True, stop=True))
                    if k == 7:
                        hidden()
                    if k < G:
                        scores(k)
                    for n in range(7 * k, min(7 * k + 7, 32)):
                        compress(n // 16, n % 16)
                    if 0 <= k - 1 < G:
                        turn_p(k - 1)
                    if k == 7:
                        compressed()
                    if 0 <= k - 2 < G:
                        values(k - 2)

                b = TP.fill(pe, ("bn",))
                pe.wait_ge(E("rkr").sem, 1)
                TP.full(pe.matmul(b[:, :], chip.ones[:], TM2.rearrange("p c s -> p (c s)"), start=True, stop=True))

                def units(use, L, R):
                    b = UB.fill(pe, use)
                    for n in range(4):
                        for par in range(2):
                            r = slice(64 * par, 64 * par + 64)
                            c, t = n // 2, n % 2
                            ins = pe.matmul(b[:, 4 * par + n, :], L[r, c, t * P:(t + 1) * P], R[r, c, t * P:(t + 1) * P],
                                            start=True, stop=True)
                    UB.full(ins)

                units(("g", 0), FT[:, F_GK:F_GK + 2, :], FT[:, F_GQ:F_GQ + 2, :])
                for n in range(LEVELS):
                    pe.wait_ge(E("pn").sem, n + 1)
                    units(("g", n + 1), PN[:, n % 2], PN[:, n % 2])
                pe.wait_ge(E("tilde").sem, 1)
                units("AB", BB, KK)
                units("AK", FT[:, F_K:F_K + 2, :], KK)
                units("RB", BB, FT[:, F_R:F_R + 2, :])
                units("RK", FT[:, F_K:F_K + 2, :], FT[:, F_R:F_R + 2, :])
                for t in range(NT):
                    turn(("kp", t), [KP[:, c, t * P:(t + 1) * P] for c in range(4)])
                for t in range(NT):
                    turn(("ba", t), [BP[:, 0, t * P:(t + 1) * P], BP[:, 1, t * P:(t + 1) * P],
                                     KK[:, 0, t * P:(t + 1) * P], KK[:, 1, t * P:(t + 1) * P]])
                turn(("vt",), [FT[:, F_V + c, t * P:(t + 1) * P] for t in range(NT) for c in range(2)])
                b = TP.fill(pe, ("W",))
                TP.drained(pe, ("vt",))
                for u, (par, c, t) in enumerate(HEADS):
                    ins = pe.matmul(b[:, u * CH:(u + 1) * CH], AK[:, u, :], VT[:, t, (2 * c + par) * HD:(2 * c + par + 1) * HD],
                                    start=True, stop=True)
                TP.full(ins)

                def four(use, par, L, R):
                    b = LB.fill(pe, use)
                    for u in range(4):
                        ins = pe.matmul(b[:, u, :], L[:, 4 * par + u, :], R[:, 4 * par + u, :], start=True, stop=True)
                    LB.full(ins)

                UB.drained(pe, "RK")
                pe.wait_ge(E("bt").sem, 1)
                for par in range(2):
                    b = LB.fill(pe, ("X", 0, par))
                    for u in range(4):
                        ins = pe.transpose(b[:, u, :], BT[:, 4 * par + u, :], chip.ident[:])
                    LB.full(ins)
                for n in range(1, LEVELS):
                    pe.wait_ge(E("bt").sem, n + 1)
                    for par in range(2):
                        LB.taken(pe, ("X", n - 1, par))
                        four(("U", n, par), par, BT, T_)
                    for par in range(2):
                        LB.taken(pe, ("U", n, par))
                        if n == 1:
                            pe.wait_ge(E("tt1").sem, 1)
                        else:
                            LB.taken(pe, ("XT", n - 1, par))
                        if n < LEVELS - 1:
                            four(("X", n, par), par, TT, UU)
                        four(("XT", n, par), par, UU, TT)
                for par in range(2):
                    LB.taken(pe, ("XT", LEVELS - 1, par))
                b = TP.fill(pe, ("Q",))
                TP.drained(pe, ("W",))
                for u in range(8):
                    ins = pe.matmul(b[:, u * CH:(u + 1) * CH], TT[:, u, :], Wb[:, u, :], start=True, stop=True)
                TP.full(ins)
                for par in range(2):
                    b = LB.fill(pe, ("P", par))
                    for n in range(4):
                        c, t = n // 2, n % 2
                        ins = pe.matmul(b[:, n, :], BAt[:, t, 256 + c * P:256 + (c + 1) * P], TT[:, 4 * par + n, :],
                                        start=True, stop=True)
                    LB.full(ins)
                LB.drained(pe, ("P", 1))
                for i in range(2):
                    turn(("n", i), [NS[:, t, (2 * i + c) * P:(2 * i + c + 1) * P] for c in range(2) for t in range(NT)])

                def out_nsa(n):
                    TP.taken(pe, ("n", 1))
                    W.multiply(pe, ("out_nsa", n // 2), n % 2, by_feature(OT), by_feature(x_lo))

                def outputs(t):
                    b = TP.fill(pe, ("Y", t))
                    TP.taken(pe, ("U", 2 * t + 1))
                    for c in range(2):
                        for par in range(2):
                            u, h = 4 * par + 2 * c + t, 2 * c + par
                            pe.matmul(b[:, h * HD:(h + 1) * HD], SC[:, u, :], H[:, t, GV + h * HD:GV + (h + 1) * HD],
                                      start=True, stop=True)
                            o = b[:, 256 + h * HD:256 + (h + 1) * HD]
                            pe.matmul(o, RK[:, u, :], VT[:, t, h * HD:(h + 1) * HD], start=True, stop=False)
                            ins = pe.matmul(o, RB[:, u, :], Us[:, t, h * HD:(h + 1) * HD], start=False, stop=True)
                    TP.full(ins)

                for i in range(4):
                    t, r = i // 2, slice(64 * (i % 2), 64 * (i % 2) + 64)
                    pe.wait_ge(E("state").sem, 1)
                    if i:
                        TP.drained(pe, ("D", i - 1))
                    b = TP.fill(pe, ("U", i))
                    for c in range(2):
                        ins = pe.matmul(b[:, c * P:(c + 1) * P], PTf[:, c, t * P:(t + 1) * P], SP[:, 2 + c, :], start=True, stop=True)
                    TP.full(ins)
                    b = TP.fill(pe, ("I", i))
                    for c in range(4):
                        q = GQt[:, c] if c < 2 else FT[:, F_R + c - 2]
                        ins = pe.matmul(b[:, c * P:(c + 1) * P], q[:, t * P:(t + 1) * P], SP[:, c, :], start=True, stop=True)
                    TP.full(ins)
                    if i == 3:
                        break
                    b = TP.fill(pe, ("D", i))
                    TP.drained(pe, ("U", i))
                    for c in range(4):
                        v = H[r, t, GV + c * P:GV + (c + 1) * P] if c < 2 else VT[r, t, (c - 2) * P:(c - 1) * P]
                        ins = pe.matmul(b[:, c * P:(c + 1) * P], KPt[r, t, c * P:(c + 1) * P], v, start=True, stop=(c < 2))
                        if c >= 2:
                            ins = pe.matmul(b[:, c * P:(c + 1) * P], BAt[r, t, (c - 2) * P:(c - 1) * P],
                                            Us[r, t, (c - 2) * P:(c - 1) * P], start=False, stop=True)
                    TP.full(ins)
                    out_nsa(i) if i < 2 else None
                    if i == 1:
                        outputs(0)
                outputs(1)
                for t in range(NT):
                    out_nsa(2 + t)
                    pe.wait_ge(E("normed").sem, t + 1)
                    turn(("y", t), [Y[:, t, c * P:(c + 1) * P] for c in range(4)])
                for t in range(NT):
                    pe.wait_ge(E("mixed").sem, t + 1)
                    for j in range(2):
                        for n in range(2):
                            W.multiply(pe, ("out_mix", j), n, by_feature(OT), by_feature(x_lo), [t])
                for t in range(NT):
                    pe.wait_ge(E("x1").sem, t + 1)
                    for i in range(2):
                        turn(("x1", t, i), [x[:, t, (4 * i + c) * P:(4 * i + c + 1) * P] for c in range(4)])
                    for n in range(KC // 2):
                        W.multiply(pe, ("gt", 0), n, by_feature(xT), by_feature(x1_lo), [t], parts_in=(
                            lambda: pe.wait_ge(E("x1_high").sem, 2 * t + n // 2 + 1), lambda: TP.taken(pe, ("x1", t, n // 2))))

                def turn_acts(j):
                    c0, w = fcols[j]
                    PJ.drained(pe, (("up", j), 1))
                    for i in range(c0 // 256, (c0 + w) // 256):
                        turn(("a", i), [H[:, t, (2 * i + c) * P:(2 * i + c + 1) * P] for c in range(2) for t in range(NT)])

                for j in range(6):
                    if j >= 1:
                        product(("gt", j), by_feature(xT), by_feature(x1_lo))
                        turn_acts(j - 1)
                    product(("up", j), by_feature(xT), by_feature(x1_lo))
                turn_acts(5)
                turned_before = FC // 2 - 2
                TP.taken(pe, ("a", turned_before - 1))
                for j in range(2):
                    product(("dn", j), by_feature(aT), lambda k, t: H_lo[:, t, k * P:(k + 1) * P], apart=3 * j,
                            parts_in=lambda n: None if j or n < turned_before else (
                                lambda: pe.wait_ge(E("a_high").sem, n + 1), lambda: TP.taken(pe, ("a", n))))

            @block.scalar
            def _(act):
                lane = act_lane
                sc = nc.scalar
                for i in range(4):
                    b = TP.read(act, ("x", i))
                    lane.done(sc.copy(xT[:, 2 * i:2 * i + 2, :], turned(b)), E("x_high"))
                    if i >= 1:
                        W.high(act, i - 1)

                def pace(s, read=lambda: None):
                    for i in range(W.first[s], W.last[s] + 1):
                        W.high(act, i + SPLIT - 1)
                    read()

                def take_in(j):
                    for t in range(NT):
                        b = PJ.read(act, (("in", j), t))
                        c0, w = cols[j]
                        PJ.empty(lane, sc.copy(H[:, t, c0:c0 + w], b[:, 0:w]), (("in", j), t))

                W.high(act, SPLIT - 2)
                for j in range(MIXED):
                    pace(("in", j), lambda: take_in(j))
                for i in range(9):
                    b = TP.read(act, ("f", i))
                    n = len(WIN[2 * i:2 * i + 2])
                    TP.empty(lane, sc.activation(FT[:, 2 * i:2 * i + n, :], turned(b, n), ACT.Copy,
                                                 scale=0.125 if i == 0 else 1.0), ("f", i))
                pace(("in", MIXED), lambda: take_in(MIXED))
                act.wait_ge(E("shifted").sem, 1)
                lane.done(sc.activation(TM[:, 0, :], FT[:, F_WA, :], ACT.Tanh), E("ranks"))
                for k in range(2):
                    lane.done(sc.activation(FT[:, F_G0 + k, :], FT[:, F_G0 + k, :], ACT.Sigmoid), E("ranks"))
                b = TP.read(act, ("mv",))
                for c in range(2):
                    ins = sc.activation(BON[:, c, :], b[:, c * S:(c + 1) * S], ACT.Sigmoid, bias=vec[:, V_V0 + c:V_V0 + c + 1])
                    lane.done(ins) if c == 0 else TP.empty(lane, ins, ("mv",))
                b = TP.read(act, ("mw",))
                for c in range(2):
                    ins = sc.activation(LD[:, 2 + c, :], b[:, c * S:(c + 1) * S], ACT.Sigmoid, bias=vec[:, V_W0 + c:V_W0 + c + 1])
                    lane.done(ins) if c == 0 else TP.empty(lane, ins, ("mw",))
                b = TP.read(act, ("ma",))
                for c in range(2):
                    ins = sc.activation(IC[:, c, :], b[:, c * S:(c + 1) * S], ACT.Sigmoid, bias=vec[:, V_A0 + c:V_A0 + c + 1])
                    lane.done(ins) if c == 0 else TP.empty(lane, ins, ("ma",))
                b = TP.read(act, ("mg",))
                TP.empty(lane, sc.copy(GT[:, :, :], both(b)), ("mg",))
                lane.done(sc.activation(EN[:, :, :], FT[:, F_GG:F_GG + 2, :], ACT.Sigmoid), E("gg_sig"))
                for j in range(MIXED + 1, len(cols)):
                    pace(("in", j), lambda: take_in(j))
                for i in range(2):
                    b = TP.read(act, ("q", i))
                    TP.empty(lane, sc.copy(qT[:, 2 * i:2 * i + 2, :], turned(b)), ("q", i))
                act.wait_ge(E("az").sem, 1)
                lane.done(sc.activation(GQt[:, :, :], GQt[:, :, :], ACT.Exp, scale=-1.0))
                lane.settle()
                lane.done(sc.activation(GQt[:, :, :], GQt[:, :, :], ACT.Ln, bias=1.0), E("lnz"))
                for i in range(4):
                    b = TP.read(act, ("d", i))
                    TP.empty(lane, sc.copy(KT[:, 2 * i:2 * i + 2, :], turned(b)), ("d", i))
                lane.settle()
                lane.done(sc.activation(gate[:, :, :], H[:, :, NGT:NGT + 24], ACT.Sigmoid), E("gate"))
                G = len(GROUPS2)
                for a in range(G + 1):
                    if a == 0:
                        act.wait_ge(E("cum").sem, 1)
                        lane.done(sc.activation(EP[:, :, :], CUM[:, :, :], ACT.Exp), E("exps"))
                        lane.done(sc.activation(EE[:, :, :], EE[:, :, :], ACT.Exp), E("exps"))
                    if a == 1:
                        lane.done(sc.activation(EN[:, :, :], CUM[:, 2:4, :], ACT.Exp, scale=-1.0), E("exps"))
                        lane.done(sc.activation(EM[:, :, :], EM[:, :, :], ACT.Exp), E("exps"))
                    if a == 6:
                        act.wait_ge(E("ge_in").sem, 1)
                        lane.done(sc.activation(ge[2][0:2 * NC], ge[1][0:2 * NC], ACT.Sigmoid, scale=2.0 * 0.7978845608028654), E("ge_sig"))
                    if a == 2:
                        b = TP.read(act, ("kn",))
                        TP.empty(lane, sc.activation(TM, both(b), ACT.Sqrt), ("kn",))
                    if a >= 1:
                        act.wait_ge(E("pt_full").sem, a)
                        if a - 1 >= 2:
                            act.wait_ge(TP.filled.sem, TP.at[("o", a - 3)] + 1)
                        n = keys(a - 1) // P
                        lane.done(sc.copy(PT[:, (a - 1) % 2, 0:n, :], ptb[:, 0:n, :]), E("pt"))
                    if a < G:
                        act.wait_ge(E("mx").sem, a + 1)
                        for s in range(4):
                            p = sm[:, a % 2, s, 0:keys(a)]
                            lane.done(sc.activation(p, p, ACT.Exp, bias=nmx[:, a, s:s + 1], accum_out=den[:, a, s:s + 1]),
                                      E("p") if s == 3 else None)
                for n in range(LEVELS):
                    act.wait_ge(E("pd").sem, n + 1)
                    lane.done(sc.activation(PN[:, n % 2], PN[:, n % 2], ACT.Exp), E("pe"))
                for use, dst in ((("kp", 0), KPt[:, 0]), (("kp", 1), KPt[:, 1]), (("ba", 0), BAt[:, 0]), (("ba", 1), BAt[:, 1]),
                                 (("vt",), VT)):
                    b = TP.read(act, use)
                    TP.empty(lane, sc.copy(dst, both(b) if use == ("vt",) else b[:, :]), use)
                b = TP.read(act, ("W",))
                TP.empty(lane, sc.copy(Wb[:, :, :].rearrange("p u d -> p (u d)"), b[:, :]), ("W",))
                for n in range(1, LEVELS):
                    for par in range(2):
                        b = LB.read(act, ("U", n, par))
                        if n >= 2:
                            act.wait_ge(LB.filled.sem, LB.at[("XT", n - 1, par)] + 1)
                        LB.empty(lane, sc.copy(UU[:, 4 * par:4 * par + 4, :], b), ("U", n, par))
                b = TP.read(act, ("Q",))
                TP.empty(lane, sc.copy(Qb[:, :, :].rearrange("p u d -> p (u d)"), b[:, :]), ("Q",))
                for par in range(2):
                    r = slice(64 * par, 64 * par + 64)
                    b = LB.read(act, ("P", par))
                    LB.empty(lane, sc.copy(PTf[r, :, :].rearrange("p c s -> p (c s)"), b[r, :, :].rearrange("p u n -> p (u n)")), ("P", par))
                for k, n in enumerate(("ln1_w_2", "ln1_b_2", "ln2_w_2", "ln2_b_2")):
                    act.dma_start(ln[:, k, :], A[n][l].partition_broadcast(P)).then_inc(E("ln_in").sem, 16)
                for i in range(2):
                    b = TP.read(act, ("n", i))
                    lane.done(sc.copy(OT[:, 4 + 2 * i:6 + 2 * i, :], turned(b)), E("n_high"))
                W.high(act, W.first[("out_nsa", 0)] + SPLIT - 1)
                for i in range(4):
                    r = slice(64 * (i % 2), 64 * (i % 2) + 64)
                    b = TP.read(act, ("I", i))
                    TP.empty(lane, sc.copy(Y[r, i // 2, :], b[r, :]), ("I", i))
                    if i in (1, 2):
                        W.high(act, W.first[("out_nsa", 0)] + SPLIT - 1 + i)
                for t in range(NT):
                    act.wait_ge(E("var").sem, t + 1)
                    half = slice(8 * t, 8 * t + 8)
                    lane.done(sc.activation(st[:, 2, half], st[:, 1, half], ACT.Sqrt), E("sd"))
                for t in range(NT):
                    b = TP.read(act, ("y", t))
                    for c in range(4):
                        ins = sc.activation(VAL[:, c, t * P:(t + 1) * P], b[:, c * P:(c + 1) * P], ACT.Identity,
                                            scale=vec[:, V_LNW + c:V_LNW + c + 1], bias=vec[:, V_LNB + c:V_LNB + c + 1])
                        lane.done(ins) if c < 3 else TP.empty(lane, ins, ("y", t))
                    W.high(act, W.first[("out_mix", 1)] + t)
                for k in range(2):
                    first_gate = W.first[("gt", 0)]

                    def root(t):
                        act.wait_ge(E("lnv").sem, 2 * k + t + 1)
                        lane.done(sc.activation(mv[:, t, 1:2], mv[:, t, 1:2], ACT.Sqrt), E("lns"))

                    def x1_high(t):
                        for i in range(2):
                            b = TP.read(act, ("x1", t, i))
                            lane.done(sc.copy(xT[:, 4 * i:4 * i + 4, t * P:(t + 1) * P], b.rearrange("p (c n) -> p c n", c=4)),
                                      E("x1_high"))

                    if k == 0:
                        W.high(act, first_gate)
                    root(0)
                    if k == 0:
                        W.high(act, first_gate + 3)
                        x1_high(0)
                    root(1)
                    if k == 0:
                        x1_high(1)

                        def turned_acts(j):
                            c0, w = fcols[j]
                            for i in range(c0 // 256, (c0 + w) // 256):
                                b = TP.read(act, ("a", i))
                                lane.done(sc.copy(aT[:, 2 * i:2 * i + 2, :], turned(b)), E("a_high"))

                        def sigmoids(j, tiles=range(NT)):
                            for t in tiles:
                                b = PJ.read(act, (("gt", j), t))
                                if j >= 1:
                                    PJ.drained(act, (("up", j - 1), t))
                                w = fcols[j][1]
                                lane.done(sc.activation(sg[:, t, 0:w], b[:, 0:w], ACT.Sigmoid), E("sig"))
                            if j >= 1:
                                turned_acts(j - 1)
                        sigmoids(0, [0])
                        for j in range(6):
                            pace(("gt", j), lambda: sigmoids(j, [1] if j == 0 else range(NT)))
                            pace(("up", j))
                        turned_acts(5)
                        for j in range(2):
                            pace(("dn", j))

            @block.vector
            def _(dve):
                lane = dve_lane
                v = nc.vector

                def tt(out, a, b, op, e=None, settle=True):
                    if settle:
                        lane.settle()
                    lane.done(v.tensor_tensor(out, a, b, op), e)

                def ts(out, a, s1, s2, o1, o2=None, e=None, settle=True):
                    if settle:
                        lane.settle()
                    ins = v.tensor_scalar(out, a, s1, s2, o1, o2) if o2 is not None else v.tensor_scalar(out, a, s1, None, o1)
                    lane.done(ins, e)

                def stt(out, a, s, b, o0, o1, e=None, settle=True):
                    if settle:
                        lane.settle()
                    lane.done(v.scalar_tensor_tensor(out=out, in0=a, scalar=s, in1=b, op0=o0, op1=o1), e)

                def low(dst, use, hi, i, e):
                    b = TP.read(dve, use)
                    dve.wait_ge(E(e).sem, i + 1)
                    TP.empty(lane, v.tensor_tensor(dst, turned(b), hi, ALU.subtract), use)

                for i in range(4):
                    low(x_lo[:, 2 * i:2 * i + 2, :], ("x", i), xT[:, 2 * i:2 * i + 2, :], i, "x_high")
                ra, rb = (u.rearrange("p a s -> p (a s)").rearrange("p (t h d) -> p t h d", t=NT, d=HD) for u in (EP, EE))

                def rope(X, a_, b_, C, Sn, shape, e=None):
                    def bc(w):
                        for _ in shape[1:-1] if len(shape) == 4 else shape[1:-1]:
                            w = w.unsqueeze(len(w.shape) - 1)
                        return w
                    n = len(shape)
                    lo, hi = (slice(None),) * (n - 1) + (slice(0, 32),), (slice(None),) * (n - 1) + (slice(32, 64),)
                    c_, s_ = C, Sn
                    while len(c_.shape) < n:
                        c_, s_ = c_.unsqueeze(len(c_.shape) - 1), s_.unsqueeze(len(s_.shape) - 1)
                    half = shape[:-1] + [32]
                    tt(a_, X, c_.to_broadcast(shape), ALU.mult)
                    tt(b_[lo], X[hi], s_[(slice(None),) * (n - 1) + (slice(0, 32),)].to_broadcast(half), ALU.mult, settle=False)
                    tt(b_[hi], X[lo], s_[(slice(None),) * (n - 1) + (slice(32, 64),)].to_broadcast(half), ALU.mult, settle=False)
                    tt(X, a_, b_, ALU.add, e)

                R10 = FT[:, F_R:F_R + 10, :]
                TP.drained(dve, ("f", 8))
                tt(DL[:, :, 1:S], R10[:, :, 0:S - 1], R10[:, :, 1:S], ALU.subtract)
                ts(DL[:, :, 0:1], R10[:, :, 0:1], -1.0, None, ALU.mult, settle=False)
                lane.settle()
                for c in range(10):
                    last = c == 9
                    stt(R10[:, c, :], DL[:, c, :], vec[:, V_MU + c:V_MU + c + 1], R10[:, c, :], ALU.mult, ALU.add,
                        E("shifted") if last else None, settle=last)
                lane.done(v.memset(HID[:, :, :, :], 0.0))
                PJ.drained(dve, (("in", MIXED), 1))
                rope(H[:, :, NQ:NQ + 512].rearrange("p t (h d) -> p t h d", d=HD), ra, rb,
                     chip.rope2[:, :, 0, :], chip.rope2[:, :, 1, :], [P, NT, 8, HD], E("roped"))
                Vf, Vn = chip.vfirst[:, :, :], FT[:, F_V:F_V + 2, :]
                tt(TM2[:, :, :], Vn, Vf, ALU.subtract)
                stt(Vf, TM2[:, :, :], vec[:, V_FLAG:V_FLAG + 1], Vf, ALU.mult, ALU.add)
                tt(TM2[:, :, :], Vf, Vn, ALU.subtract)
                TP.drained(dve, ("mv",))
                tt(TM2[:, :, :], TM2[:, :, :], BON[:, :, :], ALU.mult)
                tt(Vn, Vn, TM2[:, :, :], ALU.add)
                b = TP.read(dve, ("mz",))
                for c in range(2):
                    ins = v.tensor_scalar(LD[:, c, :], b[:, c * S:(c + 1) * S], vec[:, V_BA + c:V_BA + c + 1], None, ALU.add)
                    lane.done(ins) if c == 0 else TP.empty(lane, ins, ("mz",))
                stt(GQt[:, :, :], LD[:, 0:2, :], -1.0, LD[:, 0:2, :], ALU.mult, ALU.max, E("az"))
                for c in range(2):
                    ts(KK[:, c, :], FT[:, F_K + c, :], vec[:, V_KK + c:V_KK + c + 1], None, ALU.mult, settle=False)
                tt(TM2[:, :, :], KK[:, :, :], KK[:, :, :], ALU.mult, E("ksq"))
                for t in range(NT):
                    PJ.drained(dve, (("in", len(cols) - 1), t))
                    rope(H[:, t, NKC:NKC + 768].rearrange("p (k o d) -> p k o d", k=3, o=4)[:, :, 0:2, :],
                         ra[:, t, 0:6, :].rearrange("p (k g) d -> p k g d", k=3), rb[:, t, 0:6, :].rearrange("p (k g) d -> p k g d", k=3),
                         chip.rope2[:, t, 0, :], chip.rope2[:, t, 1, :], [P, 3, 2, HD])
                    lane.settle()
                    for n, c0 in enumerate((NKS, NKW, NKC, NVC)):
                        src = H[:, t, c0:c0 + P].rearrange("p (g d) -> p g d", g=2).unsqueeze(2).to_broadcast([P, 2, 2, HD])
                        lane.done(v.tensor_copy(DD[:, t, 2 * n:2 * n + 2, :, :], src), E("dup") if (n, t) == (3, 1) else None)
                dve.wait_ge(E("lnz").sem, 1)
                stt(LD[:, 0:2, :], LD[:, 0:2, :], 0.0, GQt[:, :, :], ALU.min, ALU.subtract)
                ts(LD[:, 0:2, :], LD[:, 0:2, :], 1.0 / 16, None, ALU.mult)
                TP.drained(dve, ("ma",))
                ts(LD[:, 2:4, :], LD[:, 2:4, :], -E_HALF, None, ALU.mult)
                lane.settle()
                for c in range(4):
                    lane.done(v.tensor_tensor_scan(CUM[:, c, :], chip.reset[:, :], LD[:, c, :], 0.0, ALU.mult, ALU.add))
                dve.wait_ge(E("gg_sig").sem, 1)
                tt(FT[:, F_GG:F_GG + 2, :], FT[:, F_GG:F_GG + 2, :], EN[:, :, :], ALU.mult)
                cv = CUM.rearrange("p c (k t) -> p c k t", t=CH)
                tt(EE.rearrange("p c (k t) -> p c k t", t=CH), cv[:, :, :, CH - 1:CH].to_broadcast([P, 4, 4, CH]), cv, ALU.subtract)
                tt(EM[:, :, :], CUM[:, 2:4, :], LD[:, 2:4, :], ALU.subtract, E("cum"))
                TP.drained(dve, ("d", 3))
                dve.wait_ge(E("small_in").sem, 96)
                for kv in range(2):
                    for g in range(2):
                        for hf in range(2):
                            r = slice(64 * hf, 64 * hf + 64)
                            src = KT[r, 4 + 2 * kv + g, :]
                            src = src[:, 16 * hf:16 * hf + 16 * NC].rearrange("p (c i) -> p i c", i=16)
                            last = (g, hf) == (1, 1)
                            tt(BLK[r, kv, :, g * NC:(g + 1) * NC], src, posT[r, kv, :].unsqueeze(2).to_broadcast([64, 16, NC]),
                               ALU.add, E("blk") if last else None, settle=last)
                def output(a):
                    kind, t, g = GROUPS2[a]
                    b = TP.read(dve, ("o", a))
                    dve.wait_ge(E("p").sem, a + 1)
                    f = fac[:, a, :].rearrange("p (b a) -> p b a", a=2)
                    gt = gate[:, t, :].rearrange("p (g a b k) -> p g b a k", g=2, a=2, b=2)[:, g, :, :, "csw".index(kind)]
                    lane.settle()
                    lane.done(v.reciprocal(fac[:, a, :], den[:, a, :]))
                    tt(f, f, gt, ALU.mult)
                    if kind == "c":
                        ts(fac[:, a, :], fac[:, a, :], chip.rowv[:, t:t + 1], None, ALU.mult)
                    lane.settle()
                    dst = NS[:, t, g * 256:(g + 1) * 256]
                    out = dst if kind == "s" else part_out
                    TP.empty(lane, v.tensor_tensor(out.rearrange("p (a b d) -> p b a d", a=2, b=2),
                                                   b[:, 0:256].rearrange("p (b a d) -> p b a d", a=2, b=2),
                                                   f.unsqueeze(3).to_broadcast([P, 2, 2, HD]), ALU.mult), ("o", a))
                    if kind != "s":
                        tt(dst, dst, part_out, ALU.add)

                Kn, Rn = FT[:, F_K:F_K + 2, :], FT[:, F_R:F_R + 2, :]

                def hidden():
                    b = TP.read(dve, ("hd",))
                    for kv in range(2):
                        ins = v.tensor_copy(HID[:, kv, :, :].rearrange("p f (g n) -> p f g n", g=2)[:, :, :, 0:NC],
                                            b[:, kv * 4 * NC:(kv + 1) * 4 * NC].rearrange("p (f g n) -> p f g n", f=2, g=2))
                        lane.done(ins) if kv == 0 else TP.empty(lane, ins, ("hd",))

                def compressed():
                    b = TP.read(dve, ("kc",))
                    TP.empty(lane, v.tensor_copy(H[:, 0, 0:S], b[:, 0:2 * P]), ("kc",))
                    b = TP.read(dve, ("vc",))
                    TP.empty(lane, v.tensor_copy(H[:, 1, 0:P], b[:, 0:2 * HD]), ("vc",))

                def keys_mixed():
                    for c in range(2):
                        ts(BB[:, c, :], IC[:, c, :], 1.0, vec[:, V_KA + c:V_KA + c + 1], ALU.subtract, ALU.mult, settle=False)
                    stt(Kn, BB[:, :, :], 1.0, Kn, ALU.add, ALU.mult)

                blocks = slice(0, 2 * NC)

                def gelu_in():
                    for kv in range(2):
                        b = PJ.read(dve, (("cmp", kv), 0))
                        PJ.empty(lane, v.tensor_copy(ge[0][blocks, kv, :], b[blocks, 0:S]), (("cmp", kv), 0))
                    tt(ge[1][blocks], ge[0][blocks], ge[0][blocks], ALU.mult)
                    ts(ge[1][blocks], ge[1][blocks], 0.044715, 1.0, ALU.mult, ALU.add)
                    tt(ge[1][blocks], ge[1][blocks], ge[0][blocks], ALU.mult, E("ge_in"))

                def gelu_out():
                    dve.wait_ge(E("ge_sig").sem, 1)
                    tt(ge[0][blocks], ge[0][blocks], ge[2][blocks], ALU.mult, E("gelu"))

                def keys_normalised():
                    TP.drained(dve, ("kn",))
                    ts(TM, TM, 1e-12, None, ALU.max)
                    lane.settle()
                    lane.done(v.reciprocal(TM, TM))
                    tt(KK[:, :, :], KK[:, :, :], TM, ALU.mult)

                def bonus():
                    for c in range(2):
                        stt(TM2[:, c, :], FT[:, F_R + c, :], vec[:, V_RK + c:V_RK + c + 1], FT[:, F_K + c, :], ALU.mult, ALU.mult,
                            E("rkr") if c else None)
                    tt(BB[:, :, :], KK[:, :, :], IC[:, :, :], ALU.mult)

                def to_the_end():
                    dve.wait_ge(E("exps").sem, 4)
                    tt(BP[:, :, :], BB[:, :, :], EE[:, 2:4, :], ALU.mult)
                    tt(KP[:, 0:2, :], FT[:, F_GK:F_GK + 2, :], EE[:, 0:2, :], ALU.mult, settle=False)
                    tt(KP[:, 2:4, :], Kn, EE[:, 2:4, :], ALU.mult, settle=False)

                def from_the_start_1():
                    tt(GQt[:, :, :], FT[:, F_GQ:F_GQ + 2, :], EP[:, 0:2, :], ALU.mult)
                    stt(KK[:, :, :], KK[:, :, :], -1.0, EM[:, :, :], ALU.mult, ALU.mult)

                def from_the_start_2():
                    tt(BB[:, :, :], BB[:, :, :], EN[:, :, :], ALU.mult)
                    tt(Kn, Kn, EN[:, :, :], ALU.mult)
                    tt(Rn, Rn, EP[:, 2:4, :], ALU.mult, E("tilde"))

                with_group = {1: keys_mixed, 3: keys_normalised, 4: bonus, 5: gelu_in, 6: gelu_out, 8: to_the_end,
                              9: from_the_start_1, 10: from_the_start_2}
                G = len(GROUPS2)
                dve.wait_ge(E("gate").sem, 1)
                for k in range(G + 2):
                    if k == 7:
                        hidden()
                    if k < G:
                        kind, t, g = GROUPS2[k]
                        nk = keys(k)
                        dve.wait_ge(E("sc_full").sem, k + 1)
                        if k >= 2:
                            dve.wait_ge(E("pt_full").sem, k - 1)
                        p = sm[:, k % 2, :, 0:nk]
                        bias = (chip.cmpb if kind == "c" else chip.cbias)[:, t, 0:nk].unsqueeze(1).to_broadcast([P, 4, nk])
                        stt(p, scb[:, :, 0:nk], 0.125, bias, ALU.mult, ALU.add, E("sc_read"))
                        lane.settle()
                        lane.done(v.tensor_reduce(nmx[:, k, :], p, AX_X, ALU.max, negate=True), E("mx"))
                    if k == 7:
                        compressed()
                    if k - 2 >= 0:
                        output(k - 2)
                    if k in with_group:
                        with_group[k]()

                def mask(m):
                    return masks[:, m, :].unsqueeze(1).to_broadcast([P, 8, P])

                b = TP.read(dve, ("bn",))
                TP.empty(lane, v.tensor_tensor(BON[:, :, :], both(b), Vn, ALU.mult), ("bn",))

                def level(n, u):
                    w = 1 << n
                    return u.rearrange("p c (k h t) -> p (c k) h t", h=2, t=w)

                def parts(n):
                    w = 1 << n
                    return [level(n, u) for u in (PN[:, n % 2], CUM[:, 0:2, :], FT[:, F_GQ:F_GQ + 2, :], FT[:, F_GK:F_GK + 2, :])]

                def decays(n):
                    w = 1 << n
                    pn, cu, _, _ = parts(n)
                    mid = cu[:, :, 0, w - 1:w].to_broadcast([P, S // w, w])
                    if n >= 2:
                        dve.wait_ge(UB.filled.sem, UB.at[("g", n - 1)] + 1)
                    tt(pn[:, :, 0, :], mid, cu[:, :, 0, :], ALU.subtract)
                    tt(pn[:, :, 1, :], cu[:, :, 1, :], mid, ALU.subtract, E("pd"), settle=False)

                decays(0)
                for n in range(LEVELS + 1):
                    if n < LEVELS:
                        pn, _, q_, k_ = parts(n)
                        dve.wait_ge(E("pe").sem, n + 1)
                        tt(pn[:, :, 0, :], pn[:, :, 0, :], k_[:, :, 0, :], ALU.mult)
                        tt(pn[:, :, 1, :], pn[:, :, 1, :], q_[:, :, 1, :], ALU.mult, E("pn"), settle=False)
                    if n + 1 < LEVELS:
                        decays(n + 1)
                    b = UB.read(dve, ("g", n))
                    lane.settle()
                    if n == 0:
                        UB.empty(lane, v.tensor_tensor(SC[:, :, :], b, mask(M_EYE), ALU.mult), ("g", n))
                    else:
                        UB.empty(lane, v.copy_predicated(SC[:, :, :], mask(n - 1).bitcast(mybir.dt.int32), b), ("g", n))
                for use, dst, m in (("AB", AB, M_STRICT), ("AK", AK, M_STRICT), ("RB", RB, M_INCL), ("RK", RK, M_INCL)):
                    b = UB.read(dve, use)
                    UB.empty(lane, v.tensor_tensor(dst[:, :, :], b, mask(m), ALU.mult), use)
                    if use == "AB":
                        tt(BT[:, :, :], AB[:, :, :], mask(0), ALU.mult, E("bt"))
                tt(TT[:, :, :], BT[:, :, :], chip.ident[:].unsqueeze(1).to_broadcast([P, 8, P]), ALU.add, E("tt1"))
                for n in range(LEVELS):
                    if n + 1 < LEVELS:
                        dve.wait_ge(LB.filled.sem, LB.at[("U", n, 1) if n else ("X", 0, 1)] + 1)
                        tt(BT[:, :, :], AB[:, :, :], mask(n + 1), ALU.mult, E("bt"))
                    for par in range(2):
                        four = slice(4 * par, 4 * par + 4)
                        if n < LEVELS - 1:
                            b = LB.read(dve, ("X", n, par))
                            lane.settle()
                            LB.empty(lane, v.tensor_tensor(T_[:, four, :], b, T_[:, four, :] if n else
                                                           chip.ident[:].unsqueeze(1).to_broadcast([P, 4, P]), ALU.add), ("X", n, par))
                        if n:
                            b = LB.read(dve, ("XT", n, par))
                            lane.settle()
                            LB.empty(lane, v.tensor_tensor(TT[:, four, :], b, TT[:, four, :], ALU.add), ("XT", n, par))
                lane.settle()
                lane.done(v.memset(SP[:, :, :], 0.0), E("state"))
                for i in range(2):
                    low(x_lo[:, 4 + 2 * i:6 + 2 * i, :], ("n", i), OT[:, 4 + 2 * i:6 + 2 * i, :], i, "n_high")

                def norm(t):
                    yv = Y[:, t, :].rearrange("p (h d) -> p h d", d=HD)
                    sv = CUM[:, 2 * t:2 * t + 2, :].rearrange("p m (h d) -> p (m h) d", d=HD)
                    mean, var, sd = (st[:, n, 8 * t:8 * t + 8] for n in (0, 1, 2))
                    return yv, sv, mean, var, sd

                def centre(t):
                    b = TP.read(dve, ("Y", t))
                    TP.taken(dve, ("I", 2 * t + 1))
                    lane.settle()
                    TP.empty(lane, v.tensor_tensor(Y[:, t, :], b[:, :], Y[:, t, :], ALU.add), ("Y", t))
                    yv, _, mean, _, _ = norm(t)
                    lane.settle()
                    lane.done(v.tensor_reduce(mean, yv, AX_X, ALU.add))
                    ts(mean, mean, 1.0 / HD, None, ALU.mult)
                    tt(yv, yv, mean.unsqueeze(2).to_broadcast([P, 8, HD]), ALU.subtract)

                def scale(t):
                    yv, sv, inv, var, sd = norm(t)
                    tt(sv, yv, yv, ALU.mult)
                    lane.settle()
                    lane.done(v.tensor_reduce(var, sv, AX_X, ALU.add))
                    for m, eps in ((0, LN_EPS), (1, RWKV_GN_EPS)):
                        ts(var[:, 4 * m:4 * m + 4], var[:, 4 * m:4 * m + 4], 1.0 / HD, eps, ALU.mult, ALU.add,
                           E("var") if m else None, settle=m == 0)
                    dve.wait_ge(E("sd").sem, t + 1)
                    lane.settle()
                    lane.done(v.reciprocal(inv, sd))
                    tt(yv, yv, inv.unsqueeze(2).to_broadcast([P, 8, HD]), ALU.mult, E("normed"))

                def mixed(t):
                    n = slice(t * P, (t + 1) * P)
                    TP.taken(dve, ("y", t))
                    tt(VAL[:, 0:2, n], VAL[:, 0:2, n], FT[:, F_GG:F_GG + 2, n], ALU.mult)
                    tt(VAL[:, 2:4, n], VAL[:, 2:4, n], BON[:, :, n], ALU.add, settle=False)
                    tt(VAL[:, 2:4, n], VAL[:, 2:4, n], GT[:, :, n], ALU.mult)
                    lane.settle()
                    lane.done(v.tensor_copy(OT[:, 0:4, n], VAL[:, :, n]))
                    tt(x_lo[:, 0:4, n], VAL[:, :, n], OT[:, 0:4, n], ALU.subtract, E("mixed"))

                for i in range(4):
                    t, r = i // 2, slice(64 * (i % 2), 64 * (i % 2) + 64)
                    b = TP.read(dve, ("U", i))
                    TP.drained(dve, ("Q",)) if i == 0 else None
                    q_ = Qb.rearrange("p (a c t) d -> p c a t d", a=2, c=2)[r, :, :, t, :]
                    lane.settle()
                    TP.empty(lane, v.tensor_tensor(Us[r, t, :].rearrange("p (c a d) -> p c a d", c=2, a=2),
                                                   b[r, 0:256].rearrange("p (c a d) -> p c a d", c=2, a=2), q_, ALU.add), ("U", i))
                    if i < 3:
                        b = TP.read(dve, ("D", i))
                        for hf in range(2):
                            h = slice(64 * hf, 64 * hf + 64)
                            tt(SP[h, :, h], SP[h, :, h], EP[h, :, i * CH + CH - 1:i * CH + CH].to_broadcast([64, 4, 64]), ALU.mult,
                               settle=False)
                        lane.settle()
                        for hf in range(2):
                            h = slice(64 * hf, 64 * hf + 64)
                            ins = v.tensor_tensor(SP[h, :, h], b.rearrange("p (c n) -> p c n", c=4)[h, :, h], SP[h, :, h], ALU.add)
                            lane.done(ins) if hf == 0 else TP.empty(lane, ins, ("D", i))
                    if i == 1:
                        centre(0)
                scale(0)
                centre(1)
                scale(1)
                mixed(0)
                mixed(1)

                def residual(banks, s, j, t):
                    b = banks.read(dve, ((s, j), t))
                    xs = x[:, t, j * HALF:(j + 1) * HALF]
                    banks.empty(lane, v.scalar_tensor_tensor(out=xs, in0=xs, scalar=ALPHA, in1=b[:, :],
                                                             op0=ALU.mult, op1=ALU.add), ((s, j), t))
                    lane.settle()
                    lane.done(v.bn_stats(bn[:, t, j, :], xs))

                def layer_norm(k, t):
                    lane.settle()
                    lane.done(v.bn_aggr(mv[:, t, :], bn[:, t, :, :].rearrange("p a b -> p (a b)")))
                    ts(mv[:, t, 1:2], mv[:, t, 1:2], LN_EPS, None, ALU.add, e=E("lnv"))
                    dve.wait_ge(E("ln_in").sem, 64)
                    stt(x[:, t, :], x[:, t, :], mv[:, t, 0:1], ln[:, 2 * k, :], ALU.subtract, ALU.mult, settle=False)
                    dve.wait_ge(E("lns").sem, 2 * k + t + 1)
                    lane.done(v.reciprocal(mv[:, t, 1:2], mv[:, t, 1:2]))
                    stt(x[:, t, :], x[:, t, :], mv[:, t, 1:2], ln[:, 2 * k + 1, :], ALU.mult, ALU.add, E("x1") if k == 0 else None)

                def x1_low_part(t):
                    for i in range(2):
                        b = TP.read(dve, ("x1", t, i))
                        dve.wait_ge(E("x1_high").sem, 2 * t + i + 1)
                        n = (slice(None), slice(4 * i, 4 * i + 4), slice(t * P, (t + 1) * P))
                        TP.empty(lane, v.tensor_tensor(x1_lo[n], b.rearrange("p (c n) -> p c n", c=4), xT[n], ALU.subtract), ("x1", t, i))

                residual(OB, "out", 0, 0)
                residual(OB, "out", 1, 0)
                layer_norm(0, 0)
                residual(OB, "out", 0, 1)
                x1_low_part(0)
                residual(OB, "out", 1, 1)
                layer_norm(0, 1)
                x1_low_part(1)

                def low_acts(j):
                    c0, w = fcols[j]
                    for i in range(c0 // 256, (c0 + w) // 256):
                        b = TP.read(dve, ("a", i))
                        dve.wait_ge(E("a_high").sem, i + 1)
                        TP.empty(lane, v.tensor_tensor(
                            H_lo[:, :, 2 * i * P:(2 * i + 2) * P].rearrange("p t (c n) -> p c t n", c=2),
                            turned(b).rearrange("p c (t n) -> p c t n", t=NT),
                            aT[:, 2 * i:2 * i + 2, :].rearrange("p c (t n) -> p c t n", t=NT), ALU.subtract), ("a", i))

                for j in range(6):
                    c0, w = fcols[j]
                    for t in range(NT):
                        b = PJ.read(dve, (("gt", j), t))
                        dve.wait_ge(E("sig").sem, 2 * j + t + 1)
                        PJ.empty(lane, v.tensor_tensor(sg[:, t, 0:w], b[:, 0:w], sg[:, t, 0:w], ALU.mult), (("gt", j), t))
                    if j >= 1:
                        low_acts(j - 1)
                    lane.settle()
                    for t in range(NT):
                        b = PJ.read(dve, (("up", j), t))
                        lane.settle()
                        ins = v.tensor_tensor(H[:, t, c0:c0 + w], b[:, 0:w], sg[:, t, 0:w], ALU.mult)
                        PJ.empty(lane, ins, (("up", j), t))
                low_acts(5)
                for j, t in ((0, 0), (0, 1), (1, 0)):
                    residual(PJ, "dn", j, t)
                layer_norm(1, 0)
                residual(PJ, "dn", 1, 1)
                layer_norm(1, 1)
                lane.settle()
          close_layer(nc, ctx.sems)


def layout(inputs):
    a = {k: np.ascontiguousarray(v) for k, v in inputs.items()}

    def by_feature(v):
        return np.ascontiguousarray(v.reshape(DEPTH, -1, P).transpose(0, 2, 1))

    a["vec1"] = np.concatenate([by_feature(a["norm_g"]), by_feature(a["mem_norm_g"])], axis=2)
    a["ident"] = np.eye(P, dtype=np.float32)
    tok = np.arange(S).reshape(NT, P).T
    a["cbias"] = np.where(np.arange(S)[None, None, :] <= tok[:, :, None], 0.0, NEG).astype(np.float32)

    def rope(theta, half):
        inv = np.float32(theta) ** (-np.arange(half, dtype=np.float32) / np.float32(half))
        ang = tok[:, :, None].astype(np.float32) * inv[None, None, :]
        c, s = np.cos(ang), np.sin(ang)
        return np.stack([np.concatenate([c, c], -1), np.concatenate([-s, s], -1)], axis=2).astype(np.float32)

    a["rope1"] = rope(500000.0, 8)
    a["rope2"] = rope(10000.0, 32)

    def at(v, size, off):
        out = np.zeros((DEPTH, size), np.float32)
        out[:, off:off + v.shape[1]] = v
        return out

    def late(v):
        return np.concatenate([np.zeros_like(v[:1]), v], axis=0)

    mu = a["rwkv_mu_2"]
    cols = [mu[:, 0:1024], at(mu[:, 1024:], P, P - 32), at(late(a["rwkv_mu_vres_2"]), P, P - 32), a["rwkv_w0_2"], a["rwkv_a0_2"],
            late(a["rwkv_v0_2"]), a["rwkv_k_k_2"], a["rwkv_k_a_2"], a["rwkv_r_k_2"].reshape(DEPTH, -1), a["gla_b_a_2"],
            a["gla_ln_w_2"], a["rwkv_ln_w_2"], a["gla_ln_b_2"], a["rwkv_ln_b_2"],
            np.repeat(np.array([[1.0], [0.0]], np.float32), P, axis=1)]
    a["vec2"] = np.concatenate([by_feature(v) for v in cols], axis=2)

    def rows(v, off):
        out = np.zeros((DEPTH, P, S), np.float32)
        out[:, off:off + v.shape[1]] = v
        return out

    g2 = a["rwkv_g2_2"]
    a["smallw"] = np.ascontiguousarray(np.stack([
        rows(a["gla_w_a2_2"], 0), rows(late(a["rwkv_v2_2"]), P - 32), rows(a["rwkv_w2_2"], 0), rows(a["rwkv_a2_2"], 64),
        g2[:, 0:P], rows(g2[:, P:], P - 32)], axis=2))
    a["pos"] = np.ascontiguousarray(np.stack([a["nsa_pos_k_2"], a["nsa_pos_v_2"]], axis=1)
                                    .reshape(DEPTH, 2, 2, 16, HD).transpose(0, 2, 4, 1, 3).reshape(DEPTH, P, 2, 16))
    for n in ("nsa_wk1_2", "nsa_wv1_2"):
        a[n] = np.ascontiguousarray(a[n].reshape(DEPTH, 2, 16, HD, 256).transpose(0, 1, 3, 2, 4).reshape(DEPTH, P, 16, 256))
    a["w_in_2"] = np.concatenate([a["w_in_2"][:, :, :VRES], late(a["w_in_vres_2"]), a["w_in_2"][:, :, VRES:]], axis=2)
    c = np.arange(P)
    ends = 16 * c + 31
    ok = (ends[None, None, :] <= tok[:, :, None]) & (c < 15)
    a["cmpb"] = np.where(ok, 0.0, NEG).astype(np.float32)
    a["rowv"] = (tok >= 31).astype(np.float32)
    a["ones"] = (c[:, None] // 64 == c[None, :] // 64).astype(np.float32)
    s_, t_ = c[:, None], c[None, :]
    same = s_ // 64 == t_ // 64
    m = [(s_ // (2 << n) == t_ // (2 << n)) & (s_ // (1 << n) % 2 == 0) & (t_ // (1 << n) % 2 == 1) for n in range(6)]
    m += [same & (s_ < t_), same & (s_ <= t_), s_ == t_]
    a["masks"] = np.ascontiguousarray(np.stack(m, axis=1).astype(np.float32))
    a["reset"] = np.repeat((np.arange(S)[None] % 64 != 0).astype(np.float32), P, axis=0)
    return {k: a[k] for k in USED}


USED = ["x", "mem", "vec1", "w_in", "w_mem_kv", "w_branch", "w_out", "ident", "cbias", "rope1", "final_g", "rope2", "vec2",
        "smallw", "pos", "nsa_wk1_2", "nsa_wk2_2", "nsa_wv1_2", "nsa_wv2_2", "w_in_2", "w_out_2", "ffn_w_gate_2", "ffn_w_up_2",
        "ffn_w_down_2", "ln1_w_2", "ln1_b_2", "ln2_w_2", "ln2_b_2", "cmpb", "rowv", "ones", "masks", "reset"]


def build(nc, A, out, first=DEPTH, second=DEPTH):
    with ExitStack() as ctx:
        chip = Chip(ctx, nc)
        with ExitStack() as c1:
            chip.memT = c1.enter_context(nc.sbuf_tensor("memT", [P, KC, S], F32))
            chip.rope1 = c1.enter_context(nc.sbuf_tensor("rope1s", [P, NT, 2, 16], F32))
            first_prologue(nc, chip, A)
            first_layers(nc, chip, A, first)

        def sb(name, shape):
            return ctx.enter_context(nc.sbuf_tensor(name, shape, F32))

        chip.vfirst = sb("vfirst", [P, 2, S])
        chip.rope2 = sb("rope2s", [P, NT, 2, HD])
        chip.cmpb = sb("cmpb", [P, NT, P])
        chip.rowv = sb("rowv", [P, NT])
        chip.ones = sb("ones", [P, P])
        chip.masks = sb("masks", [P, 9, P])
        chip.reset = sb("reset", [P, S])
        second_prologue(nc, chip, A)
        second_layers(nc, chip, A, second)
        with Scope() as c3:
            done = Count(c3, nc, "out_written")
            with nc.Block() as block:

                @block.sync
                def _(sp):
                    sp.dma_start(out.rearrange("(t p) d -> p t d", p=P), chip.x[:]).then_inc(done.sem, 16)
                    sp.wait_ge(done.sem, 16)


def kernel(**inputs):
    import concourse.bacc as _bacc
    from concourse.bass_utils import run_bass_kernel_spmd as _run

    nc = _bacc.Bacc("TRN2", target_bir_lowering=False, num_devices=1)
    arrays = layout({n: np.asarray(v) for n, v in inputs.items()})
    A = {n: nc.dram_tensor("in_" + n, a.shape, F32, kind="ExternalInput").ap() for n, a in arrays.items()}
    out = nc.dram_tensor("out", (S, D), F32, kind="ExternalOutput").ap()
    build(nc, A, out)
    r = _run(nc, [{"in_" + n: a for n, a in arrays.items()}], core_ids=[0])
    return r.results[0]["out"].reshape(1, S, D)
```
